# Optimizing a Trainium2 kernel written in Bass

```python
import jax, jax.numpy as jnp
from jax import lax
import numpy as np

D_MODEL = 1024
BATCH = 1
SEQ = 2048
DEPTH = 1
DEC_BATCH = 1
DEC_SEQ = 32
PAST_LEN = 512

'''One inference step of a chunk-causal hybrid streaming encoder (DEPTH layers).

Each layer: pre-RMSNorm -> single combined input projection whose columns are split into
  head group A (chunk-band attention, 8 heads x 64, QK-norm, clipped relative-position bias,
  each frame reads its own chunk and the previous 8 chunks) and
  head group B (Conformer convolution module, 512 channels: GLU -> causal depthwise conv
  width 31 -> LayerNorm over channels -> swish),
-> concat over groups -> single output projection -> residual add;
pre-RMSNorm -> SwiGLU FFN -> residual add;
per-layer input embedding p[i] projected to D_MODEL, gated by sigmoid(RMSNorm(h) @ W) -> residual add.

Inputs:
  x_prompt (BATCH, SEQ, D_MODEL), x_sample (DEC_BATCH, DEC_SEQ, D_MODEL)
  p_prompt (DEPTH, BATCH, SEQ, 256), p_sample (DEPTH, DEC_BATCH, DEC_SEQ, 256)
  cache_k, cache_v (DEPTH, DEC_BATCH, min(512, PAST_LEN), N_HEADS, HEAD_DIM): newest K (post QK-norm) / V rows, oldest first
  state_conv (DEPTH, DEC_BATCH, 30, CONV_W): last 30 GLU outputs feeding the depthwise conv
Returns the tuple:
  (y_prompt (BATCH, SEQ, D_MODEL),
   y_sample (DEC_BATCH, DEC_SEQ, D_MODEL),
   new_k_prompt (DEPTH, BATCH, min(512, SEQ), N_HEADS, HEAD_DIM),
   new_v_prompt (DEPTH, BATCH, min(512, SEQ), N_HEADS, HEAD_DIM),
   new_conv_prompt (DEPTH, BATCH, 30, CONV_W),
   new_k_sample (DEPTH, DEC_BATCH, min(512, PAST_LEN), N_HEADS, HEAD_DIM),
   new_v_sample (DEPTH, DEC_BATCH, min(512, PAST_LEN), N_HEADS, HEAD_DIM),
   new_conv_sample (DEPTH, DEC_BATCH, 30, CONV_W))
'''

CHUNK = 64
PAST_CHUNKS = 8
ATT_WINDOW = PAST_CHUNKS * CHUNK
BAND = ATT_WINDOW + CHUNK
MIX_W = D_MODEL
ATT_W = MIX_W // 2
CONV_W = MIX_W - ATT_W
HEAD_DIM = 64
N_HEADS = ATT_W // HEAD_DIM
REL_CLIP = 128
N_REL = 2 * REL_CLIP + 1
CONV_WIDTH = 31
CONV_HIST = CONV_WIDTH - 1
D_FF = -(-8 * D_MODEL // (3 * 256)) * 256
PLE_DIM = 256
IN_COLS = 3 * ATT_W + 2 * CONV_W
EPS = 1e-6
NEG = -1e30

kernel_name = 'hybrid_chunk_attn_conformer_conv_step'

def rms_norm(x, g):
    xf = x.astype(jnp.float32)
    y = xf * lax.rsqrt(jnp.mean(xf * xf, axis=-1, keepdims=True) + EPS)
    return (y * g.astype(jnp.float32)).astype(x.dtype)

def layer_norm(x, g, b):
    xf = x.astype(jnp.float32)
    mu = jnp.mean(xf, axis=-1, keepdims=True)
    xc = xf - mu
    y = xc * lax.rsqrt(jnp.mean(xc * xc, axis=-1, keepdims=True) + EPS)
    return (y * g.astype(jnp.float32) + b.astype(jnp.float32)).astype(x.dtype)

def project_mix_inputs(h, g_mix, w_in, q_gain, k_gain):
    u = rms_norm(h, g_mix)
    z = u @ w_in
    q, k, v, a, b = jnp.split(z, [ATT_W, 2 * ATT_W, 3 * ATT_W, 3 * ATT_W + CONV_W], axis=-1)
    shp = h.shape[:-1] + (N_HEADS, HEAD_DIM)
    q = rms_norm(q.reshape(shp), q_gain)
    k = rms_norm(k.reshape(shp), k_gain)
    v = v.reshape(shp)
    glu = a * jax.nn.sigmoid(b)
    return q, k, v, glu

def band_attend(q, k, v, q_pos, k_pos, rel_bias):
    s = jnp.einsum('nqhd,nkhd->nhqk', q.astype(jnp.float32), k.astype(jnp.float32)) * (HEAD_DIM ** -0.5)
    dist = q_pos[:, None] - k_pos[None, :]
    bias = rel_bias.astype(jnp.float32)[:, jnp.clip(dist, -REL_CLIP, REL_CLIP) + REL_CLIP]
    qc = (q_pos // CHUNK)[:, None]
    kc = (k_pos // CHUNK)[None, :]
    mask = (k_pos[None, :] >= 0) & (kc <= qc) & (kc >= qc - PAST_CHUNKS)
    s = jnp.where(mask, s + bias, NEG)
    p = jax.nn.softmax(s, axis=-1).astype(v.dtype)
    return jnp.einsum('nhqk,nkhd->nqhd', p, v)

def prompt_attention(q, k, v, rel_bias):
    n, s = q.shape[0], q.shape[1]
    n_chunks = s // CHUNK
    pad = jnp.zeros((n, ATT_WINDOW, N_HEADS, HEAD_DIM), k.dtype)
    kp = jnp.concatenate([pad, k], axis=1)
    vp = jnp.concatenate([pad, v], axis=1)

    def one_chunk(c):
        start = c * CHUNK
        qc = lax.dynamic_slice_in_dim(q, start, CHUNK, axis=1)
        kc = lax.dynamic_slice_in_dim(kp, start, BAND, axis=1)
        vc = lax.dynamic_slice_in_dim(vp, start, BAND, axis=1)
        q_pos = start + jnp.arange(CHUNK)
        k_pos = start - ATT_WINDOW + jnp.arange(BAND)
        return band_attend(qc, kc, vc, q_pos, k_pos, rel_bias)

    out = lax.map(one_chunk, jnp.arange(n_chunks))
    return jnp.moveaxis(out, 0, 1).reshape(n, s, ATT_W)

def conv_module_tail(glu, hist, conv_w, conv_b, ln_g, ln_b):
    xp = jnp.concatenate([hist, glu], axis=1)
    y = lax.conv_general_dilated(xp, conv_w[:, None, :], (1,), 'VALID',
                                 dimension_numbers=('NWC', 'WIO', 'NWC'),
                                 feature_group_count=CONV_W)
    y = y + conv_b
    return jax.nn.silu(layer_norm(y, ln_g, ln_b))

def finish_layer(h, att, cv, p, w_out, g_ffn, w_gate_up, w_down, g_ple, w_ple_gate, w_ple_proj):
    h = h + jnp.concatenate([att, cv], axis=-1) @ w_out
    u = rms_norm(h, g_ffn)
    gate, up = jnp.split(u @ w_gate_up, 2, axis=-1)
    h = h + (jax.nn.silu(gate) * up) @ w_down
    g = jax.nn.sigmoid(rms_norm(h, g_ple) @ w_ple_gate)
    return h + g * (p @ w_ple_proj)

def setup_inputs(seed: int = 0) -> dict:
    key = jax.random.key(seed)
    ks = jax.random.split(key, 23)
    rows = min(ATT_WINDOW, PAST_LEN)

    def nrm(k, shape, scale):
        return jax.random.normal(k, shape, jnp.float32) * scale

    return {
        'x_prompt': nrm(ks[0], (BATCH, SEQ, D_MODEL), 1.0),
        'x_sample': nrm(ks[1], (DEC_BATCH, DEC_SEQ, D_MODEL), 1.0),
        'p_prompt': nrm(ks[2], (DEPTH, BATCH, SEQ, PLE_DIM), 1.0),
        'p_sample': nrm(ks[3], (DEPTH, DEC_BATCH, DEC_SEQ, PLE_DIM), 1.0),
        'cache_k': nrm(ks[4], (DEPTH, DEC_BATCH, rows, N_HEADS, HEAD_DIM), 1.0),
        'cache_v': nrm(ks[5], (DEPTH, DEC_BATCH, rows, N_HEADS, HEAD_DIM), 0.5),
        'state_conv': nrm(ks[6], (DEPTH, DEC_BATCH, CONV_HIST, CONV_W), 0.5),
        'g_mix': 1.0 + nrm(ks[7], (DEPTH, D_MODEL), 0.02),
        'w_in': nrm(ks[8], (DEPTH, D_MODEL, IN_COLS), D_MODEL ** -0.5),
        'q_gain': 1.0 + nrm(ks[9], (DEPTH, HEAD_DIM), 0.02),
        'k_gain': 1.0 + nrm(ks[10], (DEPTH, HEAD_DIM), 0.02),
        'rel_bias': nrm(ks[11], (DEPTH, N_HEADS, N_REL), 0.1),
        'conv_w': nrm(ks[12], (DEPTH, CONV_WIDTH, CONV_W), CONV_WIDTH ** -0.5),
        'conv_b': nrm(ks[13], (DEPTH, CONV_W), 0.01),
        'conv_ln_g': 1.0 + nrm(ks[14], (DEPTH, CONV_W), 0.02),
        'conv_ln_b': nrm(ks[15], (DEPTH, CONV_W), 0.01),
        'w_out': nrm(ks[16], (DEPTH, MIX_W, D_MODEL), MIX_W ** -0.5),
        'g_ffn': 1.0 + nrm(ks[17], (DEPTH, D_MODEL), 0.02),
        'w_gate_up': nrm(ks[18], (DEPTH, D_MODEL, 2 * D_FF), D_MODEL ** -0.5),
        'w_down': nrm(ks[19], (DEPTH, D_FF, D_MODEL), D_FF ** -0.5),
        'g_ple': 1.0 + nrm(ks[20], (DEPTH, D_MODEL), 0.02),
        'w_ple_gate': nrm(ks[21], (DEPTH, D_MODEL, D_MODEL), D_MODEL ** -0.5),
        'w_ple_proj': nrm(ks[22], (DEPTH, PLE_DIM, D_MODEL), PLE_DIM ** -0.5),
    }

def reference(x_prompt, x_sample, p_prompt, p_sample, cache_k, cache_v, state_conv,
              g_mix, w_in, q_gain, k_gain, rel_bias, conv_w, conv_b, conv_ln_g, conv_ln_b,
              w_out, g_ffn, w_gate_up, w_down, g_ple, w_ple_gate, w_ple_proj):
    hp, hs = x_prompt, x_sample
    n_p, s_p = x_prompt.shape[0], x_prompt.shape[1]
    n_s, l_s = x_sample.shape[0], x_sample.shape[1]
    keep_p = min(ATT_WINDOW, s_p)
    rows_s = cache_k.shape[2]
    kp_l, vp_l, cp_l, ks_l, vs_l, cs_l = [], [], [], [], [], []
    for i in range(DEPTH):
        q, k, v, glu = project_mix_inputs(hp, g_mix[i], w_in[i], q_gain[i], k_gain[i])
        att = prompt_attention(q, k, v, rel_bias[i])
        hist0 = jnp.zeros((n_p, CONV_HIST, CONV_W), glu.dtype)
        cv = conv_module_tail(glu, hist0, conv_w[i], conv_b[i], conv_ln_g[i], conv_ln_b[i])
        hp_next = finish_layer(hp, att, cv, p_prompt[i], w_out[i], g_ffn[i], w_gate_up[i],
                               w_down[i], g_ple[i], w_ple_gate[i], w_ple_proj[i])
        kp_l.append(k[:, s_p - keep_p:])
        vp_l.append(v[:, s_p - keep_p:])
        cp_l.append(glu[:, s_p - CONV_HIST:])
        hp = hp_next

        q, k, v, glu = project_mix_inputs(hs, g_mix[i], w_in[i], q_gain[i], k_gain[i])
        k_all = jnp.concatenate([cache_k[i], k], axis=1)
        v_all = jnp.concatenate([cache_v[i], v], axis=1)
        q_pos = PAST_LEN + jnp.arange(l_s)
        k_pos = PAST_LEN - rows_s + jnp.arange(rows_s + l_s)
        att = band_attend(q, k_all, v_all, q_pos, k_pos, rel_bias[i]).reshape(n_s, l_s, ATT_W)
        cv = conv_module_tail(glu, state_conv[i], conv_w[i], conv_b[i], conv_ln_g[i], conv_ln_b[i])
        hs_next = finish_layer(hs, att, cv, p_sample[i], w_out[i], g_ffn[i], w_gate_up[i],
                               w_down[i], g_ple[i], w_ple_gate[i], w_ple_proj[i])
        ks_l.append(k_all[:, l_s:])
        vs_l.append(v_all[:, l_s:])
        conv_all = jnp.concatenate([state_conv[i], glu], axis=1)
        cs_l.append(conv_all[:, l_s:])
        hs = hs_next

    new_k_prompt = jnp.stack(kp_l)
    new_v_prompt = jnp.stack(vp_l)
    new_conv_prompt = jnp.stack(cp_l)
    new_k_sample = jnp.stack(ks_l)
    new_v_sample = jnp.stack(vs_l)
    new_conv_sample = jnp.stack(cs_l)
    return (hp, hs, new_k_prompt, new_v_prompt, new_conv_prompt, new_k_sample, new_v_sample, new_conv_sample)


_drawn_inputs = setup_inputs


def setup_inputs(seed=0):
    import zlib

    import numpy as np

    out = dict(_drawn_inputs(seed))
    spreads = {}
    factors = {'q_gain': 31.469,
     'rel_bias': 8.0,
     'conv_b': 7.398,
     'conv_ln_g': 6.148,
     'conv_ln_b': 25.997,
     'g_ffn': 4.444,
     'g_ple': 64.0}
    for name, (base, spread) in spreads.items():
        noise = np.random.default_rng([zlib.crc32(name.encode()), seed]).standard_normal(out[name].shape)
        drawn = base * np.exp(spread * noise) if base else spread * noise
        out[name] = __import__('jax').numpy.asarray(drawn.astype(out[name].dtype))
    for name, factor in factors.items():
        out[name] = (out[name] * factor).astype(out[name].dtype)
    return out
```

```python
from contextlib import ExitStack

import concourse.bass as bass
from concourse import mybir

F32 = mybir.dt.float32
F32R = mybir.dt.float32r
ACT = mybir.ActivationFunctionType
ALU = mybir.AluOpType
AX = mybir.AxisListType

P = 128
D = 1024
SEQ, DEC = 2048, 32
NT = SEQ + DEC
NB = 5
N = NT // NB
KD = D // P
AW = 512
CT = AW // P
HEADS, HD = 8, 64
CHUNK, PAST = 64, 512
TAPS, HIST = 31, 30
FF = 2816
KF = FF // P
PLE = 256
KP = PLE // P
EPS = 1e-6
NEG = -1e30
TG = 104
NG = N // TG

V_GMIX, V_GFFN, V_GPLE, V_GQ, V_GK, V_CB, V_LG, V_LB, V_CW = 0, 8, 16, 24, 25, 26, 30, 34, 38
NVEC = V_CW + CT * TAPS
EXT = 767


def build(nc, t):
    with ExitStack() as ctx:
        def sb(name, shape, dt=F32):
            return ctx.enter_context(nc.sbuf_tensor(name, shape, dt))

        def dram(name, shape, dt):
            return nc.dram_tensor(name, shape, dt, kind="Internal").ap()

        c = {
            "vec": sb("vec", [P, NVEC]), "ones": sb("ones", [P, P]), "ident": sb("ident", [P, P]),
            "sel": sb("sel", [P, 8, 16]), "selT": sb("selT", [16, 8, P]), "eps": sb("eps", [P, 1]),
            "gq8": sb("gq8", [P, 1]),
        }
        s = {
            "qh": dram("qh_d", (AW, NT), F32), "ql": dram("ql_d", (AW, NT), F32),
            "kh": dram("kh_d", (AW, NT), F32), "kl": dram("kl_d", (AW, NT), F32),
            "vh": dram("vh_d", (NT, AW), F32), "vl": dram("vl_d", (NT, AW), F32),
            "mh": dram("mh_d", (D, NT), F32), "ml": dram("ml_d", (D, NT), F32),
        }
        constants(nc, t, c)
        project(nc, t, c, s)
        conv(nc, t, c, s)
        attend(nc, t, c, s)
        finish(nc, t, c, s)


def constants(nc, t, c):
    with nc.semaphore("vec_in") as vec_in, nc.semaphore("passed") as passed, \
            nc.semaphore("cleared") as cleared, nc.semaphore("filled") as filled, nc.semaphore("shaped") as shaped, nc.Block() as block:
        @block.sync
        def _(sp):
            sp.dma_start(c["vec"][:, :], t["vec"]).then_inc(vec_in, 16)
            sp.dma_start(t["o_ck"], t["ck_rows"]).then_inc(passed, 16)
            sp.dma_start(t["o_cv"], t["cv_rows"]).then_inc(passed, 16)
            sp.wait_ge(passed, 32)

        @block.vector
        def _(dve):
            nc.vector.memset(c["ones"][:, :], 1.0)
            nc.vector.memset(c["eps"][:, :], EPS)
            nc.vector.memset(c["sel"][:, :, :], 0.0).then_inc(cleared, 1)
            dve.wait_ge(cleared, 1)
            for u in range(8):
                for half in range(2):
                    nc.vector.memset(c["sel"][HD * half:HD * half + HD, u, 2 * u + half:2 * u + half + 1], 1.0)
            dve.wait_ge(vec_in, 16)
            nc.vector.tensor_scalar(c["gq8"][:, :], c["vec"][:, V_GQ:V_GQ + 1], HD ** -0.5, None, ALU.mult)

        @block.gpsimd
        def _(pool):
            nc.gpsimd.memset(c["ident"][:, :], 0.0).then_inc(filled, 1)
            nc.gpsimd.memset(c["selT"][:, :, :], 1.0).then_inc(filled, 1)
            pool.wait_ge(filled, 2)
            nc.gpsimd.affine_select(out=c["ident"][:, :], in_=c["ident"][:, :], compare_op=ALU.not_equal,
                                    fill=1.0, base=0, pattern=[[-1, P]], channel_multiplier=1).then_inc(shaped, 1)
            pool.wait_ge(shaped, 1)
            nc.gpsimd.affine_select(out=c["selT"][:, :, :], in_=c["selT"][:, :, :], compare_op=ALU.is_ge,
                                    fill=0.0, base=0, pattern=[[P, 8], [1, P]],
                                    channel_multiplier=-HD).then_inc(shaped, 1)
            pool.wait_ge(shaped, 2)
            nc.gpsimd.affine_select(out=c["selT"][:, :, :], in_=c["selT"][:, :, :], compare_op=ALU.is_ge,
                                    fill=0.0, base=HD - 1, pattern=[[-P, 8], [-1, P]], channel_multiplier=HD)


def passes(nc, out, w, u, kts, first, last):
    mm = None
    for n, (kw, ku) in enumerate(kts):
        for j, (wp, up) in enumerate(((0, 0), (0, 1), (1, 0))):
            mm = nc.tensor.matmul(out, w[wp](kw), u[up](ku), start=first and n == 0 and j == 0,
                                  stop=last and n == len(kts) - 1 and j == 2)
    return mm


class WeightRing:

    def __init__(self, nc, ctx, tag, kmax):
        self.nc = nc
        self.raw = ctx.enter_context(nc.sbuf_tensor(f"{tag}w_raw", [P, 2, kmax, P], F32))
        self.hi = ctx.enter_context(nc.sbuf_tensor(f"{tag}w_hi", [P, 2, kmax, P], F32R))
        self.lo = ctx.enter_context(nc.sbuf_tensor(f"{tag}w_lo", [P, 2, kmax, P], F32R))
        self.loaded = [ctx.enter_context(nc.semaphore(f"{tag}w_loaded{i}")) for i in range(2)]
        self.hi_done = ctx.enter_context(nc.semaphore(f"{tag}w_hi_done"))
        self.lo_done = ctx.enter_context(nc.semaphore(f"{tag}w_lo_done"))
        self.used = ctx.enter_context(nc.semaphore(f"{tag}w_used"))

    def load(self, sp, src, slot, kts):
        sp.dma_start(self.raw[:, slot, 0:kts, :].rearrange("p k c -> p (k c)"), src).then_inc(self.loaded[slot], 16)

    def high(self, act, v, pair, slot, kts):
        act.wait_ge(self.loaded[slot], pair * 16 + 16)
        act.wait_ge(self.used, v + 1)
        self.nc.scalar.activation(self.hi[:, slot, 0:kts, :], self.raw[:, slot, 0:kts, :],
                                  ACT.Copy).then_inc(self.hi_done, 1)

    def low(self, pool, v, slot, kts):
        pool.wait_ge(self.hi_done, v + 1)
        self.nc.gpsimd.tensor_tensor(self.lo[:, slot, 0:kts, :], self.raw[:, slot, 0:kts, :],
                                     self.hi[:, slot, 0:kts, :].bitcast(F32), ALU.subtract).then_inc(self.lo_done, 1)


def wrapped(b):
    return (b + 1) % NB


def project(nc, t, c, s):
    NU = 20
    QK, VU, GU = 8, 8, 12
    FIN = 10
    with ExitStack() as ctx:
        def sb(name, shape, dt=F32):
            return ctx.enter_context(nc.sbuf_tensor("a_" + name, shape, dt))

        def ps(name, shape):
            return ctx.enter_context(nc.psum_tensor("a_" + name, shape, F32))

        def sem(name):
            return ctx.enter_context(nc.semaphore("a_" + name))

        ring = WeightRing(nc, ctx, "a_", KD)
        x = sb("x", [P, KD, N])
        xsq = sb("xsq", [P, KD, N])
        ssum = sb("ssum", [P, N])
        sd, rstd = sb("sd", [P, N]), sb("rstd", [P, N])
        uh, ul = sb("uh", [P, KD, N], F32R), sb("ul", [P, KD, N], F32R)
        zqk = sb("zqk", [P, QK, N])
        zsq = sb("zsq", [P, 2, N])
        sd16, r16 = sb("sd16", [16, N]), sb("r16", [16, N])
        zn = sb("zn", [P, 2, N])
        znh, znl = sb("znh", [P, 2, N], F32R), sb("znl", [P, 2, N], F32R)
        z = sb("z", [P, 2, N])
        vt = sb("vt", [TG, NG, AW])
        vh, vl = sb("vh", [TG, NG, AW], F32R), sb("vl", [TG, NG, AW], F32R)
        sig = sb("sig", [P, N])
        glu = sb("glu", [P, 2, N])

        acc = ps("acc", [P, 2, 512])
        ps_rs = ps("ps_rs", [P, 512])
        ps_ss = ps("ps_ss", [P, 512])
        ps_bc = ps("ps_bc", [P, 2, 512])
        ps_vt = ps("ps_vt", [P, 2, 512])

        x_in, x_hi, x_lo, x_sq, x_sum = sem("x_in"), sem("x_hi"), sem("x_lo"), sem("x_sq"), sem("x_sum")
        rs_mm, rs_sd, rs = sem("rs_mm"), sem("rs_sd"), sem("rs")
        z_out, z_sq = sem("z_out"), sem("z_sq")
        ss_mm, ss_sd, ss_r = sem("ss_mm"), sem("ss_sd"), sem("ss_r")
        bc_mm, zn_out, znh_out, znl_out = sem("bc_mm"), sem("zn_out"), sem("znh_out"), sem("znl_out")
        v_tr, v_out, vh_out, vl_out = sem("v_tr"), sem("v_out"), sem("vh_out"), sem("vl_out")
        sig_out, glu_out = sem("sig_out"), sem("glu_out")
        st_qk = [sem("st_q"), sem("st_k")]
        st_v = sem("st_v")
        st_glu = [sem("st_g0"), sem("st_g1")]
        vec = c["vec"]

        def weights(sp, i):
            m = i % NU
            ring.load(sp, t["w_in"][m * P:(m + 1) * P, :], i % 2, KD)

        block = ctx.enter_context(nc.Block())

        @block.sync
        def _(sp):
            sp.dma_start(x[:, :, :].rearrange("p k n -> p (k n)"), t["x"][0:P, :]).then_inc(x_in, 16)
            weights(sp, 0)
            weights(sp, 1)
            for i in range(2, 4):
                sp.wait_ge(ring.lo_done, i - 1)
                weights(sp, i)
            sp.sem_inc(st_v, 48)
            for q in range(2):
                sp.sem_inc(st_qk[q], (32, 48)[q])
                sp.sem_inc(st_glu[q], 16)
            with sp.Fori(0, NB) as b:
                for i in range(NU):
                    if i == 2:
                        sp.wait_ge(x_hi, b * KD + KD)
                        sp.wait_ge(x_lo, b * KD + KD)
                        sp.dma_start(x[:, :, :].rearrange("p k n -> p (k n)"),
                                     t["x"][bass.ds(wrapped(b) * P, P), :]).then_inc(x_in, 16)
                    if FIN <= i < FIN + QK:
                        j = i - FIN
                        m, q = j // 2, j % 2
                        rows = slice(m * P, (m + 1) * P)
                        sp.wait_ge(znl_out, b * QK + (j + 1))
                        sp.dma_start(s["qk"[q] + "h"][rows, bass.ds(b * N, N)], znh[:, q, :].bitcast(F32)).then_inc(st_qk[q], 16)
                        sp.dma_start(s["qk"[q] + "l"][rows, bass.ds(b * N, N)], znl[:, q, :].bitcast(F32)).then_inc(st_qk[q], 16)
                        if q:
                            sp.dma_start(t["o_k"][rows, bass.ds(b * N, N)], zn[:, q, :]).then_inc(st_qk[q], 16)
                    if i == VU + CT:
                        sp.wait_ge(vl_out, b * CT + CT)
                        for dst, src in ((t["o_v"], vt[:, :, :]), (s["vh"], vh[:, :, :].bitcast(F32)),
                                         (s["vl"], vl[:, :, :].bitcast(F32))):
                            sp.dma_start(dst[bass.ds(b * N, N), :].rearrange("(g p) d -> p g d", p=TG),
                                         src).then_inc(st_v, 16)
                    if i > GU and i % 2:
                        m = (i - GU) // 2
                        sp.wait_ge(glu_out, b * CT + (m + 2))
                        sp.dma_start(t["o_g"][m * P:(m + 1) * P, bass.ds(b * N, N)],
                                     glu[:, m % 2, :]).then_inc(st_glu[m % 2], 16)
                    sp.wait_ge(ring.lo_done, b * NU + (i + 3))
                    weights(sp, i + 4)
            for q in range(2):
                sp.wait_ge(ring.loaded[q], 16 * (NU * NB // 2 + 2))
                sp.wait_ge(st_qk[q], (32, 48)[q] * (1 + NB * CT))
                sp.wait_ge(st_glu[q], 16 * (1 + 2 * NB))
            sp.wait_ge(x_in, 16 * (NB + 1))
            sp.wait_ge(st_v, 48 * (NB + 1))

        @block.scalar
        def _(act):
            def square_x(n_in):
                act.wait_ge(x_in, n_in)
                nc.scalar.activation(xsq[:, :, :], x[:, :, :], ACT.Square).then_inc(x_sq, 1)

            square_x(16)
            ring.high(act, 0, 0, 0, KD)
            ring.high(act, 1, 0, 1, KD)
            with act.Fori(0, NB) as b:
                act.wait_ge(x_in, b * 16 + 16)
                act.wait_ge(ring.used, b * NU + 2)
                for k in range(KD):
                    nc.scalar.activation(uh[:, k, :], x[:, k, :], ACT.Identity,
                                         scale=vec[:, V_GMIX + k:V_GMIX + k + 1]).then_inc(x_hi, 1)
                for i in range(NU):
                    ring.high(act, b * NU + (i + 2), b * (NU // 2) + (i + 2) // 2, i % 2, KD)
                    if i == 0:
                        act.wait_ge(rs_mm, b + 1)
                        nc.scalar.activation(sd[:, :], ps_rs[:, 0:N], ACT.Sqrt, scale=1.0 / D,
                                             bias=c["eps"][:, :]).then_inc(rs_sd, 1)
                    if i == 4:
                        square_x(b * 16 + 32)
                    if i < QK:
                        act.wait_ge(z_out, b * NU + (i + 3))
                        if i >= 2:
                            act.wait_ge(ss_mm, b * QK + (i - 1))
                        nc.scalar.activation(zsq[:, i % 2, :], zqk[:, i, :], ACT.Square).then_inc(z_sq, 1)
                    if i == QK:
                        act.wait_ge(ss_mm, b * QK + QK)
                        nc.scalar.activation(sd16[:, :], ps_ss[0:16, 0:N], ACT.Sqrt, scale=1.0 / HD,
                                             bias=c["eps"][0:16, :]).then_inc(ss_sd, 1)
                    if VU < i <= VU + CT:
                        m = i - 1 - VU
                        act.wait_ge(v_tr, b * CT + (m + 1))
                        act.wait_ge(st_v, b * 48 + 48)
                        nc.scalar.activation(vh[:, :, m * P:(m + 1) * P],
                                             ps_vt[0:TG, m % 2, :].rearrange("p (g d) -> p g d", g=NG),
                                             ACT.Copy).then_inc(vh_out, 1)
                    if FIN <= i < FIN + QK:
                        j = i - FIN
                        q = j % 2
                        act.wait_ge(zn_out, b * QK + (j + 1))
                        nc.scalar.activation(znh[:, q, :], zn[:, q, :], ACT.Copy).then_inc(znh_out, 1)
                    if i > GU and i % 2:
                        m = (i - GU) // 2
                        act.wait_ge(z_out, b * NU + (i + 3))
                        nc.scalar.activation(sig[:, :], z[:, 1, :], ACT.Sigmoid).then_inc(sig_out, 1)

        @block.gpsimd
        def _(pool):
            ring.low(pool, 0, 0, KD)
            ring.low(pool, 1, 1, KD)
            with pool.Fori(0, NB) as b:
                for i in range(NU):
                    ring.low(pool, b * NU + (i + 2), i % 2, KD)

        @block.vector
        def _(dve):
            def sum_x(n):
                dve.wait_ge(x_sq, n)
                nc.vector.tensor_reduce(out=ssum[:, :], in_=xsq[:, :, :].rearrange("p k n -> p n k"),
                                        axis=AX.X, op=ALU.add).then_inc(x_sum, 1)

            sum_x(1)
            dve.sem_inc(z_out, 2)
            dve.sem_inc(glu_out, 1)
            with dve.Fori(0, NB) as b:
                for k in range(KD):
                    dve.wait_ge(x_hi, b * KD + (k + 1))
                    nc.vector.scalar_tensor_tensor(ul[:, k, :], x[:, k, :], vec[:, V_GMIX + k:V_GMIX + k + 1],
                                                   uh[:, k, :].bitcast(F32), ALU.mult, ALU.subtract).then_inc(x_lo, 1)
                for i in range(NU):
                    if i == 0:
                        dve.wait_ge(rs_sd, b + 1)
                        dve.wait_ge(z_out, b * NU + 2)
                        nc.vector.reciprocal(rstd[:, :], sd[:, :]).then_inc(rs, 1)
                        dve.wait_ge(rs, b + 1)
                    if i == 5:
                        sum_x(b + 2)
                    dve.wait_ge(ring.used, b * NU + (i + 3))
                    if i == VU or (i >= GU and i % 2 == 0):
                        dve.wait_ge(glu_out, b * CT + (max(i - GU, 0) // 2 + 1))
                    dst = zqk[:, i, :] if i < QK else z[:, i % 2, :]
                    nc.vector.tensor_tensor(dst, acc[:, i % 2, 0:N], rstd[:, :], ALU.mult).then_inc(z_out, 1)
                    if i == QK:
                        dve.wait_ge(ss_sd, b + 1)
                        nc.vector.reciprocal(r16[:, :], sd16[:, :]).then_inc(ss_r, 1)
                    if VU < i <= VU + CT:
                        m = i - 1 - VU
                        cols = slice(m * P, (m + 1) * P)
                        tr = ps_vt[0:TG, m % 2, :].rearrange("p (g d) -> p g d", g=NG)
                        dve.wait_ge(vh_out, b * CT + (m + 1))
                        nc.vector.tensor_copy(vt[:, :, cols], tr).then_inc(v_out, 1)
                        nc.vector.tensor_tensor(vl[:, :, cols], tr, vh[:, :, cols].bitcast(F32),
                                                ALU.subtract).then_inc(vl_out, 1)
                    if FIN <= i < FIN + QK:
                        j = i - FIN
                        q = j % 2
                        gain = vec[:, V_GK:V_GK + 1] if q else c["gq8"][:, :]
                        dve.wait_ge(bc_mm, b * QK + (j + 1))
                        dve.wait_ge(st_qk[q], (b * CT + (j // 2 + 1)) * (32, 48)[q])
                        nc.vector.scalar_tensor_tensor(zn[:, q, :], zqk[:, j, :], gain, ps_bc[:, q, 0:N],
                                                       ALU.mult, ALU.mult).then_inc(zn_out, 1)
                        dve.wait_ge(zn_out, b * QK + (j + 1))
                        dve.wait_ge(znh_out, b * QK + (j + 1))
                        nc.vector.tensor_tensor(znl[:, q, :], zn[:, q, :], znh[:, q, :].bitcast(F32),
                                                ALU.subtract).then_inc(znl_out, 1)
                    if i > GU and i % 2:
                        m = (i - GU) // 2
                        dve.wait_ge(sig_out, b * CT + (m + 1))
                        dve.wait_ge(z_out, b * NU + (i + 3))
                        dve.wait_ge(st_glu[m % 2], b * 32 + 16 * (m // 2 + 1))
                        nc.vector.tensor_tensor(glu[:, m % 2, :], z[:, 0, :], sig[:, :],
                                                ALU.mult).then_inc(glu_out, 1)

        @block.tensor
        def _(pe):
            pe.sem_inc(ring.used, 2)
            with pe.Fori(0, NB) as b:
                for i in range(NU):
                    pe.wait_ge(ring.lo_done, b * NU + (i + 1))
                    pe.wait_ge(z_out, b * NU + (i + 1))
                    w = [lambda k: ring.hi[:, i % 2, k, :], lambda k: ring.lo[:, i % 2, k, :]]
                    u = [lambda k: uh[:, k, :], lambda k: ul[:, k, :]]
                    if i == 0:
                        for k in range(KD):
                            pe.wait_ge(x_lo, b * KD + (k + 1))
                            mm = passes(nc, acc[:, 0, 0:N], w, u, [(k, k)], k == 0, k == KD - 1)
                    else:
                        mm = passes(nc, acc[:, i % 2, 0:N], w, u, [(k, k) for k in range(KD)], True, True)
                    mm.then_inc(ring.used, 1)
                    if i == 0:
                        pe.wait_ge(x_sum, b + 1)
                        nc.tensor.matmul(ps_rs[:, 0:N], c["ones"][:, :], ssum[:, :], start=True,
                                         stop=True).then_inc(rs_mm, 1)
                    if 1 <= i <= QK:
                        j = i - 1
                        pe.wait_ge(z_sq, b * QK + (j + 1))
                        nc.tensor.matmul(ps_ss[0:16, 0:N], c["sel"][:, j, :], zsq[:, j % 2, :], start=j == 0,
                                         stop=j == QK - 1).then_inc(ss_mm, 1)
                    if VU < i <= VU + CT:
                        m = i - 1 - VU
                        pe.wait_ge(z_out, b * NU + (i + 2))
                        if m >= 2:
                            pe.wait_ge(vl_out, b * CT + (m - 1))
                        for g in range(NG):
                            tr = nc.tensor.transpose(ps_vt[0:TG, m % 2, g * P:(g + 1) * P],
                                                     z[:, (i - 1) % 2, g * TG:(g + 1) * TG], c["ident"][:, :])
                        tr.then_inc(v_tr, 1)
                    if FIN <= i < FIN + QK:
                        j = i - FIN
                        pe.wait_ge(ss_r, b + 1)
                        if j >= 2:
                            pe.wait_ge(zn_out, b * QK + (j - 1))
                        nc.tensor.matmul(ps_bc[:, j % 2, 0:N], c["selT"][:, j, :], r16[:, :], start=True,
                                         stop=True).then_inc(bc_mm, 1)


def conv(nc, t, c, s):
    W = 512
    NW = SEQ // W
    with ExitStack() as ctx:
        def sb(name, shape, dt=F32):
            return ctx.enter_context(nc.sbuf_tensor("v_" + name, shape, dt))

        def ps(name, shape):
            return ctx.enter_context(nc.psum_tensor("v_" + name, shape, F32))

        def sem(name):
            return ctx.enter_context(nc.semaphore("v_" + name))

        g = sb("g", [P, 2, CT, HIST + W])
        y = sb("y", [P, CT, W])
        part = sb("part", [P, W])
        xc, sq = sb("xc", [P, CT, W]), sb("sq", [P, CT, W])
        sd, r = sb("sd", [P, W]), sb("r", [P, W])
        xn, tt, sg, out = (sb(n, [P, CT, W]) for n in ("xn", "tt", "sg", "out"))
        oh, ol = sb("oh", [P, CT, W], F32R), sb("ol", [P, CT, W], F32R)
        ps_m, ps_v = ps("ps_m", [P, W]), ps("ps_v", [P, W])
        g_in = [sem("g_in0"), sem("g_in1")]
        tap, part_out, mean_mm = sem("tap"), sem("part_out"), sem("mean_mm")
        xc_out, sq_out, var_mm, sd_out = sem("xc_out"), sem("sq_out"), sem("var_mm"), sem("sd_out")
        r_out, xn_out, tt_out, sg_out = sem("r_out"), sem("xn_out"), sem("tt_out"), sem("sg_out")
        o_out, oh_out, ol_out, st = sem("o_out"), sem("oh_out"), sem("ol_out"), sem("st")
        vec = c["vec"]
        NTAP = CT * TAPS
        block = ctx.enter_context(nc.Block())

        def rows(d):
            return d.rearrange("(c p) n -> p c n", p=P)

        @block.sync
        def _(sp):
            def load(slot, src0, width, dst0):
                sp.dma_start(g[:, slot, :, dst0:dst0 + width],
                             rows(t["o_g"])[:, :, src0]).then_inc(g_in[slot], 16)

            def store(n, c0, width):
                sp.wait_ge(ol_out, n)
                sp.dma_start(rows(s["mh"][AW:D, :])[:, :, c0], oh[:, :, 0:width].bitcast(F32)).then_inc(st, 16)
                sp.dma_start(rows(s["ml"][AW:D, :])[:, :, c0], ol[:, :, 0:width].bitcast(F32)).then_inc(st, 16)

            sp.dma_start(g[:, 1, :, 0:HIST], rows(t["state"])).then_inc(g_in[1], 16)
            load(1, slice(SEQ, NT), DEC, HIST)
            load(0, slice(0, W), W, HIST)
            store(1, slice(SEQ, NT), DEC)
            load(1, bass.ds(W - HIST, W + HIST), W + HIST, 0)
            store(2, slice(0, W), W)
            for n in range(1, NW):
                if n + 1 < NW:
                    load((n + 1) % 2, bass.ds((n + 1) * W - HIST, W + HIST), W + HIST, 0)
                store(n + 2, slice(n * W, n * W + W), W)
            sp.wait_ge(st, 32 * (NW + 1))

        def windows():
            return [(0, 1, DEC, 32)] + [(n + 1, n % 2, W, 16 * (n // 2 + 1) + 32 * (n % 2)) for n in range(NW)]

        @block.vector
        def _(dve):
            nc.vector.memset(g[:, 0, :, 0:HIST], 0.0).then_inc(tap, 1)
            taps = 1
            for n, slot, wd, got in windows():
                dve.wait_ge(g_in[slot], got)
                if n:
                    dve.wait_ge(ol_out, n)
                for k in range(TAPS):
                    for ct in range(CT):
                        src = g[:, slot, ct, k:k + wd]
                        wk = vec[:, V_CW + ct * TAPS + k:V_CW + ct * TAPS + k + 1]
                        if k == 0:
                            dve.wait_ge(tap, taps - ct)
                            nc.vector.tensor_scalar(y[:, ct, 0:wd], src, wk, vec[:, V_CB + ct:V_CB + ct + 1],
                                                    ALU.mult, ALU.add).then_inc(tap, 1)
                        else:
                            dve.wait_ge(tap, taps - CT + 1)
                            nc.vector.scalar_tensor_tensor(y[:, ct, 0:wd], src, wk, y[:, ct, 0:wd],
                                                           ALU.mult, ALU.add).then_inc(tap, 1)
                        taps += 1
                dve.wait_ge(tap, taps)
                nc.vector.tensor_reduce(out=part[:, 0:wd], in_=y[:, :, 0:wd].rearrange("p c n -> p n c"),
                                        axis=AX.X, op=ALU.add).then_inc(part_out, 1)
                dve.wait_ge(mean_mm, n + 1)
                for ct in range(CT):
                    nc.vector.scalar_tensor_tensor(xc[:, ct, 0:wd], ps_m[:, 0:wd], -1.0 / AW, y[:, ct, 0:wd],
                                                   ALU.mult, ALU.add).then_inc(xc_out, 1)
                dve.wait_ge(sq_out, n + 1)
                nc.vector.tensor_reduce(out=part[:, 0:wd], in_=sq[:, :, 0:wd].rearrange("p c n -> p n c"),
                                        axis=AX.X, op=ALU.add).then_inc(part_out, 1)
                dve.wait_ge(sd_out, n + 1)
                nc.vector.reciprocal(r[:, 0:wd], sd[:, 0:wd]).then_inc(r_out, 1)
                dve.wait_ge(r_out, n + 1)
                dve.wait_ge(xc_out, CT * (n + 1))
                for ct in range(CT):
                    nc.vector.tensor_tensor(xn[:, ct, 0:wd], xc[:, ct, 0:wd], r[:, 0:wd], ALU.mult).then_inc(xn_out, 1)
                dve.wait_ge(sg_out, n + 1)
                nc.vector.tensor_tensor(out[:, :, 0:wd], tt[:, :, 0:wd], sg[:, :, 0:wd], ALU.mult).then_inc(o_out, 1)
                dve.wait_ge(oh_out, n + 1)
                dve.wait_ge(o_out, n + 1)
                nc.vector.tensor_tensor(ol[:, :, 0:wd], out[:, :, 0:wd], oh[:, :, 0:wd].bitcast(F32),
                                        ALU.subtract).then_inc(ol_out, 1)

        @block.tensor
        def _(pe):
            for n, slot, wd, got in windows():
                pe.wait_ge(part_out, 2 * n + 1)
                nc.tensor.matmul(ps_m[:, 0:wd], c["ones"][:, :], part[:, 0:wd], start=True, stop=True).then_inc(mean_mm, 1)
                pe.wait_ge(part_out, 2 * n + 2)
                nc.tensor.matmul(ps_v[:, 0:wd], c["ones"][:, :], part[:, 0:wd], start=True, stop=True).then_inc(var_mm, 1)

        @block.scalar
        def _(act):
            for n, slot, wd, got in windows():
                act.wait_ge(xc_out, CT * (n + 1))
                nc.scalar.activation(sq[:, :, 0:wd], xc[:, :, 0:wd], ACT.Square).then_inc(sq_out, 1)
                act.wait_ge(var_mm, n + 1)
                nc.scalar.activation(sd[:, 0:wd], ps_v[:, 0:wd], ACT.Sqrt, scale=1.0 / AW,
                                     bias=c["eps"][:, :]).then_inc(sd_out, 1)
                act.wait_ge(xn_out, CT * (n + 1))
                for ct in range(CT):
                    nc.scalar.activation(tt[:, ct, 0:wd], xn[:, ct, 0:wd], ACT.Identity,
                                         scale=vec[:, V_LG + ct:V_LG + ct + 1],
                                         bias=vec[:, V_LB + ct:V_LB + ct + 1]).then_inc(tt_out, 1)
                act.wait_ge(tt_out, CT * (n + 1))
                nc.scalar.activation(sg[:, :, 0:wd], tt[:, :, 0:wd], ACT.Sigmoid).then_inc(sg_out, 1)
                act.wait_ge(o_out, n + 1)
                if n:
                    act.wait_ge(st, 32 * n)
                nc.scalar.activation(oh[:, :, 0:wd], out[:, :, 0:wd], ACT.Copy).then_inc(oh_out, 1)


def attend(nc, t, c, s):
    PQ, GT, WIN, PW = P, 6, 6 * P, 5 * P
    UG = 2 * HEADS
    CD = CT
    with ExitStack() as ctx:
        def sb(name, shape, dt=F32):
            return ctx.enter_context(nc.sbuf_tensor("b_" + name, shape, dt))

        def ps(name, shape):
            return ctx.enter_context(nc.psum_tensor("b_" + name, shape, F32))

        def sem(name):
            return ctx.enter_context(nc.semaphore("b_" + name))

        bias = sb("bias", [P, HEADS, PW])
        qh, ql = (sb(n, [P, 2, CD, 2 * PQ], F32R) for n in ("qh", "ql"))
        kh, kl = (sb(n, [P, 2, CD, WIN], F32R) for n in ("kh", "kl"))
        vh, vl = (sb(n, [P, 2, GT, AW], F32R) for n in ("vh", "vl"))
        sc = sb("sc", [P, 2, PW])
        pr = sb("pr", [P, 2, PW])
        nmx = sb("nmx", [P, 2])
        rsum = sb("rsum", [P, 2, HEADS])
        rinv = sb("rinv", [P, HEADS])
        pth, ptl = (sb(n, [P, 2, PW], F32R) for n in ("pth", "ptl"))
        att = sb("att", [P, AW])
        ath, atl = (sb(n, [P, 2, CD, PQ], F32R) for n in ("ath", "atl"))
        craw = sb("craw", [P, 2, CD * 512])

        ps_s = ps("ps_s", [P, 2, 2, 512])
        ps_t = ps("ps_t", [P, 1024])
        ps_o = ps("ps_o", [P, AW])
        ps_a = ps("ps_a", [P, CD, PQ])

        bias_in, masked, cache_in, cache_hi, cache_lo = (sem(n) for n in (
            "bias_in", "masked", "cache_in", "cache_hi", "cache_lo"))
        win_in = [sem("win_in0"), sem("win_in1")]
        sc_turn = sem("sc_turn")
        qk_done, sc_done, ex_done, tr_done = sem("qk_done"), sem("sc_done"), sem("ex_done"), sem("tr_done")
        pth_done, ptl_done, pv_done = sem("pth_done"), sem("ptl_done"), sem("pv_done")
        rinv_done, att_done, at_tr, ath_done, atl_done = (sem(n) for n in (
            "rinv_done", "att_done", "at_tr", "ath_done", "atl_done"))
        stored = [sem("stored0"), sem("stored1")]

        def pair(j, tiles):
            return {"q0": j * PQ, "mq": PQ, "tile0": j + 5 - tiles, "keys": [P] * tiles, "bias0": (5 - tiles) * P}

        FIRST = [{"g": g, "slot": g % 2, "pairs": [pair(j, 2 * g + j + 1) for j in range(2)]} for g in range(2)]
        SAMPLE = {"g": 8, "slot": 0, "pairs": [{"q0": 0, "mq": DEC, "tile0": 0, "keys": [P] * 4 + [DEC], "bias0": 0}]}

        def inner(it):
            return [{"g": it * 2 + (2 + k), "slot": k, "pairs": [pair(j, 5) for j in range(2)]} for k in range(2)]

        def sections(eng, run):
            run(FIRST, 0, 0)
            with eng.Fori(0, 3) as it:
                run(inner(it), it * (2 * UG) + 2 * UG, it * 4 + 4)
            run([SAMPLE], 8 * UG, 16)

        def units(groups):
            out = []
            for k, g in enumerate(groups):
                for j, p in enumerate(g["pairs"]):
                    for h in range(HEADS):
                        out.append({**p, "slot": g["slot"], "h": h, "pair": 2 * k + j, "g": g["g"], "group": k,
                                    "w": sum(p["keys"])})
            return out

        def head(u):
            lo = HD * (u["h"] % 2)
            return u["h"] // 2, slice(lo, lo + HD)

        def rows(d):
            return d.rearrange("(c p) n -> p c n", p=P)

        block = ctx.enter_context(nc.Block())

        @block.sync
        def _(sp):
            def load_window(g):
                sl, at = g["slot"], g["g"]
                short = (2 - at) * 2 * PQ if isinstance(at, int) and at < 2 else 0
                k0 = at * (2 * PQ) - (PAST - short)
                for dst, src in ((qh, "qh"), (ql, "ql")):
                    sp.dma_start(dst[:, sl, :, :].bitcast(F32), rows(s[src])[:, :, bass.ds(at * (2 * PQ), 2 * PQ)]).then_inc(win_in[sl], 16)
                for dst, src in ((kh, "kh"), (kl, "kl")):
                    sp.dma_start(dst[:, sl, :, short:WIN].bitcast(F32),
                                 rows(s[src])[:, :, bass.ds(k0, WIN - short)]).then_inc(win_in[sl], 16)
                for dst, src in ((vh, "vh"), (vl, "vl")):
                    sp.dma_start(dst[:, sl, short // P:GT, :].bitcast(F32),
                                 s[src][bass.ds(k0, WIN - short), :].rearrange("(t p) d -> p t d", p=P)).then_inc(win_in[sl], 16)

            def store_pair(n, slot, c0, width):
                sp.wait_ge(atl_done, n + 1)
                for dst, src in ((s["mh"], ath), (s["ml"], atl)):
                    sp.dma_start(rows(dst[0:AW, :])[:, :, c0], src[:, slot, :, 0:width].bitcast(F32)).then_inc(stored[slot], 16)

            load_window(FIRST[0])
            ext = t["ext"]
            sp.dma_start(bias[:, :, :], bass.AP(ext.tensor, P - 1, [[EXT - 1, P], [P * EXT, HEADS], [1, PW]])).then_inc(bias_in, 16)
            load_window(FIRST[1])
            sp.dma_start(craw[:, 0, :], t["ckT"]).then_inc(cache_in, 16)
            sp.dma_start(craw[:, 1, :], t["cvT"]).then_inc(cache_in, 16)
            for q in range(2):
                sp.sem_inc(stored[q], 32)
            for k in range(2):
                for j in range(2):
                    store_pair(2 * k + j, j, bass.ds(2 * PQ * k + PQ * j, PQ), PQ)
                sp.wait_ge(pv_done, UG * (k + 1))
                load_window({"g": 2 + k, "slot": k})
            with sp.Fori(0, 2) as it:
                for k in range(2):
                    for j in range(2):
                        store_pair(it * 4 + (4 + 2 * k + j), j, bass.ds((it * 2 + (2 + k)) * (2 * PQ) + PQ * j, PQ), PQ)
                    sp.wait_ge(pv_done, it * (2 * UG) + UG * (k + 3))
                    load_window({"g": it * 2 + (4 + k), "slot": k})
            for k in range(2):
                for j in range(2):
                    store_pair(12 + 2 * k + j, j, bass.ds(2 * PQ * (6 + k) + PQ * j, PQ), PQ)
                if k == 0:
                    sp.wait_ge(pv_done, 7 * UG)
                    new = bass.ds(SEQ, DEC)
                    sp.dma_start(qh[:, 0, :, 0:DEC].bitcast(F32), rows(s["qh"])[:, :, new]).then_inc(win_in[0], 16)
                    sp.dma_start(ql[:, 0, :, 0:DEC].bitcast(F32), rows(s["ql"])[:, :, new]).then_inc(win_in[0], 16)
                    sp.dma_start(kh[:, 0, :, PAST:PAST + DEC].bitcast(F32), rows(s["kh"])[:, :, new]).then_inc(win_in[0], 16)
                    sp.dma_start(kl[:, 0, :, PAST:PAST + DEC].bitcast(F32), rows(s["kl"])[:, :, new]).then_inc(win_in[0], 16)
                    sp.dma_start(vh[0:DEC, 0, 4, :].bitcast(F32), s["vh"][new, :]).then_inc(win_in[0], 16)
                    sp.dma_start(vl[0:DEC, 0, 4, :].bitcast(F32), s["vl"][new, :]).then_inc(win_in[0], 16)
            store_pair(16, 0, bass.ds(SEQ, DEC), DEC)
            sp.wait_ge(stored[0], 32 * 10)
            sp.wait_ge(stored[1], 32 * 9)

        def pieces(u):
            mq, full = u["mq"], sum(k == P for k in u["keys"])

            def whole(tl, slot):
                flat = tl[:, 0:full * P] if slot is None else tl[:, slot, 0:full * P]
                return flat if mq == P else flat.rearrange("p (t q) -> p t q", q=P)[:, :, 0:mq]

            def rest(tl, slot):
                k = u["keys"][-1]
                return tl[0:k, full * P:full * P + mq] if slot is None else tl[0:k, slot, full * P:full * P + mq]

            return [(0, whole)] + ([(1, rest)] if full < len(u["keys"]) else [])

        def loaded(eng, g):
            eng.wait_ge(win_in[g["slot"]], g["g"] * 48 + (96 - 48 * g["slot"]))

        @block.vector
        def _(dve):
            dve.wait_ge(bias_in, 16)
            nc.vector.memset(bias[0:CHUNK, :, PW - CHUNK:PW], NEG).then_inc(masked, 1)
            nc.vector.memset(bias[CHUNK:P, :, 0:CHUNK], NEG).then_inc(masked, 1)
            dve.wait_ge(masked, 2)

            def run(groups, n0, p0):
                us = units(groups)

                def scores(i):
                    u, half = us[i], us[i]["w"] // 2
                    mq = u["mq"]
                    dve.wait_ge(masked, 2)
                    dve.wait_ge(qk_done, n0 + (i + 1))
                    if i >= 2:
                        dve.wait_ge(ex_done, n0 + (i - 1))
                    dve.sem_inc(sc_turn, 1)
                    nc.vector.tensor_tensor_reduce(
                        out=sc[0:mq, i % 2, 0:2 * half].rearrange("p (a b) -> p a b", a=2),
                        in0=ps_s[0:mq, i % 2, :, 0:half],
                        in1=bias[0:mq, u["h"], u["bias0"]:u["bias0"] + 2 * half].rearrange("p (a b) -> p a b", a=2),
                        scale=-1.0, scalar=3e38, op0=ALU.add, op1=ALU.min,
                        accum_out=nmx[0:mq, i % 2:i % 2 + 1]).then_inc(sc_done, 1)

                def low(i):
                    u = us[i]
                    mq = u["mq"]
                    dve.wait_ge(pth_done, n0 + (i + 1))
                    if i >= 2:
                        dve.wait_ge(pv_done, n0 + (i - 1))
                    for rng, a in pieces(u):
                        last = nc.vector.tensor_tensor(a(ptl, i % 2), a(ps_t, None), a(pth, i % 2).bitcast(F32), ALU.subtract)
                    last.then_inc(ptl_done, 1)

                def normalise(pi, mq):
                    if pi or not isinstance(p0, int) or p0:
                        dve.wait_ge(att_done, p0 + pi)
                    nc.vector.reciprocal(rinv[0:mq, :], rsum[0:mq, pi % 2, :]).then_inc(rinv_done, 1)
                    dve.wait_ge(rinv_done, p0 + (pi + 1))
                    dve.wait_ge(pv_done, n0 + HEADS * (pi + 1))
                    nc.vector.tensor_tensor(att[0:mq, :].rearrange("p (h d) -> p h d", h=HEADS),
                                            ps_o[0:mq, :].rearrange("p (h d) -> p h d", h=HEADS),
                                            rinv[0:mq, :].unsqueeze(2).to_broadcast([mq, HEADS, HD]),
                                            ALU.mult).then_inc(att_done, 1)

                def att_low(pi, mq):
                    dve.wait_ge(ath_done, p0 + (pi + 1))
                    nc.vector.tensor_tensor(atl[:, pi % 2, :, 0:mq], ps_a[:, :, 0:mq],
                                            ath[:, pi % 2, :, 0:mq].bitcast(F32), ALU.subtract).then_inc(atl_done, 1)

                scores(0)
                scores(1)
                for i in range(len(us)):
                    low(i)
                    if i + 2 < len(us):
                        scores(i + 2)
                    if i >= 1 and us[i - 1]["h"] == HEADS - 1:
                        normalise(us[i - 1]["pair"], us[i - 1]["mq"])
                    if i >= 2 and us[i - 2]["h"] == HEADS - 1:
                        att_low(us[i - 2]["pair"], us[i - 2]["mq"])
                normalise(us[-1]["pair"], us[-1]["mq"])
                att_low(us[-1]["pair"], us[-1]["mq"])

            sections(dve, run)

        @block.scalar
        def _(act):
            def run(groups, n0, p0):
                us = units(groups)

                def split_cache():
                    act.wait_ge(cache_in, 32)
                    act.wait_ge(pv_done, 7 * UG)
                    nc.scalar.activation(kh[:, 0, :, 0:PAST], craw[:, 0, :].rearrange("p (c n) -> p c n", c=CD),
                                         ACT.Copy).then_inc(cache_hi, 1)
                    nc.scalar.activation(vh[:, 0, 0:4, :], craw[:, 1, :].rearrange("p (c n) -> p c n", c=CD),
                                         ACT.Copy).then_inc(cache_hi, 1)

                def exp(i):
                    u = us[i]
                    mq, w = u["mq"], u["w"]
                    act.wait_ge(sc_done, n0 + (i + 1))
                    if i >= 2:
                        act.wait_ge(tr_done, n0 + (i - 1))
                    if u["h"] == 0 and u["pair"] >= 2:
                        act.wait_ge(rinv_done, p0 + (u["pair"] - 1))
                    nc.scalar.activation(pr[0:mq, i % 2, 0:w], sc[0:mq, i % 2, 0:w], ACT.Exp, scale=-1.0,
                                         bias=nmx[0:mq, i % 2:i % 2 + 1],
                                         accum_out=rsum[0:mq, u["pair"] % 2, u["h"]:u["h"] + 1]).then_inc(ex_done, 1)

                def high(i):
                    u = us[i]
                    act.wait_ge(tr_done, n0 + (i + 1))
                    if i >= 2:
                        act.wait_ge(pv_done, n0 + (i - 1))
                    for _, a in pieces(u):
                        last = nc.scalar.activation(a(pth, i % 2), a(ps_t, None), ACT.Copy)
                    last.then_inc(pth_done, 1)

                def att_high(pi, mq):
                    act.wait_ge(at_tr, p0 + (pi + 1))
                    act.wait_ge(stored[pi % 2], (p0 + pi) // 2 * 32 + 32 if isinstance(p0, int)
                                else p0 * 16 + 32 * (pi // 2 + 1))
                    nc.scalar.activation(ath[:, pi % 2, :, 0:mq], ps_a[:, :, 0:mq], ACT.Copy).then_inc(ath_done, 1)

                if groups[0]["g"] is SAMPLE["g"]:
                    split_cache()
                exp(0)
                exp(1)
                for i in range(len(us)):
                    high(i)
                    if i + 2 < len(us):
                        exp(i + 2)
                    if i >= 2 and us[i - 2]["h"] == HEADS - 1:
                        att_high(us[i - 2]["pair"], us[i - 2]["mq"])
                att_high(us[-1]["pair"], us[-1]["mq"])

            sections(act, run)

        @block.gpsimd
        def _(pool):
            pool.wait_ge(cache_hi, 2)
            nc.gpsimd.tensor_tensor(kl[:, 0, :, 0:PAST], craw[:, 0, :].rearrange("p (c n) -> p c n", c=CD),
                                    kh[:, 0, :, 0:PAST].bitcast(F32), ALU.subtract).then_inc(cache_lo, 1)
            nc.gpsimd.tensor_tensor(vl[:, 0, 0:4, :], craw[:, 1, :].rearrange("p (c n) -> p c n", c=CD),
                                    vh[:, 0, 0:4, :].bitcast(F32), ALU.subtract).then_inc(cache_lo, 1)

        @block.tensor
        def _(pe):
            def run(groups, n0, p0):
                us = units(groups)

                def scores(i):
                    u, half = us[i], us[i]["w"] // 2
                    ct, part = head(u)
                    mq, sl, q0, k0 = u["mq"], u["slot"], u["q0"], u["tile0"] * P
                    if i == 0 or us[i - 1]["group"] != u["group"]:
                        loaded(pe, u)
                    if i >= 2:
                        pe.wait_ge(sc_done, n0 + (i - 1))
                    for a in range(2):
                        keys = slice(k0 + a * half, k0 + (a + 1) * half)
                        for j, (qt, kt) in enumerate(((qh, kh), (qh, kl), (ql, kh))):
                            mm = nc.tensor.matmul(ps_s[0:mq, i % 2, a, 0:half], qt[part, sl, ct, q0:q0 + mq],
                                                  kt[part, sl, ct, keys], start=j == 0, stop=j == 2)
                    mm.then_inc(qk_done, 1)

                def transposes(i):
                    u = us[i]
                    mq = u["mq"]
                    pe.wait_ge(ex_done, n0 + (i + 1))
                    if i >= 1:
                        pe.wait_ge(ptl_done, n0 + i)
                    for k, wd in enumerate(u["keys"]):
                        mm = nc.tensor.transpose(ps_t[0:wd, k * P:k * P + mq], pr[0:mq, i % 2, k * P:k * P + wd],
                                                 c["ident"][0:mq, 0:mq])
                    mm.then_inc(tr_done, 1)

                def values(i):
                    u = us[i]
                    mq, h = u["mq"], u["h"]
                    pe.wait_ge(ptl_done, n0 + (i + 1))
                    if h == 0 and u["pair"] >= 1:
                        pe.wait_ge(att_done, p0 + u["pair"])
                    for k, wd in enumerate(u["keys"]):
                        for j, (pt, vt) in enumerate(((pth, vh), (pth, vl), (ptl, vh))):
                            mm = nc.tensor.matmul(ps_o[0:mq, h * HD:(h + 1) * HD], pt[0:wd, i % 2, k * P:k * P + mq],
                                                  vt[0:wd, u["slot"], u["tile0"] + k, h * HD:(h + 1) * HD],
                                                  start=k == 0 and j == 0, stop=k == len(u["keys"]) - 1 and j == 2)
                    mm.then_inc(pv_done, 1)

                def att_transposes(pi, mq):
                    pe.wait_ge(att_done, p0 + (pi + 1))
                    if pi >= 1:
                        pe.wait_ge(atl_done, p0 + pi)
                    for k in range(CD):
                        mm = nc.tensor.transpose(ps_a[:, k, 0:mq], att[0:mq, k * P:(k + 1) * P], c["ident"][0:mq, 0:mq])
                    mm.then_inc(at_tr, 1)

                if groups[0]["g"] is SAMPLE["g"]:
                    pe.wait_ge(cache_lo, 2)
                scores(0)
                scores(1)
                for i in range(len(us)):
                    transposes(i)
                    if i + 2 < len(us):
                        scores(i + 2)
                    if i >= 2 and us[i - 2]["h"] == HEADS - 1:
                        att_transposes(us[i - 2]["pair"], us[i - 2]["mq"])
                    if i >= 1:
                        values(i - 1)
                values(len(us) - 1)
                att_transposes(us[-1]["pair"], us[-1]["mq"])

            sections(pe, run)


def finish(nc, t, c, s):
    OU, GU, DU = 8, 2 * KF, 3 * KD
    NU = OU + GU + DU + KD
    D0, E0 = OU + GU, OU + GU + DU
    PARTS = [(0, 8), (8, 16), (16, KF)]
    KE = KD + KP
    T0 = KF + KD
    with ExitStack() as ctx:
        def sb(name, shape, dt=F32):
            return ctx.enter_context(nc.sbuf_tensor("c_" + name, shape, dt))

        def ps(name, shape):
            return ctx.enter_context(nc.psum_tensor("c_" + name, shape, F32))

        def sem(name):
            return ctx.enter_context(nc.semaphore("c_" + name))

        ring = WeightRing(nc, ctx, "c_", KE)
        h = sb("h", [P, KD, N])
        mh, ml = (sb(n, [P, KD, N], F32R) for n in ("mh", "ml"))
        uh, ul = (sb(n, [P, KD, N], F32R) for n in ("uh", "ul"))
        hh, hl = (sb(n, [P, KF, N], F32R) for n in ("hh", "hl"))
        p = sb("p", [P, KP, N])
        ph, pl = (sb(n, [P, KP, N], F32R) for n in ("ph", "pl"))
        sq, ssum, sd, rstd = (sb(n, [P, N]) for n in ("sq", "ssum", "sd", "rstd"))
        g, sig, up = (sb(n, [P, N]) for n in ("g", "sig", "up"))
        hid = sb("hid", [P, N])
        y = sb("y", [P, 2, N])
        acc, acc_p = ps("acc", [P, 2, 512]), ps("acc_p", [P, 2, 512])
        ps_n = ps("ps_n", [P, 512])

        x_in, mix_in, p_in, p_hi, p_lo = (sem(n) for n in ("x_in", "mix_in", "p_in", "p_hi", "p_lo"))
        h_out, u_hi, u_lo, sq_out, sum_out = (sem(n) for n in ("h_out", "u_hi", "u_lo", "sq_out", "sum_out"))
        n_mm, n_sd, n_r = sem("n_mm"), sem("n_sd"), sem("n_r")
        g_out, sig_out, gs_out, up_out, hid_out, hid_hi, hid_lo = (sem(n) for n in (
            "g_out", "sig_out", "gs_out", "up_out", "hid_out", "hid_hi", "hid_lo"))
        e_out, y_out = sem("e_out"), sem("y_out")
        stored = [sem("stored0"), sem("stored1")]
        vec = c["vec"]

        def weights(sp, u):
            if u < OU:
                src, k = t["w_out"][u * P:(u + 1) * P, :], KD
            elif u < D0:
                src, k = t["w_gu"][(u - OU) * P:(u - OU + 1) * P, :], KD
            elif u < E0:
                m, part = divmod(u - D0, 3)
                a, z = PARTS[part]
                src, k = t["w_down"][m * P:(m + 1) * P, a * P:z * P], z - a
            else:
                src, k = t["w_ple"][(u - E0) * P:(u - E0 + 1) * P, :], KE
            ring.load(sp, src, u % 2, k)

        def ktiles(u):
            return KD if u < D0 else (PARTS[(u - D0) % 3][1] - PARTS[(u - D0) % 3][0]) if u < E0 else KE

        def phases(eng, b, step, fstep):
            for u in range(OU):
                step(b, u)
            with eng.Fori(0, KF) as f:
                fstep(b, f)
            for u in range(D0, NU):
                step(b, u)

        block = ctx.enter_context(nc.Block())

        def mix_load(sp, b):
            for dst, src in ((mh, "mh"), (ml, "ml")):
                sp.dma_start(dst[:, :, :].bitcast(F32), s[src].rearrange("(k p) n -> p k n", p=P)[:, :, bass.ds(b * N, N)]).then_inc(mix_in, 16)

        def x_load(sp, b, m):
            sp.dma_start(h[:, m, :], t["x"][bass.ds(b * P, P), m * N:(m + 1) * N]).then_inc(x_in, 16)

        def p_load(sp, b):
            sp.dma_start(p[:, :, :].rearrange("p k n -> p (k n)"), t["p"][bass.ds(b * P, P), :]).then_inc(p_in, 16)

        @block.sync
        def _(sp):
            weights(sp, 0)
            mix_load(sp, 0)
            weights(sp, 1)
            for m in range(KD):
                x_load(sp, 0, m)
            p_load(sp, 0)
            for u in range(2, 4):
                sp.wait_ge(ring.lo_done, u - 1)
                weights(sp, u)
            for q in range(2):
                sp.sem_inc(stored[q], 16)

            def step(b, u):
                if u >= E0:
                    m = u - E0
                    sp.wait_ge(y_out, b * KD + (m + 1))
                    sp.dma_start(t["o_y"][bass.ds(b * P, P), m * N:(m + 1) * N], y[:, m % 2, :]).then_inc(stored[m % 2], 16)
                    x_load(sp, wrapped(b), m)
                if u == D0 + 3:
                    sp.wait_ge(ring.used, b * NU + (OU + 2))
                    mix_load(sp, wrapped(b))
                    sp.wait_ge(p_lo, b + 1)
                    p_load(sp, wrapped(b))
                sp.wait_ge(ring.lo_done, b * NU + (u + 3))
                weights(sp, (u + 4) % NU)

            def fstep(b, f):
                for j in range(2):
                    sp.wait_ge(ring.lo_done, b * NU + f * 2 + (OU + j + 3))
                    ring.load(sp, t["w_gu"][bass.ds(f * (2 * P) + (4 + j) * P, P), :], j, KD)

            with sp.Fori(0, NB) as b:
                for u in range(OU):
                    step(b, u)
                with sp.Fori(0, KF - 2) as f:
                    fstep(b, f)
                for u in range(D0 - 4, NU):
                    step(b, u)
            for q in range(2):
                sp.wait_ge(ring.loaded[q], 16 * (NU * NB // 2 + 2))
                sp.wait_ge(stored[q], 16 * (1 + NB * KD // 2))
            sp.wait_ge(x_in, 16 * KD * (NB + 1))
            sp.wait_ge(mix_in, 32 * (NB + 1))
            sp.wait_ge(p_in, 16 * (NB + 1))

        @block.scalar
        def _(act):
            ring.high(act, 0, 0, 0, KD)
            ring.high(act, 1, 0, 1, KD)

            def tile_out(b, u, n, m, gain):
                act.wait_ge(h_out, b * (2 * KD) + (n + m + 1))
                nc.scalar.activation(uh[:, m, :], h[:, m, :], ACT.Identity,
                                     scale=vec[:, gain + m:gain + m + 1]).then_inc(u_hi, 1)
                if m == 0:
                    if n:
                        act.wait_ge(n_mm, b * 2 + 1)
                    nc.scalar.activation(ssum[:, :], h[:, m, :], ACT.Square).then_inc(sq_out, 1)
                else:
                    if m >= 2:
                        act.wait_ge(sum_out, b * 14 + (n // KD * 7 + m - 1))
                    nc.scalar.activation(sq[:, :], h[:, m, :], ACT.Square).then_inc(sq_out, 1)

            def norm(b, i):
                act.wait_ge(n_mm, b * 2 + (i + 1))
                nc.scalar.activation(sd[:, :], ps_n[:, 0:N], ACT.Sqrt, scale=1.0 / D, bias=c["eps"][:, :]).then_inc(n_sd, 1)

            def step(b, u):
                v = u + 2
                ring.high(act, b * NU + v, b * (NU // 2) + v // 2, v % 2, ktiles(v % NU))
                if u < OU:
                    tile_out(b, u, 0, u, V_GFFN)
                elif u < E0 and (u - D0) % 3 == 2:
                    tile_out(b, u, KD, (u - D0) // 3, V_GPLE)
                elif u >= E0:
                    m = u - E0
                    if m == 0:
                        norm(b, 1)
                    act.wait_ge(g_out, b * T0 + (KF + m + 2))
                    nc.scalar.activation(sig[:, :], g[:, :], ACT.Sigmoid).then_inc(sig_out, 1)
                if u == OU - 1:
                    norm(b, 0)

            def fstep(b, f):
                ring.high(act, b * NU + f * 2 + (OU + 2), b * (NU // 2) + f + (OU // 2 + 1), 0, KD)
                act.wait_ge(g_out, b * T0 + f + 2)
                nc.scalar.activation(sig[:, :], g[:, :], ACT.Sigmoid).then_inc(sig_out, 1)
                ring.high(act, b * NU + f * 2 + (OU + 3), b * (NU // 2) + f + (OU // 2 + 1), 1, KD)
                act.wait_ge(hid_out, b * KF + f + 1)
                nc.scalar.activation(hh[:, bass.ds(f, 1), :], hid[:, :].unsqueeze(1), ACT.Copy).then_inc(hid_hi, 1)

            with act.Fori(0, NB) as b:
                act.wait_ge(p_in, b * 16 + 16)
                act.wait_ge(ring.used, b * NU + 2)
                nc.scalar.activation(ph[:, :, :], p[:, :, :], ACT.Copy).then_inc(p_hi, 1)
                phases(act, b, step, fstep)

        @block.gpsimd
        def _(pool):
            ring.low(pool, 0, 0, KD)
            ring.low(pool, 1, 1, KD)

            def step(b, u):
                ring.low(pool, b * NU + (u + 2), u % 2, ktiles((u + 2) % NU))

            def fstep(b, f):
                for j in range(2):
                    ring.low(pool, b * NU + f * 2 + (OU + j + 2), j, KD)

            with pool.Fori(0, NB) as b:
                phases(pool, b, step, fstep)

        @block.vector
        def _(dve):
            dve.sem_inc(g_out, 1)
            dve.sem_inc(up_out, 1)

            def tile_out(b, u, n, m, gain, q):
                dve.wait_ge(ring.used, b * NU + (u + 3))
                if n == 0 and m == 0:
                    dve.wait_ge(x_in, b * (16 * KD) + 16 * KD)
                nc.vector.tensor_tensor(h[:, m, :], acc[:, q, 0:N], h[:, m, :], ALU.add).then_inc(h_out, 1)
                dve.wait_ge(h_out, b * (2 * KD) + (n + m + 1))
                dve.wait_ge(u_hi, b * (2 * KD) + (n + m + 1))
                nc.vector.scalar_tensor_tensor(ul[:, m, :], h[:, m, :], vec[:, gain + m:gain + m + 1],
                                               uh[:, m, :].bitcast(F32), ALU.mult, ALU.subtract).then_inc(u_lo, 1)
                if m:
                    dve.wait_ge(sq_out, b * (2 * KD) + (n + m + 1))
                    if m >= 2:
                        dve.wait_ge(sum_out, b * 14 + (n // KD * 7 + m - 1))
                    nc.vector.tensor_tensor(ssum[:, :], ssum[:, :], sq[:, :], ALU.add).then_inc(sum_out, 1)

            def norm(b, i):
                dve.wait_ge(n_sd, b * 2 + (i + 1))
                nc.vector.reciprocal(rstd[:, :], sd[:, :]).then_inc(n_r, 1)

            def step(b, u):
                if u < OU:
                    tile_out(b, u, 0, u, V_GFFN, u % 2)
                elif u < E0:
                    m = (u - D0) // 3
                    if (u - D0) % 3 == 2:
                        tile_out(b, u, KD, m, V_GPLE, m % 2)
                else:
                    m = u - E0
                    if m == 0:
                        norm(b, 1)
                    dve.wait_ge(ring.used, b * NU + (u + 3))
                    dve.wait_ge(n_r, b * 2 + 2)
                    nc.vector.tensor_tensor(g[:, :], acc[:, m % 2, 0:N], rstd[:, :], ALU.mult).then_inc(g_out, 1)
                    dve.wait_ge(sig_out, b * T0 + (KF + m + 1))
                    nc.vector.tensor_tensor(up[:, :], acc_p[:, m % 2, 0:N], sig[:, :], ALU.mult).then_inc(e_out, 1)
                    dve.wait_ge(e_out, b * KD + (m + 1))
                    dve.wait_ge(stored[m % 2], b * (8 * KD) + 16 * (m // 2 + 1))
                    nc.vector.tensor_tensor(y[:, m % 2, :], up[:, :], h[:, m, :], ALU.add).then_inc(y_out, 1)
                if u == 1:
                    dve.wait_ge(p_hi, b + 1)
                    nc.vector.tensor_tensor(pl[:, :, :], p[:, :, :], ph[:, :, :].bitcast(F32), ALU.subtract).then_inc(p_lo, 1)
                if u == OU - 1:
                    norm(b, 0)

            def fstep(b, f):
                dve.wait_ge(n_r, b * 2 + 1)
                dve.wait_ge(ring.used, b * NU + f * 2 + (OU + 3))
                nc.vector.tensor_tensor(g[:, :], acc[:, 0, 0:N], rstd[:, :], ALU.mult).then_inc(g_out, 1)
                dve.wait_ge(sig_out, b * T0 + f + 1)
                dve.wait_ge(g_out, b * T0 + f + 2)
                nc.vector.tensor_tensor(g[:, :], g[:, :], sig[:, :], ALU.mult).then_inc(gs_out, 1)
                dve.wait_ge(ring.used, b * NU + f * 2 + (OU + 4))
                nc.vector.tensor_tensor(up[:, :], acc[:, 1, 0:N], rstd[:, :], ALU.mult).then_inc(up_out, 1)
                dve.wait_ge(gs_out, b * KF + f + 1)
                dve.wait_ge(up_out, b * KF + f + 2)
                nc.vector.tensor_tensor(hid[:, :], g[:, :], up[:, :], ALU.mult).then_inc(hid_out, 1)
                dve.wait_ge(hid_out, b * KF + f + 1)
                dve.wait_ge(hid_hi, b * KF + f + 1)
                nc.vector.tensor_tensor(hl[:, bass.ds(f, 1), :], hid[:, :].unsqueeze(1),
                                        hh[:, bass.ds(f, 1), :].bitcast(F32), ALU.subtract).then_inc(hid_lo, 1)

            with dve.Fori(0, NB) as b:
                phases(dve, b, step, fstep)

        @block.tensor
        def _(pe):
            pe.sem_inc(ring.used, 2)

            def w(q):
                return [lambda k: ring.hi[:, q, k, :], lambda k: ring.lo[:, q, k, :]]

            U = [lambda k: uh[:, k, :], lambda k: ul[:, k, :]]
            M = [lambda k: mh[:, k, :], lambda k: ml[:, k, :]]
            H = [lambda k: hh[:, k, :], lambda k: hl[:, k, :]]
            E = [lambda k: ph[:, k, :], lambda k: pl[:, k, :]]
            ALL = [(k, k) for k in range(KD)]

            def norm(b, i):
                pe.wait_ge(sum_out, b * 14 + 7 * (i + 1))
                nc.tensor.matmul(ps_n[:, 0:N], c["ones"][:, :], ssum[:, :], start=True, stop=True).then_inc(n_mm, 1)

            def step(b, u):
                if u == 0:
                    pe.wait_ge(mix_in, b * 32 + 32)
                    pe.wait_ge(g_out, b * T0 + 1)
                if u == E0:
                    pe.wait_ge(u_lo, b * (2 * KD) + 2 * KD)
                    norm(b, 1)
                pe.wait_ge(ring.lo_done, b * NU + (u + 1))
                q = u % 2
                if u < OU:
                    if u >= 2:
                        pe.wait_ge(h_out, b * (2 * KD) + (u - 1))
                    mm = passes(nc, acc[:, q, 0:N], w(q), M, ALL, True, True)
                elif u < E0:
                    m, part = divmod(u - D0, 3)
                    a, z = PARTS[part]
                    if part == 0:
                        if m >= 2:
                            pe.wait_ge(h_out, b * (2 * KD) + (KD + m - 1))
                        elif m:
                            pe.wait_ge(up_out, b * KF + (KF + 1))
                        else:
                            pe.wait_ge(g_out, b * T0 + (KF + 1))
                    if m == 0:
                        pe.wait_ge(hid_lo, b * KF + z)
                    mm = passes(nc, acc[:, m % 2, 0:N], w(q), H, [(k - a, k) for k in range(a, z)], part == 0, part == 2)
                else:
                    m = u - E0
                    if m < 2:
                        pe.wait_ge(h_out, b * (2 * KD) + 2 * KD)
                        pe.wait_ge(p_lo, b + 1)
                    else:
                        pe.wait_ge(g_out, b * T0 + (KF + m))
                        pe.wait_ge(e_out, b * KD + (m - 1))
                    passes(nc, acc[:, m % 2, 0:N], w(q), U, ALL, True, True)
                    mm = passes(nc, acc_p[:, m % 2, 0:N], w(q), E, [(KD + k, k) for k in range(KP)], True, True)
                mm.then_inc(ring.used, 1)
                if u == OU - 1:
                    pe.wait_ge(u_lo, b * (2 * KD) + KD)
                    norm(b, 0)

            def fstep(b, f):
                pe.wait_ge(ring.lo_done, b * NU + f * 2 + (OU + 1))
                pe.wait_ge(g_out, b * T0 + f + 1)
                passes(nc, acc[:, 0, 0:N], w(0), U, ALL, True, True).then_inc(ring.used, 1)
                pe.wait_ge(ring.lo_done, b * NU + f * 2 + (OU + 2))
                pe.wait_ge(up_out, b * KF + f + 1)
                passes(nc, acc[:, 1, 0:N], w(1), U, ALL, True, True).then_inc(ring.used, 1)

            with pe.Fori(0, NB) as b:
                phases(pe, b, step, fstep)


def kernel(x_prompt, x_sample, p_prompt, p_sample, cache_k, cache_v, state_conv, g_mix, w_in, q_gain, k_gain,
           rel_bias, conv_w, conv_b, conv_ln_g, conv_ln_b, w_out, g_ffn, w_gate_up, w_down, g_ple, w_ple_gate,
           w_ple_proj):
    import numpy as np
    import concourse.bacc as bacc
    from concourse.bass_utils import run_bass_kernel_spmd

    a = np.asarray

    def tiles(w):
        k, m = w.shape
        return a(w).reshape(k // P, P, m // P, P).transpose(2, 1, 0, 3).reshape(m, k)

    def blocks(v):
        f = v.shape[1]
        return v.reshape(NB, N, f // P, P).transpose(0, 3, 2, 1).reshape(NB * P, f // P * N)

    def paired(first, second):
        return np.stack([first.reshape(-1, P, first.shape[1]), second.reshape(-1, P, second.shape[1])],
                        1).reshape(-1, first.shape[1])

    def columns(v):
        return a(v).reshape(-1, P).T

    wi = tiles(w_in[0])
    part = [wi[AW * i:AW * (i + 1)] for i in range(5)]
    gu = tiles(w_gate_up[0])
    ins = {
        "x": blocks(np.concatenate([a(x_prompt)[0], a(x_sample)[0]])),
        "p": blocks(np.concatenate([a(p_prompt)[0, 0], a(p_sample)[0, 0]])),
        "w_in": np.concatenate([paired(part[0], part[1]), part[2], paired(part[3], part[4])]),
        "w_out": tiles(w_out[0]),
        "w_gu": paired(gu[:FF], gu[FF:]),
        "w_down": tiles(w_down[0]),
        "w_ple": np.concatenate([tiles(w_ple_gate[0]), tiles(w_ple_proj[0])], 1),
        "ck_rows": a(cache_k)[0, 0, DEC:].reshape(PAST - DEC, AW),
        "cv_rows": a(cache_v)[0, 0, DEC:].reshape(PAST - DEC, AW),
        "ckT": a(cache_k)[0, 0].reshape(PAST, CT, P).transpose(2, 1, 0).reshape(P, CT * PAST),
        "cvT": a(cache_v)[0, 0].reshape(PAST // P, P, AW).transpose(1, 0, 2).reshape(P, PAST // P * AW),
        "state": a(state_conv)[0, 0].T,
        "vec": np.concatenate([
            columns(g_mix), columns(g_ffn), columns(g_ple),
            np.tile(a(q_gain)[0], 2)[:, None], np.tile(a(k_gain)[0], 2)[:, None],
            columns(conv_b), columns(conv_ln_g), columns(conv_ln_b),
            a(conv_w)[0].reshape(TAPS, CT, P).transpose(2, 1, 0).reshape(P, CT * TAPS)], 1),
        "ext": np.tile(np.concatenate([np.repeat(a(rel_bias)[0, :, 256:257], PAST, 1),
                                       a(rel_bias)[0, :, 255:0:-1]], 1), (1, P)),
    }
    outs = {"o_y": (NB * P, KD * N), "o_k": (AW, NT), "o_v": (NT, AW), "o_g": (AW, NT),
            "o_ck": (PAST - DEC, AW), "o_cv": (PAST - DEC, AW)}
    nc = bacc.Bacc("TRN2", target_bir_lowering=False, num_devices=1)
    t, arrays = {}, {}
    for name, v in ins.items():
        arrays["in_" + name] = np.ascontiguousarray(v)
        t[name] = nc.dram_tensor("in_" + name, v.shape, F32, kind="ExternalInput").ap()
    for name, shape in outs.items():
        t[name] = nc.dram_tensor(name, shape, F32, kind="ExternalOutput").ap()
    build(nc, t)
    r = run_bass_kernel_spmd(nc, [arrays], core_ids=[0]).results[0]
    y = r["o_y"].reshape(NB, P, KD, N).transpose(0, 3, 2, 1).reshape(NT, D)
    k, v, g = r["o_k"].T, r["o_v"], r["o_g"].T
    heads = (1, 1, PAST, HEADS, HD)
    return (y[None, :SEQ], y[None, SEQ:],
            k[SEQ - PAST:SEQ].reshape(heads), v[SEQ - PAST:SEQ].reshape(heads), g[None, None, SEQ - HIST:SEQ],
            np.concatenate([r["o_ck"], k[SEQ:]]).reshape(heads), np.concatenate([r["o_cv"], v[SEQ:]]).reshape(heads),
            g[None, None, NT - HIST:])
```

```python
from contextlib import ExitStack

import concourse.bass as bass
from concourse import mybir

F32 = mybir.dt.float32
F32R = mybir.dt.float32r
ACT = mybir.ActivationFunctionType
ALU = mybir.AluOpType
AX = mybir.AxisListType

P = 128
D = 1024
SEQ, DEC = 2048, 32
NT = SEQ + DEC
NB = 5
N = NT // NB
KD = D // P
AW = 512
CT = AW // P
HEADS, HD = 8, 64
CHUNK, PAST = 64, 512
TAPS, HIST = 31, 30
FF = 2816
KF = FF // P
PLE = 256
KP = PLE // P
EPS = 1e-6
NEG = -1e30
TG = 104
NG = N // TG

V_GMIX, V_GFFN, V_GPLE, V_GQ, V_GK, V_CB, V_LG, V_LB, V_CW = 0, 8, 16, 24, 25, 26, 30, 34, 38
NVEC = V_CW + CT * TAPS
GPAD = HIST + SEQ + HIST + DEC
CW = 32
NCH = N // CW
EXT = 767


def build(nc, t):
    with ExitStack() as ctx:
        def sb(name, shape, dt=F32, until=None):
            return (until or ctx).enter_context(nc.sbuf_tensor(name, shape, dt))

        def dram(name, shape, dt):
            return nc.dram_tensor(name, shape, dt, kind="Internal").ap()

        c = {
            "vec": sb("vec", [P, NVEC]), "ones": sb("ones", [P, P]), "ident": sb("ident", [P, P]),
            "eps": sb("eps", [P, 1]), "gq8": sb("gq8", [P, 1]),
            "gw": sb("gw", [P, CT, NCH, HIST + CW]),
            "y": sb("y", [P, CT, N]),
        }
        s = {
            "qh": dram("qh_d", (AW, NT), F32), "ql": dram("ql_d", (AW, NT), F32),
            "kh": dram("kh_d", (AW, NT), F32), "kl": dram("kl_d", (AW, NT), F32),
            "vh": dram("vh_d", (NT, AW), F32), "vl": dram("vl_d", (NT, AW), F32),
            "mh": dram("mh_d", (AW, NT), F32), "ml": dram("ml_d", (AW, NT), F32),
            "ckh": dram("ckh_d", (P, CT * PAST), F32), "ckl": dram("ckl_d", (P, CT * PAST), F32),
            "cvh": dram("cvh_d", (P, CT * PAST), F32), "cvl": dram("cvl_d", (P, CT * PAST), F32),
        }
        with ExitStack() as early:
            c["sel"], c["selT"] = sb("sel", [P, 8, 16], until=early), sb("selT", [16, 8, P], until=early)
            constants(nc, t, c, s)
            project(nc, t, c, s)
        attend(nc, t, c, s)
        finish(nc, t, c, s)


def gw_load(sp, t, gw, w, ch, arrived):
    rows = t["o_g"].rearrange("(c p) n -> p c n", p=P)
    at = w * N + ch * CW if ch < NCH - 1 else w * N + ((w >> 2) * HIST + ch * CW)
    sp.dma_start(gw[:, :, ch, :], rows[:, :, bass.ds(at, HIST + CW)]).then_inc(arrived, 16)


def constants(nc, t, c, s):
    with ExitStack() as ctx:
        vec_in, raw_in, passed, cleared, filled, shaped, zeroed, high, low = (
            ctx.enter_context(nc.semaphore(n)) for n in (
                "vec_in", "raw_in", "passed", "cleared", "filled", "shaped", "zeroed", "high", "low"))
        raw = ctx.enter_context(nc.sbuf_tensor("k_raw", [P, 2, CT * PAST], F32))
        hi, lo = (ctx.enter_context(nc.sbuf_tensor(n, [P, 2, CT * PAST], F32R)) for n in ("k_hi", "k_lo"))
        zero = ctx.enter_context(nc.sbuf_tensor("k_zero", [P, CT, HIST], F32))
        block = ctx.enter_context(nc.Block())
        rows = t["o_g"].rearrange("(c p) n -> p c n", p=P)

        @block.sync
        def _(sp):
            sp.dma_start(raw[:, 0, :], t["ckT"]).then_inc(raw_in, 16)
            sp.dma_start(raw[:, 1, :], t["cvT"]).then_inc(raw_in, 16)
            sp.dma_start(c["vec"][:, :], t["vec"]).then_inc(vec_in, 16)
            sp.dma_start(t["o_ck"], t["ck_rows"]).then_inc(passed, 16)
            sp.dma_start(t["o_cv"], t["cv_rows"]).then_inc(passed, 16)
            sp.dma_start(t["o_g"][:, HIST + SEQ:HIST + SEQ + HIST], t["state"]).then_inc(passed, 16)
            sp.wait_ge(zeroed, 1)
            sp.dma_start(rows[:, :, 0:HIST], zero[:, :, :]).then_inc(passed, 16)
            for q, name in enumerate("kv"):
                sp.wait_ge(high, q + 1)
                sp.dma_start(s["c" + name + "h"], hi[:, q, :].bitcast(F32)).then_inc(passed, 16)
                sp.wait_ge(low, q + 1)
                sp.dma_start(s["c" + name + "l"], lo[:, q, :].bitcast(F32)).then_inc(passed, 16)
            sp.wait_ge(passed, 16 * 8)

        @block.scalar
        def _(act):
            act.wait_ge(raw_in, 32)
            for q in range(2):
                nc.scalar.activation(hi[:, q, :], raw[:, q, :], ACT.Copy).then_inc(high, 1)

        @block.vector
        def _(dve):
            nc.vector.memset(zero[:, :, :], 0.0).then_inc(zeroed, 1)
            nc.vector.memset(c["ones"][:, :], 1.0)
            nc.vector.memset(c["eps"][:, :], EPS)
            nc.vector.memset(c["sel"][:, :, :], 0.0).then_inc(cleared, 1)
            dve.wait_ge(cleared, 1)
            for u in range(8):
                for half in range(2):
                    nc.vector.memset(c["sel"][HD * half:HD * half + HD, u, 2 * u + half:2 * u + half + 1], 1.0)
            dve.wait_ge(vec_in, 16)
            nc.vector.tensor_scalar(c["gq8"][:, :], c["vec"][:, V_GQ:V_GQ + 1], HD ** -0.5, None, ALU.mult)
            for q in range(2):
                dve.wait_ge(high, q + 1)
                nc.vector.tensor_tensor(lo[:, q, :], raw[:, q, :], hi[:, q, :].bitcast(F32), ALU.subtract).then_inc(low, 1)

        @block.gpsimd
        def _(pool):
            nc.gpsimd.memset(c["ident"][:, :], 0.0).then_inc(filled, 1)
            nc.gpsimd.memset(c["selT"][:, :, :], 1.0).then_inc(filled, 1)
            pool.wait_ge(filled, 2)
            nc.gpsimd.affine_select(out=c["ident"][:, :], in_=c["ident"][:, :], compare_op=ALU.not_equal,
                                    fill=1.0, base=0, pattern=[[-1, P]], channel_multiplier=1).then_inc(shaped, 1)
            pool.wait_ge(shaped, 1)
            nc.gpsimd.affine_select(out=c["selT"][:, :, :], in_=c["selT"][:, :, :], compare_op=ALU.is_ge,
                                    fill=0.0, base=0, pattern=[[P, 8], [1, P]],
                                    channel_multiplier=-HD).then_inc(shaped, 1)
            pool.wait_ge(shaped, 2)
            nc.gpsimd.affine_select(out=c["selT"][:, :, :], in_=c["selT"][:, :, :], compare_op=ALU.is_ge,
                                    fill=0.0, base=HD - 1, pattern=[[-P, 8], [-1, P]], channel_multiplier=HD)


def passes(nc, out, w, u, kts, first, last):
    mm = None
    for n, (kw, ku) in enumerate(kts):
        for j, (wp, up) in enumerate(((0, 0), (0, 1), (1, 0))):
            mm = nc.tensor.matmul(out, w[wp](kw), u[up](ku), start=first and n == 0 and j == 0,
                                  stop=last and n == len(kts) - 1 and j == 2)
    return mm


class WeightRing:

    def __init__(self, nc, ctx, tag, kmax):
        self.nc = nc
        self.raw = ctx.enter_context(nc.sbuf_tensor(f"{tag}w_raw", [P, 2, kmax, P], F32))
        self.hi = ctx.enter_context(nc.sbuf_tensor(f"{tag}w_hi", [P, 2, kmax, P], F32R))
        self.lo = ctx.enter_context(nc.sbuf_tensor(f"{tag}w_lo", [P, 2, kmax, P], F32R))
        self.loaded = [ctx.enter_context(nc.semaphore(f"{tag}w_loaded{i}")) for i in range(2)]
        self.hi_done = ctx.enter_context(nc.semaphore(f"{tag}w_hi_done"))
        self.lo_done = ctx.enter_context(nc.semaphore(f"{tag}w_lo_done"))
        self.used = ctx.enter_context(nc.semaphore(f"{tag}w_used"))

    def load(self, sp, src, slot, kts):
        sp.dma_start(self.raw[:, slot, 0:kts, :].rearrange("p k c -> p (k c)"), src).then_inc(self.loaded[slot], 16)

    def high(self, act, v, pair, slot, kts):
        act.wait_ge(self.loaded[slot], pair * 16 + 16)
        act.wait_ge(self.used, v + 1)
        self.nc.scalar.activation(self.hi[:, slot, 0:kts, :], self.raw[:, slot, 0:kts, :],
                                  ACT.Copy).then_inc(self.hi_done, 1)

    def low(self, pool, v, slot, kts):
        pool.wait_ge(self.hi_done, v + 1)
        self.nc.gpsimd.tensor_tensor(self.lo[:, slot, 0:kts, :], self.raw[:, slot, 0:kts, :],
                                     self.hi[:, slot, 0:kts, :].bitcast(F32), ALU.subtract).then_inc(self.lo_done, 1)


def wrapped(b):
    return (b + 1) % NB


def project(nc, t, c, s):
    NU = 20
    QK, VU, GU = 8, 8, 12
    FIN = 10
    with ExitStack() as ctx:
        def sb(name, shape, dt=F32):
            return ctx.enter_context(nc.sbuf_tensor("a_" + name, shape, dt))

        def ps(name, shape):
            return ctx.enter_context(nc.psum_tensor("a_" + name, shape, F32))

        def sem(name):
            return ctx.enter_context(nc.semaphore("a_" + name))

        ring = WeightRing(nc, ctx, "a_", KD)
        x = sb("x", [P, KD, N])
        xsq = sb("xsq", [P, KD, N])
        ssum = sb("ssum", [P, N])
        sd, rstd = sb("sd", [P, N]), sb("rstd", [P, N])
        uh, ul = sb("uh", [P, KD, N], F32R), sb("ul", [P, KD, N], F32R)
        zqk = sb("zqk", [P, QK, N])
        zsq = sb("zsq", [P, 2, N])
        sd16, r16 = sb("sd16", [16, N]), sb("r16", [16, N])
        zn = sb("zn", [P, 2, N])
        znh, znl = sb("znh", [P, 2, N], F32R), sb("znl", [P, 2, N], F32R)
        z = sb("z", [P, 2, N])
        vt = sb("vt", [TG, NG, AW])
        vh, vl = sb("vh", [TG, NG, AW], F32R), sb("vl", [TG, NG, AW], F32R)
        sig = sb("sig", [P, N])
        glu = sb("glu", [P, 2, N])

        acc = ps("acc", [P, 2, 512])
        ps_rs = ps("ps_rs", [P, 512])
        ps_ss = ps("ps_ss", [P, 512])
        ps_bc = ps("ps_bc", [P, 2, 512])
        ps_vt = ps("ps_vt", [P, 2, 512])

        u_read = sem("u_read")
        x_in, x_hi, x_lo, x_sq, x_sum = sem("x_in"), sem("x_hi"), sem("x_lo"), sem("x_sq"), sem("x_sum")
        rs_mm, rs_sd, rs = sem("rs_mm"), sem("rs_sd"), sem("rs")
        z_out, z_sq = sem("z_out"), sem("z_sq")
        ss_mm, ss_sd, ss_r = sem("ss_mm"), sem("ss_sd"), sem("ss_r")
        bc_mm, zn_out, znh_out, znl_out = sem("bc_mm"), sem("zn_out"), sem("znh_out"), sem("znl_out")
        v_tr, v_out, vh_out, vl_out = sem("v_tr"), sem("v_out"), sem("vh_out"), sem("vl_out")
        sig_out, glu_out = sem("sig_out"), sem("glu_out")
        st_qk = [sem("st_q"), sem("st_k")]
        st_v = sem("st_v")
        st_glu = [sem("st_g0"), sem("st_g1")]
        vec = c["vec"]

        def weights(sp, i):
            m = i % NU
            ring.load(sp, t["w_in"][m * P:(m + 1) * P, :], i % 2, KD)

        block = ctx.enter_context(nc.Block())

        @block.sync
        def _(sp):
            sp.dma_start(x[:, :, :].rearrange("p k n -> p (k n)"), t["x"][0:P, :]).then_inc(x_in, 16)
            weights(sp, 0)
            weights(sp, 1)
            for i in range(2, 4):
                sp.wait_ge(ring.lo_done, i - 1)
                weights(sp, i)
            sp.sem_inc(st_v, 48)
            for q in range(2):
                sp.sem_inc(st_qk[q], (32, 48)[q])
                sp.sem_inc(st_glu[q], 32)
            with sp.Fori(0, NB) as b:
                for i in range(NU):
                    if i == 2:
                        sp.wait_ge(x_hi, b * KD + KD)
                        sp.wait_ge(x_lo, b * KD + KD)
                        sp.dma_start(x[:, :, :].rearrange("p k n -> p (k n)"),
                                     t["x"][bass.ds(wrapped(b) * P, P), :]).then_inc(x_in, 16)
                    sp.wait_ge(ring.lo_done, b * NU + (i + 3))
                    weights(sp, i + 4)
                    if FIN <= i < FIN + QK:
                        j = i - FIN
                        m, q = j // 2, j % 2
                        rows = slice(m * P, (m + 1) * P)
                        sp.wait_ge(znl_out, b * QK + (j + 1))
                        sp.dma_start(s["qk"[q] + "h"][rows, bass.ds(b * N, N)], znh[:, q, :].bitcast(F32)).then_inc(st_qk[q], 16)
                        sp.dma_start(s["qk"[q] + "l"][rows, bass.ds(b * N, N)], znl[:, q, :].bitcast(F32)).then_inc(st_qk[q], 16)
                        if q:
                            sp.dma_start(t["o_k"][rows, bass.ds(b * N, N)], zn[:, q, :]).then_inc(st_qk[q], 16)
                    if i == VU + CT:
                        sp.wait_ge(vl_out, b * CT + CT)
                        for dst, src in ((t["o_v"], vt[:, :, :]), (s["vh"], vh[:, :, :].bitcast(F32)),
                                         (s["vl"], vl[:, :, :].bitcast(F32))):
                            sp.dma_start(dst[bass.ds(b * N, N), :].rearrange("(g p) d -> p g d", p=TG),
                                         src).then_inc(st_v, 16)
                    if i > GU and i % 2:
                        m = (i - GU) // 2
                        sp.wait_ge(glu_out, b * CT + (m + 2))
                        rows, cut = slice(m * P, (m + 1) * P), N - DEC
                        sp.dma_start(t["o_g"][rows, bass.ds(b * N + HIST, cut)],
                                     glu[:, m % 2, 0:cut]).then_inc(st_glu[m % 2], 16)
                        sp.dma_start(t["o_g"][rows, bass.ds(b * N + (b >> 2) * HIST + (HIST + cut), DEC)],
                                     glu[:, m % 2, cut:N]).then_inc(st_glu[m % 2], 16)
            for q in range(2):
                sp.wait_ge(ring.loaded[q], 16 * (NU * NB // 2 + 2))
                sp.wait_ge(st_qk[q], (32, 48)[q] * (1 + NB * CT))
                sp.wait_ge(st_glu[q], 32 * (1 + 2 * NB))
            sp.wait_ge(x_in, 16 * (NB + 1))
            sp.wait_ge(st_v, 48 * (NB + 1))

        @block.scalar
        def _(act):
            def square_x(n_in):
                act.wait_ge(x_in, n_in)
                nc.scalar.activation(xsq[:, :, :], x[:, :, :], ACT.Square).then_inc(x_sq, 1)

            def split_x(k):
                nc.scalar.activation(uh[:, k, :], x[:, k, :], ACT.Identity,
                                     scale=vec[:, V_GMIX + k:V_GMIX + k + 1]).then_inc(x_hi, 1)

            def sqrt_rs(n):
                act.wait_ge(rs_mm, n)
                nc.scalar.activation(sd[:, :], ps_rs[:, 0:N], ACT.Sqrt, scale=1.0 / D,
                                     bias=c["eps"][:, :]).then_inc(rs_sd, 1)

            ring.high(act, 0, 0, 0, KD)
            act.wait_ge(x_in, 16)
            for k in range(KD):
                split_x(k)
            ring.high(act, 1, 0, 1, KD)
            square_x(16)
            sqrt_rs(1)
            with act.Fori(0, NB) as b:
                for i in range(NU):
                    if i == NU - 1:
                        act.wait_ge(x_in, b * 16 + 32)
                        for k in range(KD):
                            if k < KD - 1:
                                act.wait_ge(u_read, b * (KD - 1) + (k + 1))
                            else:
                                act.wait_ge(ring.used, b * NU + (i + 3))
                            split_x(k)
                    ring.high(act, b * NU + (i + 2), b * (NU // 2) + (i + 2) // 2, i % 2, KD)
                    if i == 4:
                        square_x(b * 16 + 32)
                    if i < QK:
                        act.wait_ge(z_out, b * NU + (i + 3))
                        if i >= 2:
                            act.wait_ge(ss_mm, b * QK + (i - 1))
                        nc.scalar.activation(zsq[:, i % 2, :], zqk[:, i, :], ACT.Square).then_inc(z_sq, 1)
                    if i == QK:
                        act.wait_ge(ss_mm, b * QK + QK)
                        nc.scalar.activation(sd16[:, :], ps_ss[0:16, 0:N], ACT.Sqrt, scale=1.0 / HD,
                                             bias=c["eps"][0:16, :]).then_inc(ss_sd, 1)
                        sqrt_rs(b + 2)
                    if VU < i <= VU + CT:
                        m = i - 1 - VU
                        act.wait_ge(v_tr, b * CT + (m + 1))
                        act.wait_ge(st_v, b * 48 + 48)
                        nc.scalar.activation(vh[:, :, m * P:(m + 1) * P],
                                             ps_vt[0:TG, m % 2, :].rearrange("p (g d) -> p g d", g=NG),
                                             ACT.Copy).then_inc(vh_out, 1)
                    if FIN <= i < FIN + QK:
                        j = i - FIN
                        q = j % 2
                        act.wait_ge(zn_out, b * QK + (j + 1))
                        nc.scalar.activation(znh[:, q, :], zn[:, q, :], ACT.Copy).then_inc(znh_out, 1)
                    if i > GU and i % 2:
                        m = (i - GU) // 2
                        act.wait_ge(z_out, b * NU + (i + 3))
                        nc.scalar.activation(sig[:, :], z[:, 1, :], ACT.Sigmoid).then_inc(sig_out, 1)

        @block.gpsimd
        def _(pool):
            ring.low(pool, 0, 0, KD)
            ring.low(pool, 1, 1, KD)
            with pool.Fori(0, NB) as b:
                for i in range(NU):
                    ring.low(pool, b * NU + (i + 2), i % 2, KD)

        @block.vector
        def _(dve):
            def sum_x(n):
                dve.wait_ge(x_sq, n)
                nc.vector.tensor_reduce(out=ssum[:, :], in_=xsq[:, :, :].rearrange("p k n -> p n k"),
                                        axis=AX.X, op=ALU.add).then_inc(x_sum, 1)

            def split_x(n, k):
                dve.wait_ge(x_hi, n + (k + 1))
                nc.vector.scalar_tensor_tensor(ul[:, k, :], x[:, k, :], vec[:, V_GMIX + k:V_GMIX + k + 1],
                                               uh[:, k, :].bitcast(F32), ALU.mult, ALU.subtract).then_inc(x_lo, 1)

            for k in range(KD):
                split_x(0, k)
            sum_x(1)
            dve.sem_inc(z_out, 2)
            dve.sem_inc(glu_out, 1)
            with dve.Fori(0, NB) as b:
                for i in range(NU):
                    if i == NU - 1:
                        for k in range(KD):
                            split_x(b * KD + KD, k)
                    if i == 0:
                        dve.wait_ge(rs_sd, b + 1)
                        dve.wait_ge(z_out, b * NU + 2)
                        nc.vector.reciprocal(rstd[:, :], sd[:, :]).then_inc(rs, 1)
                        dve.wait_ge(rs, b + 1)
                    if i == 5:
                        sum_x(b + 2)
                    dve.wait_ge(ring.used, b * NU + (i + 3))
                    if i == VU or (i >= GU and i % 2 == 0):
                        dve.wait_ge(glu_out, b * CT + (max(i - GU, 0) // 2 + 1))
                    dst = zqk[:, i, :] if i < QK else z[:, i % 2, :]
                    nc.vector.tensor_tensor(dst, acc[:, i % 2, 0:N], rstd[:, :], ALU.mult).then_inc(z_out, 1)
                    if i == QK:
                        dve.wait_ge(ss_sd, b + 1)
                        nc.vector.reciprocal(r16[:, :], sd16[:, :]).then_inc(ss_r, 1)
                    if VU < i <= VU + CT:
                        m = i - 1 - VU
                        cols = slice(m * P, (m + 1) * P)
                        tr = ps_vt[0:TG, m % 2, :].rearrange("p (g d) -> p g d", g=NG)
                        dve.wait_ge(vh_out, b * CT + (m + 1))
                        nc.vector.tensor_copy(vt[:, :, cols], tr).then_inc(v_out, 1)
                        nc.vector.tensor_tensor(vl[:, :, cols], tr, vh[:, :, cols].bitcast(F32),
                                                ALU.subtract).then_inc(vl_out, 1)
                    if FIN <= i < FIN + QK:
                        j = i - FIN
                        q = j % 2
                        gain = vec[:, V_GK:V_GK + 1] if q else c["gq8"][:, :]
                        dve.wait_ge(bc_mm, b * QK + (j + 1))
                        dve.wait_ge(st_qk[q], (b * CT + (j // 2 + 1)) * (32, 48)[q])
                        nc.vector.scalar_tensor_tensor(zn[:, q, :], zqk[:, j, :], gain, ps_bc[:, q, 0:N],
                                                       ALU.mult, ALU.mult).then_inc(zn_out, 1)
                        dve.wait_ge(zn_out, b * QK + (j + 1))
                        dve.wait_ge(znh_out, b * QK + (j + 1))
                        nc.vector.tensor_tensor(znl[:, q, :], zn[:, q, :], znh[:, q, :].bitcast(F32),
                                                ALU.subtract).then_inc(znl_out, 1)
                    if i > GU and i % 2:
                        m = (i - GU) // 2
                        dve.wait_ge(sig_out, b * CT + (m + 1))
                        dve.wait_ge(z_out, b * NU + (i + 3))
                        dve.wait_ge(st_glu[m % 2], b * 64 + 32 * (m // 2 + 1))
                        nc.vector.tensor_tensor(glu[:, m % 2, :], z[:, 0, :], sig[:, :],
                                                ALU.mult).then_inc(glu_out, 1)

        @block.tensor
        def _(pe):
            pe.sem_inc(ring.used, 2)

            def sum_x(n):
                pe.wait_ge(x_sum, n)
                nc.tensor.matmul(ps_rs[:, 0:N], c["ones"][:, :], ssum[:, :], start=True, stop=True).then_inc(rs_mm, 1)

            sum_x(1)
            with pe.Fori(0, NB) as b:
                for i in range(NU):
                    pe.wait_ge(ring.lo_done, b * NU + (i + 1))
                    pe.wait_ge(z_out, b * NU + (i + 1))
                    w = [lambda k: ring.hi[:, i % 2, k, :], lambda k: ring.lo[:, i % 2, k, :]]
                    u = [lambda k: uh[:, k, :], lambda k: ul[:, k, :]]
                    if i == 0:
                        for k in range(KD):
                            pe.wait_ge(x_lo, b * KD + (k + 1))
                            mm = passes(nc, acc[:, 0, 0:N], w, u, [(k, k)], k == 0, k == KD - 1)
                    elif i == NU - 1:
                        for k in range(KD):
                            mm = passes(nc, acc[:, i % 2, 0:N], w, u, [(k, k)], k == 0, k == KD - 1)
                            if k < KD - 1:
                                mm.then_inc(u_read, 1)
                    else:
                        mm = passes(nc, acc[:, i % 2, 0:N], w, u, [(k, k) for k in range(KD)], True, True)
                    mm.then_inc(ring.used, 1)
                    if i == QK:
                        sum_x(b + 2)
                    if 1 <= i <= QK:
                        j = i - 1
                        pe.wait_ge(z_sq, b * QK + (j + 1))
                        nc.tensor.matmul(ps_ss[0:16, 0:N], c["sel"][:, j, :], zsq[:, j % 2, :], start=j == 0,
                                         stop=j == QK - 1).then_inc(ss_mm, 1)
                    if VU < i <= VU + CT:
                        m = i - 1 - VU
                        pe.wait_ge(z_out, b * NU + (i + 2))
                        if m >= 2:
                            pe.wait_ge(vl_out, b * CT + (m - 1))
                        for g in range(NG):
                            tr = nc.tensor.transpose(ps_vt[0:TG, m % 2, g * P:(g + 1) * P],
                                                     z[:, (i - 1) % 2, g * TG:(g + 1) * TG], c["ident"][:, :])
                        tr.then_inc(v_tr, 1)
                    if FIN <= i < FIN + QK:
                        j = i - FIN
                        pe.wait_ge(ss_r, b + 1)
                        if j >= 2:
                            pe.wait_ge(zn_out, b * QK + (j - 1))
                        nc.tensor.matmul(ps_bc[:, j % 2, 0:N], c["selT"][:, j, :], r16[:, :], start=True,
                                         stop=True).then_inc(bc_mm, 1)


def attend(nc, t, c, s):
    PQ, GT, WIN, PW = P, 6, 6 * P, 5 * P
    UG = 2 * HEADS
    HP = HEADS // 2
    with ExitStack() as ctx:
        def sb(name, shape, dt=F32):
            return ctx.enter_context(nc.sbuf_tensor("b_" + name, shape, dt))

        def ps(name, shape):
            return ctx.enter_context(nc.psum_tensor("b_" + name, shape, F32))

        def sem(name):
            return ctx.enter_context(nc.semaphore("b_" + name))

        bias = sb("bias", [P, HEADS, PW])
        qh, ql = (sb(n, [P, HP, 2 * PQ], F32R) for n in ("qh", "ql"))
        kh, kl = (sb(n, [P, 2, HP, WIN], F32R) for n in ("kh", "kl"))
        vh, vl = (sb(n, [P, 2, GT, AW], F32R) for n in ("vh", "vl"))
        pr = sb("pr", [P, 2, PW])
        nmx, rsum, rinv = sb("nmx", [P, 2]), sb("rsum", [P, 2]), sb("rinv", [P, 2])
        pth, ptl = (sb(n, [P, 2, GT, 2, 2 * PQ], F32R) for n in ("pth", "ptl"))
        ath, atl = (sb(n, [P, HP, 2 * PQ], F32R) for n in ("ath", "atl"))
        tmp = sb("tmp", [P, N])

        ps_s = ps("ps_s", [P, 2, 2, 512])
        ps_t = ps("ps_t", [P, 1024])
        ps_o = ps("ps_o", [P, 2, 2, 2 * PQ])

        bias_in, masked, gw_in = sem("bias_in"), sem("masked"), sem("gw_in")
        win_in = [sem("win_in0"), sem("win_in1")]
        q_in = [sem(f"q_in{hp}") for hp in range(HP)]
        sc_turn, q_turn = sem("sc_turn"), sem("q_turn")
        qk_done, sc_done, ex_done, rinv_done, pn_done, tr_done = (sem(n) for n in (
            "qk_done", "sc_done", "ex_done", "rinv_done", "pn_done", "tr_done"))
        pth_done, ptl_done, pv_done, ath_done, atl_done = (sem(n) for n in (
            "pth_done", "ptl_done", "pv_done", "ath_done", "atl_done"))
        stored = sem("stored")
        cv_step = sem("cv_step")

        def pair(j, first):
            return {"q0": j * PQ, "j": j, "mq": PQ, "tile0": first, "keys": [P] * (j + 5 - first),
                    "bias0": (first - j) * P}

        FIRST = [{"g": g, "slot": g % 2, "pairs": [pair(j, 4 - 2 * g) for j in range(2)]} for g in range(2)]
        SAMPLE = {"g": 8, "slot": 0,
                  "pairs": [{"q0": 0, "j": 0, "mq": DEC, "tile0": 0, "keys": [P] * 4 + [DEC], "bias0": 0}]}

        def inner(it):
            return [{"g": it * 2 + (2 + k), "slot": k, "pairs": [pair(j, j) for j in range(2)]} for k in range(2)]

        def sections(eng, run):
            run(FIRST, 0, 0, 0)
            with eng.Fori(0, 3) as it:
                run(inner(it), it * (2 * UG) + 2 * UG, it * (2 * HP) + 2 * HP, it * 2 + 2)
            run([SAMPLE], 8 * UG, 8 * HP, 8)

        def units(groups):
            return [{**p, "slot": g["slot"], "hp": hp, "hh": hh, "g": g["g"], "group": k, "w": sum(p["keys"]),
                     "quad": k * HP + hp}
                    for k, g in enumerate(groups) for hp in range(HP) for p in g["pairs"] for hh in range(2)]

        def products(g):
            ps_ = g["pairs"]
            if len(ps_) == 1:
                return [(k, wd, 0, DEC) for k, wd in enumerate(ps_[0]["keys"])]
            lo, lo1 = ps_[0]["tile0"], ps_[1]["tile0"]
            whole = [(a, P, 0, 2 * PQ) for a in range(lo1, 5)]
            return whole + [(a, P, 0, PQ) for a in range(lo, lo1)] + [(5, P, PQ, PQ)]

        def pieces(u):
            mq, full, q0, a = u["mq"], sum(k == P for k in u["keys"]), u["q0"], u["tile0"]
            flat = ps_t[:, 0:full * P].rearrange("p (t q) -> p t q", q=P)[:, :, 0:mq]
            out = [(flat, lambda tl: tl[:, u["quad"] % 2, a:a + full, u["hh"], q0:q0 + mq])]
            if full < len(u["keys"]):
                k = u["keys"][-1]
                out.append((ps_t[0:k, full * P:full * P + mq],
                            lambda tl: tl[0:k, u["quad"] % 2, a + full, u["hh"], q0:q0 + mq]))
            return out

        def rows(d):
            return d.rearrange("(c p) n -> p c n", p=P)

        block = ctx.enter_context(nc.Block())

        @block.sync
        def _(sp):
            def load_window(g):
                sl, at = g["slot"], g["g"]
                short = (2 - at) * 2 * PQ if isinstance(at, int) and at < 2 else 0
                k0 = at * (2 * PQ) - (PAST - short)
                for dst, src in ((kh, "kh"), (kl, "kl")):
                    sp.dma_start(dst[:, sl, :, short:WIN].bitcast(F32),
                                 rows(s[src])[:, :, bass.ds(k0, WIN - short)]).then_inc(win_in[sl], 16)
                for dst, src in ((vh, "vh"), (vl, "vl")):
                    sp.dma_start(dst[:, sl, short // P:GT, :].bitcast(F32),
                                 s[src][bass.ds(k0, WIN - short), :].rearrange("(t p) d -> p t d", p=P)).then_inc(win_in[sl], 16)

            def load_q(n, c0, width):
                for hp in range(HP):
                    if not (isinstance(n, int) and n == 0):
                        sp.wait_ge(qk_done, n * UG + 4 * (hp + 1) - UG)
                        sp.sem_inc(q_turn, 1)
                    for dst, src in ((qh, "qh"), (ql, "ql")):
                        sp.dma_start(dst[:, hp, 0:width].bitcast(F32),
                                     s[src][hp * P:(hp + 1) * P, bass.ds(c0, width)]).then_inc(q_in[hp], 16)

            def store_group(n, c0, width):
                sp.wait_ge(atl_done, n * HP + HP)
                for dst, src in ((s["mh"], ath), (s["ml"], atl)):
                    sp.dma_start(rows(dst)[:, :, c0], src[:, :, 0:width].bitcast(F32)).then_inc(stored, 16)

            G = 2 * PQ
            load_q(0, 0, G)
            load_window(FIRST[0])
            ext = t["ext"]
            sp.dma_start(bias[:, :, :], bass.AP(ext.tensor, P - 1, [[EXT - 1, P], [P * EXT, HEADS], [1, PW]])).then_inc(bias_in, 16)
            for ch in range(NCH):
                gw_load(sp, t, c["gw"], 0, ch, gw_in)
            load_window(FIRST[1])
            sp.sem_inc(stored, 32)

            def group(n, last):
                load_q(n + 1, SEQ if last else (n + 1) * G, DEC if last else G)
                store_group(n, bass.ds(n * G, G), G)
                sp.wait_ge(pv_done, n * HP + HP)

            for k in range(2):
                group(k, False)
                load_window({"g": 2 + k, "slot": k})
            with sp.Fori(0, 2) as it:
                for k in range(2):
                    group(it * 2 + (2 + k), False)
                    load_window({"g": it * 2 + (4 + k), "slot": k})
            group(6, False)
            new = bass.ds(SEQ, DEC)
            for dst, name in ((kh, "kh"), (kl, "kl")):
                sp.dma_start(dst[:, 0, :, PAST:PAST + DEC].bitcast(F32), rows(s[name])[:, :, new]).then_inc(win_in[0], 16)
                sp.dma_start(dst[:, 0, :, 0:PAST].bitcast(F32),
                             s["c" + name].rearrange("p (c n) -> p c n", c=HP)).then_inc(win_in[0], 16)
            for dst, name in ((vh, "vh"), (vl, "vl")):
                sp.dma_start(dst[0:DEC, 0, 4, :].bitcast(F32), s[name][new, :]).then_inc(win_in[0], 16)
                sp.dma_start(dst[:, 0, 0:4, :].bitcast(F32),
                             s["c" + name].rearrange("p (c n) -> p c n", c=HP)).then_inc(win_in[0], 16)
            group(7, True)
            store_group(8, bass.ds(SEQ, DEC), DEC)
            sp.wait_ge(stored, 32 * 10)

        @block.gpsimd
        def _(pool):
            y, gw, vec = c["y"], c["gw"], c["vec"]
            pool.wait_ge(gw_in, 16 * NCH)
            n = 0
            for ct in range(CT):
                yc = y[:, ct, :].rearrange("p (a b) -> p a b", b=CW)
                w0 = V_CW + ct * TAPS
                nc.gpsimd.tensor_scalar(yc, gw[:, ct, :, 0:CW], vec[:, w0:w0 + 1],
                                        vec[:, V_CB + ct:V_CB + ct + 1], ALU.mult, ALU.add).then_inc(cv_step, 1)
            for k in range(1, TAPS):
                for ct in range(CT):
                    yc = y[:, ct, :].rearrange("p (a b) -> p a b", b=CW)
                    tc = tmp[:, :].rearrange("p (a b) -> p a b", b=CW)
                    wk = V_CW + ct * TAPS + k
                    pool.wait_ge(cv_step, CT + 2 * n)
                    nc.gpsimd.tensor_scalar(tc, gw[:, ct, :, k:k + CW], vec[:, wk:wk + 1], 0.0,
                                            ALU.mult, ALU.add).then_inc(cv_step, 1)
                    pool.wait_ge(cv_step, CT + 2 * n + 1)
                    nc.gpsimd.tensor_tensor(yc, yc, tc, ALU.add).then_inc(cv_step, 1)
                    n += 1

        @block.vector
        def _(dve):
            dve.wait_ge(bias_in, 16)
            nc.vector.memset(bias[0:CHUNK, :, PW - CHUNK:PW], NEG).then_inc(masked, 1)
            nc.vector.memset(bias[CHUNK:P, :, 0:CHUNK], NEG).then_inc(masked, 1)

            def run(groups, n0, k0, g0):
                us = units(groups)
                last_of = {u["quad"]: i for i, u in enumerate(us)}
                quad_done = {i: q for q, i in last_of.items()}

                def scores(i):
                    u, half = us[i], us[i]["w"] // 2
                    mq, h = u["mq"], 2 * u["hp"] + u["hh"]
                    dve.wait_ge(masked, 2)
                    dve.wait_ge(qk_done, n0 + (i + 1))
                    if i >= 2:
                        dve.wait_ge(tr_done, n0 + (i - 1))
                    dve.sem_inc(sc_turn, 1)
                    nc.vector.tensor_tensor_reduce(
                        out=pr[0:mq, i % 2, 0:2 * half].rearrange("p (a b) -> p a b", a=2),
                        in0=ps_s[0:mq, i % 2, :, 0:half],
                        in1=bias[0:mq, h, u["bias0"]:u["bias0"] + 2 * half].rearrange("p (a b) -> p a b", a=2),
                        scale=-1.0, scalar=3e38, op0=ALU.add, op1=ALU.min,
                        accum_out=nmx[0:mq, i % 2:i % 2 + 1]).then_inc(sc_done, 1)

                def normalise(i):
                    u = us[i]
                    mq, w, q = u["mq"], u["w"], i % 2
                    dve.wait_ge(ex_done, n0 + (i + 1))
                    if not (isinstance(n0, int) and n0 + i < 2):
                        dve.wait_ge(pn_done, n0 + (i - 1))
                    nc.vector.reciprocal(rinv[0:mq, q:q + 1], rsum[0:mq, q:q + 1]).then_inc(rinv_done, 1)
                    dve.wait_ge(rinv_done, n0 + (i + 1))
                    nc.vector.tensor_scalar(pr[0:mq, q, 0:w], pr[0:mq, q, 0:w], rinv[0:mq, q:q + 1], None,
                                            ALU.mult).then_inc(pn_done, 1)

                def low(i):
                    u = us[i]
                    dve.wait_ge(pth_done, n0 + (i + 1))
                    for src, dst in pieces(u):
                        last = nc.vector.tensor_tensor(dst(ptl), src, dst(pth).bitcast(F32), ALU.subtract)
                    last.then_inc(ptl_done, 1)

                def out_low(k):
                    u = us[last_of[k]]
                    wd = 2 * PQ if u["mq"] == P else DEC
                    dve.wait_ge(ath_done, k0 + (k + 1))
                    for hh in range(2):
                        part = slice(HD * hh, HD * hh + HD)
                        last = nc.vector.tensor_tensor(atl[part, u["hp"], 0:wd], ps_o[part, k % 2, hh, 0:wd],
                                                       ath[part, u["hp"], 0:wd].bitcast(F32), ALU.subtract)
                    last.then_inc(atl_done, 1)

                scores(0)
                scores(1)
                normalise(0)
                for i in range(len(us)):
                    if i + 1 < len(us):
                        normalise(i + 1)
                    low(i)
                    if i + 2 < len(us):
                        scores(i + 2)
                    if i >= 4 and i - 4 in quad_done and quad_done[i - 4] >= 0 and us[i]["mq"] == P:
                        out_low(quad_done[i - 4])
                    if i >= 2 and us[i]["mq"] != P and i - 2 in quad_done:
                        out_low(quad_done[i - 2])
                out_low(us[-1]["quad"])

            sections(dve, run)

        @block.scalar
        def _(act):
            def run(groups, n0, k0, g0):
                us = units(groups)
                last_of = {u["quad"]: i for i, u in enumerate(us)}
                quad_done = {i: q for q, i in last_of.items()}

                def exp(i):
                    u = us[i]
                    mq, w, q = u["mq"], u["w"], i % 2
                    act.wait_ge(sc_done, n0 + (i + 1))
                    nc.scalar.activation(pr[0:mq, q, 0:w], pr[0:mq, q, 0:w], ACT.Exp, scale=-1.0,
                                         bias=nmx[0:mq, q:q + 1], accum_out=rsum[0:mq, q:q + 1]).then_inc(ex_done, 1)

                def high(i):
                    u = us[i]
                    act.wait_ge(tr_done, n0 + (i + 1))
                    if u["quad"] >= 2:
                        act.wait_ge(pv_done, k0 + (u["quad"] - 1))
                    for src, dst in pieces(u):
                        last = nc.scalar.activation(dst(pth), src, ACT.Copy)
                    last.then_inc(pth_done, 1)

                def out_high(k):
                    u = us[last_of[k]]
                    wd = 2 * PQ if u["mq"] == P else DEC
                    act.wait_ge(pv_done, k0 + (k + 1))
                    if u["hp"] == 0:
                        act.wait_ge(stored, g0 * 32 + 32 * (u["group"] + 1))
                    for hh in range(2):
                        part = slice(HD * hh, HD * hh + HD)
                        last = nc.scalar.activation(ath[part, u["hp"], 0:wd], ps_o[part, k % 2, hh, 0:wd], ACT.Copy)
                    last.then_inc(ath_done, 1)

                exp(0)
                exp(1)
                for i in range(len(us)):
                    high(i)
                    if i + 2 < len(us):
                        exp(i + 2)
                    if i >= 4 and us[i]["mq"] == P and i - 4 in quad_done:
                        out_high(quad_done[i - 4])
                    if i >= 2 and us[i]["mq"] != P and i - 2 in quad_done:
                        out_high(quad_done[i - 2])
                out_high(us[-1]["quad"])

            sections(act, run)

        @block.tensor
        def _(pe):
            def run(groups, n0, k0, g0):
                us = units(groups)
                per = len(us) // (HP * len(groups))

                def scores(i):
                    u, half = us[i], us[i]["w"] // 2
                    part, ct = slice(HD * u["hh"], HD * u["hh"] + HD), u["hp"]
                    mq, sl, q0, at = u["mq"], u["slot"], u["q0"], u["tile0"] * P
                    if i == 0 or us[i - 1]["group"] != u["group"]:
                        got = 64 * 4 + 16 * 8 if mq != P else u["g"] * 32 + (64 - 32 * sl)
                        pe.wait_ge(win_in[sl], got)
                    if u["hh"] == 0 and u["j"] == 0:
                        pe.wait_ge(q_in[ct], u["g"] * 32 + 32)
                    if i >= 2:
                        pe.wait_ge(sc_done, n0 + (i - 1))
                    for a in range(2):
                        keys = slice(at + a * half, at + (a + 1) * half)
                        for j, (qt, kt) in enumerate(((qh, kh), (qh, kl), (ql, kh))):
                            mm = nc.tensor.matmul(ps_s[0:mq, i % 2, a, 0:half], qt[part, ct, q0:q0 + mq],
                                                  kt[part, sl, ct, keys], start=j == 0, stop=j == 2)
                    mm.then_inc(qk_done, 1)

                def transposes(i):
                    u = us[i]
                    mq = u["mq"]
                    pe.wait_ge(pn_done, n0 + (i + 1))
                    if i >= 1:
                        pe.wait_ge(ptl_done, n0 + i)
                    for k, wd in enumerate(u["keys"]):
                        mm = nc.tensor.transpose(ps_t[0:wd, k * P:k * P + mq], pr[0:mq, i % 2, k * P:k * P + wd],
                                                 c["ident"][0:mq, 0:mq])
                    mm.then_inc(tr_done, 1)

                def values(k, part):
                    u = us[k * per]
                    todo = products(groups[u["group"]])
                    n = len(todo)
                    if part == 0:
                        pe.wait_ge(ptl_done, n0 + per * (k + 1))
                        if k >= 2:
                            pe.wait_ge(atl_done, k0 + (k - 1))
                    mm = None
                    for x in range(n * part // per, n * (part + 1) // per):
                        a, wd, q0, nq = todo[x]
                        for j, (pt, vt) in enumerate(((pth, vh), (ptl, vh), (pth, vl))):
                            mm = nc.tensor.matmul(ps_o[:, k % 2, :, q0:q0 + nq],
                                                  vt[0:wd, u["slot"], a, u["hp"] * P:(u["hp"] + 1) * P],
                                                  pt[0:wd, k % 2, a, :, q0:q0 + nq],
                                                  start=x == 0 and j == 0, stop=x == n - 1 and j == 2)
                    if part == per - 1:
                        mm.then_inc(pv_done, 1)

                scores(0)
                scores(1)
                for i in range(len(us)):
                    transposes(i)
                    if i + 2 < len(us):
                        scores(i + 2)
                    if i >= per:
                        values(i // per - 1, i % per)
                for part in range(per):
                    values(us[-1]["quad"], part)

            sections(pe, run)


def finish(nc, t, c, s):
    OU, HF = 8, KF // 2
    HU = 2 * HF + KD
    GU = [OU, OU + HU]
    DU = [g + 2 * HF for g in GU]
    E0 = OU + 2 * HU
    NU = E0 + KD
    KE = KD + KP
    T0 = KF + KD
    NTAP = CT * TAPS
    with ExitStack() as ctx:
        def sb(name, shape, dt=F32):
            return ctx.enter_context(nc.sbuf_tensor("c_" + name, shape, dt))

        def ps(name, shape):
            return ctx.enter_context(nc.psum_tensor("c_" + name, shape, F32))

        def sem(name):
            return ctx.enter_context(nc.semaphore("c_" + name))

        ring = WeightRing(nc, ctx, "c_", HF)
        h = sb("h", [P, KD, N])
        mh, ml = (sb(n, [P, KD, N], F32R) for n in ("mh", "ml"))
        uh, ul = (sb(n, [P, KD, N], F32R) for n in ("uh", "ul"))
        hh, hl = (sb(n, [P, HF, N], F32R) for n in ("hh", "hl"))
        p = sb("p", [P, KP, N])
        ph, pl = (sb(n, [P, KP, N], F32R) for n in ("ph", "pl"))
        sq, ssum, sd, rstd = (sb(n, [P, N]) for n in ("sq", "ssum", "sd", "rstd"))
        g, sig, up = (sb(n, [P, N]) for n in ("g", "sig", "up"))
        hid = sb("hid", [P, N])
        yo = sb("yo", [P, 2, N])
        y, gw = c["y"], c["gw"]
        cx = sb("cx", [P, CT, N])
        csum, csd, crs = (sb(n, [P, N]) for n in ("csum", "csd", "crs"))
        acc, acc_p = ps("acc", [P, 2, 512]), ps("acc_p", [P, 2, 512])
        ps_n, ps_c = ps("ps_n", [P, 512]), ps("ps_c", [P, 512])

        x_in = [sem(f"x_in{m}") for m in range(KD)]
        mix_in, p_in, p_hi, p_lo, gw_in = (sem(n) for n in ("mix_in", "p_in", "p_hi", "p_lo", "gw_in"))
        left = sem("left")
        u_hi, u_lo, sq_out, sum_out = (sem(n) for n in ("u_hi", "u_lo", "sq_out", "sum_out"))
        n_mm, n_sd, n_r = sem("n_mm"), sem("n_sd"), sem("n_r")
        sig_out, gs_out, hid_out, hid_hi, hid_lo = (sem(n) for n in (
            "sig_out", "gs_out", "hid_out", "hid_hi", "hid_lo"))
        e_out, y_out = sem("e_out"), sem("y_out")
        stored = [sem("stored0"), sem("stored1")]
        tap = sem("tap")
        cv_sum, cv_mm, cv_xc, cv_sq, cv_sd, cv_r, cv_xn, cv_aff, cv_out, cv_hi, cv_lo = (sem("cv_" + n) for n in (
            "sum", "mm", "xc", "sq", "sd", "r", "xn", "aff", "out", "hi", "lo"))
        vec = c["vec"]

        def place(u):
            if u < OU:
                return "out", 0, u
            if u >= E0:
                return "ple", 0, u - E0
            half, r = divmod(u - OU, HU)
            return ("gu", half, r) if r < 2 * HF else ("down", half, r - 2 * HF)

        def ktiles(u):
            return {"out": KD, "gu": KD, "down": HF, "ple": KE}[place(u)[0]]

        def weights(sp, u):
            kind, half, m = place(u)
            if kind == "out":
                src = t["w_out"][m * P:(m + 1) * P, :]
            elif kind == "gu":
                r = half * 2 * HF + m
                src = t["w_gu"][r * P:(r + 1) * P, :]
            elif kind == "down":
                src = t["w_down"][m * P:(m + 1) * P, half * HF * P:(half + 1) * HF * P]
            else:
                src = t["w_ple"][m * P:(m + 1) * P, :]
            ring.load(sp, src, u % 2, ktiles(u))

        def phases(eng, b, step, fstep, cut=0, peel=0, first=0):
            for u in range(OU):
                step(b, u)
            for half in range(2):
                start = 0 if half else first
                for f in range(start):
                    fstep(b, half, f)
                with eng.Fori(start, HF - cut // 2 - peel) as f:
                    fstep(b, half, f)
                for f in range(HF - peel, HF):
                    fstep(b, half, f)
                for u in range(DU[half] - cut, DU[half] + KD):
                    step(b, u)
            for u in range(E0, NU):
                step(b, u)

        block = ctx.enter_context(nc.Block())

        def mix_load(sp, b):
            for dst, src in ((mh, "mh"), (ml, "ml")):
                sp.dma_start(dst[:, 0:CT, :].bitcast(F32),
                             s[src].rearrange("(k p) n -> p k n", p=P)[:, :, bass.ds(b * N, N)]).then_inc(mix_in, 16)

        def x_load(sp, b, m):
            sp.dma_start(h[:, m, :], t["x"][bass.ds(b * P, P), m * N:(m + 1) * N]).then_inc(x_in[m], 16)

        def p_load(sp, b):
            sp.dma_start(p[:, :, :].rearrange("p k n -> p (k n)"), t["p"][bass.ds(b * P, P), :]).then_inc(p_in, 16)

        @block.sync
        def _(sp):
            weights(sp, 0)
            mix_load(sp, 0)
            weights(sp, 1)
            for m in range(KD):
                x_load(sp, 0, m)
            p_load(sp, 0)
            for u in range(2, 4):
                sp.wait_ge(ring.lo_done, u - 1)
                weights(sp, u)
            for q in range(2):
                sp.sem_inc(stored[q], 16)

            def step(b, u):
                if u >= E0:
                    m = u - E0
                    sp.wait_ge(y_out, b * KD + (m + 1))
                    sp.dma_start(t["o_y"][bass.ds(b * P, P), m * N:(m + 1) * N], yo[:, m % 2, :]).then_inc(stored[m % 2], 16)
                    x_load(sp, wrapped(b), m)
                if 1 <= u <= 7:
                    for ch in range(2 * u - 2, min(2 * u, NCH)):
                        gw_load(sp, t, gw, wrapped(b), ch, gw_in)
                if u == DU[0] + 3:
                    sp.wait_ge(ring.used, b * NU + (OU + 2))
                    mix_load(sp, wrapped(b))
                    sp.wait_ge(p_lo, b + 1)
                    p_load(sp, wrapped(b))
                sp.wait_ge(ring.lo_done, b * NU + (u + 3))
                if u == 0:
                    sp.wait_ge(tap, b * NTAP + 1)
                weights(sp, (u + 4) % NU)

            def fstep(b, half, f):
                for j in range(2):
                    sp.wait_ge(ring.lo_done, b * NU + f * 2 + (GU[half] + j + 3))
                    ring.load(sp, t["w_gu"][bass.ds(f * (2 * P) + (half * 2 * HF + 4 + j) * P, P), :], j, KD)

            with sp.Fori(0, NB) as b:
                phases(sp, b, step, fstep, 4)
            for q in range(2):
                sp.wait_ge(ring.loaded[q], 16 * (NU * NB // 2 + 2))
                sp.wait_ge(stored[q], 16 * (1 + NB * KD // 2))
            for m in range(KD):
                sp.wait_ge(x_in[m], 16 * (NB + 1))
            sp.wait_ge(mix_in, 32 * (NB + 1))
            sp.wait_ge(p_in, 16 * (NB + 1))

        @block.scalar
        def _(act):
            ring.high(act, 0, 0, 0, KD)
            ring.high(act, 1, 0, 1, KD)

            def tail(n, stage):
                if stage == "square":
                    act.wait_ge(cv_xc, n * CT + CT)
                    nc.scalar.activation(cx[:, :, :], y[:, :, :], ACT.Square).then_inc(cv_sq, 1)
                elif stage == "sd":
                    act.wait_ge(cv_mm, n * 2 + 2)
                    nc.scalar.activation(csd[:, :], ps_c[:, 0:N], ACT.Sqrt, scale=1.0 / AW, bias=c["eps"][:, :]).then_inc(cv_sd, 1)
                elif stage == "high":
                    act.wait_ge(cv_out, n + 1)
                    nc.scalar.activation(mh[:, CT:KD, :], cx[:, :, :], ACT.Copy).then_inc(cv_hi, 1)
                else:
                    act.wait_ge(cv_xn, n * CT + (stage + 1))
                    gain, off = (vec[:, v + stage:v + stage + 1] for v in (V_LG, V_LB))
                    nc.scalar.activation(cx[:, stage, :], y[:, stage, :], ACT.Identity, scale=gain, bias=off).then_inc(cv_aff, 1)
                    act.wait_ge(cv_aff, n * (2 * CT) + (2 * stage + 1))
                    nc.scalar.activation(y[:, stage, :], y[:, stage, :], ACT.Sigmoid, scale=gain, bias=off).then_inc(cv_aff, 1)

            def tile_out(b, u, n, m, gain):
                act.wait_ge(left, b * NU + (u + 3))
                nc.scalar.activation(uh[:, m, :], h[:, m, :], ACT.Identity,
                                     scale=vec[:, gain + m:gain + m + 1]).then_inc(u_hi, 1)
                if m == 0:
                    if n:
                        act.wait_ge(n_mm, b * 2 + 1)
                    nc.scalar.activation(ssum[:, :], h[:, m, :], ACT.Square).then_inc(sq_out, 1)
                else:
                    if m >= 2:
                        act.wait_ge(sum_out, b * 14 + (n // KD * 7 + m - 1))
                    nc.scalar.activation(sq[:, :], h[:, m, :], ACT.Square).then_inc(sq_out, 1)

            def norm(b, i):
                act.wait_ge(n_mm, b * 2 + (i + 1))
                nc.scalar.activation(sd[:, :], ps_n[:, 0:N], ACT.Sqrt, scale=1.0 / D, bias=c["eps"][:, :]).then_inc(n_sd, 1)

            def step(b, u):
                v = u + 2
                kind, half, m = place(u)
                ring.high(act, b * NU + v, b * (NU // 2) + v // 2, v % 2, ktiles(v % NU))
                if kind == "out":
                    tile_out(b, u, 0, m, V_GFFN)
                elif kind == "down" and half:
                    tile_out(b, u, KD, m, V_GPLE)
                elif kind == "ple":
                    if m == 0:
                        norm(b, 1)
                    act.wait_ge(left, b * NU + (u + 3))
                    nc.scalar.activation(sig[:, :], g[:, :], ACT.Sigmoid).then_inc(sig_out, 1)
                if u == 3:
                    act.wait_ge(p_in, b * 16 + 16)
                    nc.scalar.activation(ph[:, :, :], p[:, :, :], ACT.Copy).then_inc(p_hi, 1)
                if u == OU - 1:
                    norm(b, 0)
                if u == DU[1] + 3:
                    tail(b + 1, "square")
                if u == DU[1] + 6:
                    tail(b + 1, "sd")
                if E0 < u <= E0 + CT:
                    tail(b + 1, u - E0 - 1)
                if u == E0 + 5:
                    tail(b + 1, "high")

            def fstep(b, half, f):
                n, kts = half * HF, ktiles(DU[half]) if isinstance(f, int) else KD
                ring.high(act, b * NU + f * 2 + (GU[half] + 2), b * (NU // 2) + f + (GU[half] // 2 + 1), 0, kts)
                act.wait_ge(left, b * NU + f * 2 + (GU[half] + 3))
                nc.scalar.activation(sig[:, :], g[:, :], ACT.Sigmoid).then_inc(sig_out, 1)
                ring.high(act, b * NU + f * 2 + (GU[half] + 3), b * (NU // 2) + f + (GU[half] // 2 + 1), 1, kts)
                act.wait_ge(hid_out, b * KF + f + (n + 1))
                nc.scalar.activation(hh[:, bass.ds(f, 1), :], hid[:, :].unsqueeze(1), ACT.Copy).then_inc(hid_hi, 1)

            for stage in ("square", "sd", 0, 1, 2, 3, "high"):
                tail(0, stage)
            with act.Fori(0, NB) as b:
                phases(act, b, step, fstep, peel=1)

        @block.gpsimd
        def _(pool):
            ring.low(pool, 0, 0, KD)
            ring.low(pool, 1, 1, KD)

            def step(b, u):
                ring.low(pool, b * NU + (u + 2), u % 2, ktiles((u + 2) % NU))

            def fstep(b, half, f):
                for j in range(2):
                    ring.low(pool, b * NU + f * 2 + (GU[half] + j + 2), j, ktiles(DU[half]) if isinstance(f, int) else KD)

            with pool.Fori(0, NB) as b:
                phases(pool, b, step, fstep, peel=1)

        @block.vector
        def _(dve):
            dve.sem_inc(left, 2)
            dve.sem_inc(tap, 1)

            def tail(n, stage):
                if stage == "sum":
                    nc.vector.tensor_reduce(out=csum[:, :], in_=y[:, :, :].rearrange("p c n -> p n c"),
                                            axis=AX.X, op=ALU.add).then_inc(cv_sum, 1)
                elif stage == "center":
                    dve.wait_ge(cv_mm, n * 2 + 1)
                    for ct in range(CT):
                        nc.vector.scalar_tensor_tensor(y[:, ct, :], ps_c[:, 0:N], -1.0 / AW, y[:, ct, :],
                                                       ALU.mult, ALU.add).then_inc(cv_xc, 1)
                elif stage == "sum2":
                    dve.wait_ge(cv_sq, n + 1)
                    nc.vector.tensor_reduce(out=csum[:, :], in_=cx[:, :, :].rearrange("p c n -> p n c"),
                                            axis=AX.X, op=ALU.add).then_inc(cv_sum, 1)
                elif stage == "scale":
                    dve.wait_ge(cv_sd, n + 1)
                    nc.vector.reciprocal(crs[:, :], csd[:, :]).then_inc(cv_r, 1)
                    dve.wait_ge(cv_r, n + 1)
                    for ct in range(CT):
                        nc.vector.tensor_tensor(y[:, ct, :], y[:, ct, :], crs[:, :], ALU.mult).then_inc(cv_xn, 1)
                elif stage == "swish":
                    dve.wait_ge(cv_aff, n * (2 * CT) + 2 * CT)
                    nc.vector.tensor_tensor(cx[:, :, :], cx[:, :, :], y[:, :, :], ALU.mult).then_inc(cv_out, 1)
                else:
                    dve.wait_ge(cv_hi, n + 1)
                    nc.vector.tensor_tensor(ml[:, CT:KD, :], cx[:, :, :], mh[:, CT:KD, :].bitcast(F32),
                                            ALU.subtract).then_inc(cv_lo, 1)

            def taps(b, k, n):
                for ct in range(CT):
                    yc = y[:, ct, :].rearrange("p (a b) -> p a b", b=CW)
                    dve.wait_ge(tap, b * NTAP + (n * CT + ct - CT + 2))
                    nc.vector.scalar_tensor_tensor(
                        yc, gw[:, ct, :, bass.ds(k, CW)], vec[:, bass.ds(k + (V_CW + ct * TAPS), 1)], yc,
                        ALU.mult, ALU.add).then_inc(tap, 1)

            def first_tap(b):
                dve.wait_ge(gw_in, b * (16 * NCH) + 16 * NCH)
                for ct in range(CT):
                    wk = V_CW + ct * TAPS + HIST
                    nc.vector.tensor_scalar(y[:, ct, :].rearrange("p (a b) -> p a b", b=CW), gw[:, ct, :, HIST:HIST + CW],
                                            vec[:, wk:wk + 1], vec[:, V_CB + ct:V_CB + ct + 1], ALU.mult,
                                            ALU.add).then_inc(tap, 1)

            def tile_out(b, u, n, m, gain):
                dve.wait_ge(left, b * NU + (u + 3))
                dve.wait_ge(u_hi, b * (2 * KD) + (n + m + 1))
                nc.vector.scalar_tensor_tensor(ul[:, m, :], h[:, m, :], vec[:, gain + m:gain + m + 1],
                                               uh[:, m, :].bitcast(F32), ALU.mult, ALU.subtract).then_inc(u_lo, 1)
                if m:
                    dve.wait_ge(sq_out, b * (2 * KD) + (n + m + 1))
                    if m >= 2:
                        dve.wait_ge(sum_out, b * 14 + (n // KD * 7 + m - 1))
                    nc.vector.tensor_tensor(ssum[:, :], ssum[:, :], sq[:, :], ALU.add).then_inc(sum_out, 1)

            def norm(b, i):
                dve.wait_ge(n_sd, b * 2 + (i + 1))
                nc.vector.reciprocal(rstd[:, :], sd[:, :]).then_inc(n_r, 1)

            def step(b, u):
                kind, half, m = place(u)
                if kind == "ple":
                    if m == 0:
                        norm(b, 1)
                    dve.wait_ge(ring.used, b * NU + (u + 3))
                    dve.wait_ge(n_r, b * 2 + 2)
                    nc.vector.tensor_tensor(g[:, :], acc[:, m % 2, 0:N], rstd[:, :], ALU.mult).then_inc(left, 1)
                    dve.wait_ge(sig_out, b * T0 + (KF + m + 1))
                    nc.vector.tensor_tensor(up[:, :], acc_p[:, m % 2, 0:N], sig[:, :], ALU.mult).then_inc(e_out, 1)
                    dve.wait_ge(e_out, b * KD + (m + 1))
                    dve.wait_ge(stored[m % 2], b * (8 * KD) + 16 * (m // 2 + 1))
                    nc.vector.tensor_tensor(yo[:, m % 2, :], up[:, :], h[:, m, :], ALU.add).then_inc(y_out, 1)
                else:
                    dve.wait_ge(ring.used, b * NU + (u + 3))
                    if kind == "out":
                        dve.wait_ge(x_in[m], b * 16 + 16)
                    nc.vector.tensor_tensor(h[:, m, :], acc[:, u % 2, 0:N], h[:, m, :], ALU.add).then_inc(left, 1)
                    if kind == "out":
                        tile_out(b, u, 0, m, V_GFFN)
                    elif half:
                        tile_out(b, u, KD, m, V_GPLE)
                    else:
                        taps(b, 2 * HF + m, 1 + HF + m)
                if u == 4:
                    dve.wait_ge(p_hi, b + 1)
                    nc.vector.tensor_tensor(pl[:, :, :], p[:, :, :], ph[:, :, :].bitcast(F32), ALU.subtract).then_inc(p_lo, 1)
                if u == OU - 1:
                    norm(b, 0)
                    first_tap(b)
                if u == DU[1]:
                    dve.wait_ge(tap, b * NTAP + (NTAP + 1))
                    tail(b + 1, "sum")
                for at, stage in ((DU[1] + 2, "center"), (DU[1] + 4, "sum2"), (DU[1] + 6, "scale"),
                                  (E0 + 5, "swish"), (E0 + 6, "low")):
                    if u == at:
                        tail(b + 1, stage)

            def fstep(b, half, f):
                n, u = half * HF, GU[half]
                dve.wait_ge(n_r, b * 2 + 1)
                dve.wait_ge(ring.used, b * NU + f * 2 + (u + 3))
                nc.vector.tensor_tensor(g[:, :], acc[:, 0, 0:N], rstd[:, :], ALU.mult).then_inc(left, 1)
                dve.wait_ge(sig_out, b * T0 + f + (n + 1))
                dve.wait_ge(left, b * NU + f * 2 + (u + 3))
                nc.vector.tensor_tensor(g[:, :], g[:, :], sig[:, :], ALU.mult).then_inc(gs_out, 1)
                dve.wait_ge(ring.used, b * NU + f * 2 + (u + 4))
                nc.vector.tensor_tensor(up[:, :], acc[:, 1, 0:N], rstd[:, :], ALU.mult).then_inc(left, 1)
                dve.wait_ge(gs_out, b * KF + f + (n + 1))
                dve.wait_ge(left, b * NU + f * 2 + (u + 4))
                nc.vector.tensor_tensor(hid[:, :], g[:, :], up[:, :], ALU.mult).then_inc(hid_out, 1)
                dve.wait_ge(hid_out, b * KF + f + (n + 1))
                dve.wait_ge(hid_hi, b * KF + f + (n + 1))
                nc.vector.tensor_tensor(hl[:, bass.ds(f, 1), :], hid[:, :].unsqueeze(1),
                                        hh[:, bass.ds(f, 1), :].bitcast(F32), ALU.subtract).then_inc(hid_lo, 1)
                taps(b, f + n, f + (1, HF + KD + 1)[half])

            for stage in ("sum", "center", "sum2", "scale", "swish", "low"):
                tail(0, stage)
            with dve.Fori(0, NB) as b:
                phases(dve, b, step, fstep)

        @block.tensor
        def _(pe):
            pe.sem_inc(ring.used, 2)

            def w(q):
                return [lambda k: ring.hi[:, q, k, :], lambda k: ring.lo[:, q, k, :]]

            U = [lambda k: uh[:, k, :], lambda k: ul[:, k, :]]
            M = [lambda k: mh[:, k, :], lambda k: ml[:, k, :]]
            H = [lambda k: hh[:, k, :], lambda k: hl[:, k, :]]
            E = [lambda k: ph[:, k, :], lambda k: pl[:, k, :]]
            ALL = [(k, k) for k in range(KD)]

            def norm(b, i):
                pe.wait_ge(sum_out, b * 14 + 7 * (i + 1))
                nc.tensor.matmul(ps_n[:, 0:N], c["ones"][:, :], ssum[:, :], start=True, stop=True).then_inc(n_mm, 1)

            def first_use(b, i, out, wq):
                pe.wait_ge(u_lo, b * (2 * KD) + (KD * (i + 1) - 2))
                passes(nc, out, wq, U, ALL[:KD - 2], True, False)
                for k in range(KD - 2, KD):
                    pe.wait_ge(u_lo, b * (2 * KD) + (KD * i + k + 1))
                    mm = passes(nc, out, wq, U, [(k, k)], False, k == KD - 1)
                return mm

            def tail(n, i):
                pe.wait_ge(cv_sum, n * 2 + (i + 1))
                nc.tensor.matmul(ps_c[:, 0:N], c["ones"][:, :], csum[:, :], start=True, stop=True).then_inc(cv_mm, 1)

            def step(b, u):
                kind, half, m = place(u)
                q = u % 2
                out = acc[:, q, 0:N]
                if u == 0:
                    pe.wait_ge(mix_in, b * 32 + 32)
                pe.wait_ge(ring.lo_done, b * NU + (u + 1))
                pe.wait_ge(left, b * NU + (u + 1))
                if u == 0:
                    passes(nc, out, w(q), M, ALL[:CT], True, False)
                    pe.wait_ge(cv_lo, b + 1)
                    mm = passes(nc, out, w(q), M, ALL[CT:], False, True)
                elif kind == "out":
                    mm = passes(nc, out, w(q), M, ALL, True, True)
                elif kind == "down":
                    if m == 0:
                        pe.wait_ge(hid_lo, b * KF + (HF * (half + 1) - 1))
                        passes(nc, out, w(q), H, [(k, k) for k in range(HF - 1)], True, False)
                        pe.wait_ge(hid_lo, b * KF + HF * (half + 1))
                        mm = passes(nc, out, w(q), H, [(HF - 1, HF - 1)], False, True)
                    else:
                        mm = passes(nc, out, w(q), H, [(k, k) for k in range(HF)], True, True)
                else:
                    if m == 0:
                        pe.wait_ge(p_lo, b + 1)
                    if m >= 2:
                        pe.wait_ge(e_out, b * KD + (m - 1))
                    passes(nc, acc_p[:, q, 0:N], w(q), E, [(KD + k, k) for k in range(KP)], True, True)
                    mm = first_use(b, 1, out, w(q)) if m == 0 else passes(nc, out, w(q), U, ALL, True, True)
                mm.then_inc(ring.used, 1)
                if u == E0:
                    norm(b, 1)
                if u == DU[1] + 1:
                    tail(b + 1, 0)
                if u == DU[1] + 5:
                    tail(b + 1, 1)

            def fstep(b, half, f):
                for j in range(2):
                    pe.wait_ge(ring.lo_done, b * NU + f * 2 + (GU[half] + j + 1))
                    pe.wait_ge(left, b * NU + f * 2 + (GU[half] + j + 1))
                    if isinstance(f, int) and half == j == 0:
                        mm = first_use(b, 0, acc[:, j, 0:N], w(j))
                    else:
                        mm = passes(nc, acc[:, j, 0:N], w(j), U, ALL, True, True)
                    mm.then_inc(ring.used, 1)
                    if isinstance(f, int) and half == j == 0:
                        norm(b, 0)

            tail(0, 0)
            tail(0, 1)
            with pe.Fori(0, NB) as b:
                phases(pe, b, step, fstep, first=1)


def kernel(x_prompt, x_sample, p_prompt, p_sample, cache_k, cache_v, state_conv, g_mix, w_in, q_gain, k_gain,
           rel_bias, conv_w, conv_b, conv_ln_g, conv_ln_b, w_out, g_ffn, w_gate_up, w_down, g_ple, w_ple_gate,
           w_ple_proj):
    import numpy as np
    import concourse.bacc as bacc
    from concourse.bass_utils import run_bass_kernel_spmd

    a = np.asarray

    def tiles(w):
        k, m = w.shape
        return a(w).reshape(k // P, P, m // P, P).transpose(2, 1, 0, 3).reshape(m, k)

    def blocks(v):
        f = v.shape[1]
        return v.reshape(NB, N, f // P, P).transpose(0, 3, 2, 1).reshape(NB * P, f // P * N)

    def paired(first, second):
        return np.stack([first.reshape(-1, P, first.shape[1]), second.reshape(-1, P, second.shape[1])],
                        1).reshape(-1, first.shape[1])

    def columns(v):
        return a(v).reshape(-1, P).T

    wi = tiles(w_in[0])
    part = [wi[AW * i:AW * (i + 1)] for i in range(5)]
    gu = tiles(w_gate_up[0])
    ins = {
        "x": blocks(np.concatenate([a(x_prompt)[0], a(x_sample)[0]])),
        "p": blocks(np.concatenate([a(p_prompt)[0, 0], a(p_sample)[0, 0]])),
        "w_in": np.concatenate([paired(part[0], part[1]), part[2], paired(part[3], part[4])]),
        "w_out": tiles(w_out[0]),
        "w_gu": paired(gu[:FF], gu[FF:]),
        "w_down": tiles(w_down[0]),
        "w_ple": np.concatenate([tiles(w_ple_gate[0]), tiles(w_ple_proj[0])], 1),
        "ck_rows": a(cache_k)[0, 0, DEC:].reshape(PAST - DEC, AW),
        "cv_rows": a(cache_v)[0, 0, DEC:].reshape(PAST - DEC, AW),
        "ckT": a(cache_k)[0, 0].reshape(PAST, CT, P).transpose(2, 1, 0).reshape(P, CT * PAST),
        "cvT": a(cache_v)[0, 0].reshape(PAST // P, P, AW).transpose(1, 0, 2).reshape(P, PAST // P * AW),
        "state": a(state_conv)[0, 0].T,
        "vec": np.concatenate([
            columns(g_mix), columns(g_ffn), columns(g_ple),
            np.tile(a(q_gain)[0], 2)[:, None], np.tile(a(k_gain)[0], 2)[:, None],
            columns(conv_b), columns(conv_ln_g), columns(conv_ln_b),
            a(conv_w)[0].reshape(TAPS, CT, P).transpose(2, 1, 0).reshape(P, CT * TAPS)], 1),
        "ext": np.tile(np.concatenate([np.repeat(a(rel_bias)[0, :, 256:257], PAST, 1),
                                       a(rel_bias)[0, :, 255:0:-1]], 1), (1, P)),
    }
    outs = {"o_y": (NB * P, KD * N), "o_k": (AW, NT), "o_v": (NT, AW), "o_g": (AW, GPAD),
            "o_ck": (PAST - DEC, AW), "o_cv": (PAST - DEC, AW)}
    nc = bacc.Bacc("TRN2", target_bir_lowering=False, num_devices=1)
    t, arrays = {}, {}
    for name, v in ins.items():
        arrays["in_" + name] = np.ascontiguousarray(v)
        t[name] = nc.dram_tensor("in_" + name, v.shape, F32, kind="ExternalInput").ap()
    for name, shape in outs.items():
        t[name] = nc.dram_tensor(name, shape, F32, kind="ExternalOutput").ap()
    build(nc, t)
    r = run_bass_kernel_spmd(nc, [arrays], core_ids=[0]).results[0]
    y = r["o_y"].reshape(NB, P, KD, N).transpose(0, 3, 2, 1).reshape(NT, D)
    k, v, g = r["o_k"].T, r["o_v"], r["o_g"].T
    heads = (1, 1, PAST, HEADS, HD)
    return (y[None, :SEQ], y[None, SEQ:],
            k[SEQ - PAST:SEQ].reshape(heads), v[SEQ - PAST:SEQ].reshape(heads), g[None, None, SEQ:SEQ + HIST],
            np.concatenate([r["o_ck"], k[SEQ:]]).reshape(heads), np.concatenate([r["o_cv"], v[SEQ:]]).reshape(heads),
            g[None, None, GPAD - HIST:])
```

```python
from contextlib import ExitStack

import concourse.bass as bass
from concourse import mybir

F32 = mybir.dt.float32
F32R = mybir.dt.float32r
ACT = mybir.ActivationFunctionType
ALU = mybir.AluOpType
AX = mybir.AxisListType

P = 128
D = 1024
SEQ, DEC = 2048, 32
NT = SEQ + DEC
NB = 5
N = NT // NB
KD = D // P
AW = 512
CT = AW // P
HEADS, HD = 8, 64
CHUNK, PAST = 64, 512
TAPS, HIST = 31, 30
FF = 2816
KF = FF // P
PLE = 256
KP = PLE // P
EPS = 1e-6
NEG = -1e30
TG = 104
NG = N // TG

V_GMIX, V_GFFN, V_GPLE, V_GQ, V_GK, V_CB, V_LG, V_LB, V_CW = 0, 8, 16, 24, 25, 26, 30, 34, 38
NVEC = V_CW + CT * TAPS
GPAD = HIST + SEQ + HIST + DEC
CW = 32
NCH = N // CW
BW = 5 * P
EXT = 767


def build(nc, t):
    with ExitStack() as ctx:
        def sb(name, shape, dt=F32, until=None):
            return (until or ctx).enter_context(nc.sbuf_tensor(name, shape, dt))

        def dram(name, shape, dt):
            return nc.dram_tensor(name, shape, dt, kind="Internal").ap()

        c = {
            "vec": sb("vec", [P, NVEC]), "ones": sb("ones", [P, P]), "ident": sb("ident", [P, P]),
            "eps": sb("eps", [P, 1]), "gq8": sb("gq8", [P, 1]),
            "gw": sb("gw", [P, CT, NCH, HIST + CW]),
            "y": sb("y", [P, CT, N]),
        }
        s = {
            "qh": dram("qh_d", (AW, NT), F32), "ql": dram("ql_d", (AW, NT), F32),
            "kh": dram("kh_d", (AW, NT), F32), "kl": dram("kl_d", (AW, NT), F32),
            "vh": dram("vh_d", (NT, AW), F32), "vl": dram("vl_d", (NT, AW), F32),
            "mh": dram("mh_d", (AW, NT), F32), "ml": dram("ml_d", (AW, NT), F32),
            "ch": dram("ch_d", (P, 2 * CT * PAST), F32), "cl": dram("cl_d", (P, 2 * CT * PAST), F32),
        }
        with ExitStack() as middle:
            c["bias"] = sb("bias", [P, HEADS, BW], until=middle)
            c["bias_in"] = middle.enter_context(nc.semaphore("bias_in"))
            with ExitStack() as early:
                c["sel"], c["selT"] = sb("sel", [P, 8, 16], until=early), sb("selT", [16, 8, P], until=early)
                constants(nc, t, c, s)
                project(nc, t, c, s)
            attend(nc, t, c, s)
        finish(nc, t, c, s)


def gw_load(sp, t, gw, w, ch, arrived):
    rows = t["o_g"].rearrange("(c p) n -> p c n", p=P)
    at = w * N + ch * CW if ch < NCH - 1 else w * N + ((w >> 2) * HIST + ch * CW)
    sp.dma_start(gw[:, :, ch, :], rows[:, :, bass.ds(at, HIST + CW)]).then_inc(arrived, 16)


def constants(nc, t, c, s):
    with ExitStack() as ctx:
        vec_in, cleared, filled, shaped = (
            ctx.enter_context(nc.semaphore(n)) for n in ("vec_in", "cleared", "filled", "shaped"))
        block = ctx.enter_context(nc.Block())

        @block.sync
        def _(sp):
            sp.dma_start(c["vec"][:, :], t["vec"]).then_inc(vec_in, 16)

        @block.vector
        def _(dve):
            nc.vector.memset(c["ones"][:, :], 1.0)
            nc.vector.memset(c["eps"][:, :], EPS)
            nc.vector.memset(c["sel"][:, :, :], 0.0).then_inc(cleared, 1)
            dve.wait_ge(cleared, 1)
            for u in range(8):
                for half in range(2):
                    nc.vector.memset(c["sel"][HD * half:HD * half + HD, u, 2 * u + half:2 * u + half + 1], 1.0)
            dve.wait_ge(vec_in, 16)
            nc.vector.tensor_scalar(c["gq8"][:, :], c["vec"][:, V_GQ:V_GQ + 1], HD ** -0.5, None, ALU.mult)

        @block.gpsimd
        def _(pool):
            nc.gpsimd.memset(c["ident"][:, :], 0.0).then_inc(filled, 1)
            nc.gpsimd.memset(c["selT"][:, :, :], 1.0).then_inc(filled, 1)
            pool.wait_ge(filled, 2)
            nc.gpsimd.affine_select(out=c["ident"][:, :], in_=c["ident"][:, :], compare_op=ALU.not_equal,
                                    fill=1.0, base=0, pattern=[[-1, P]], channel_multiplier=1).then_inc(shaped, 1)
            pool.wait_ge(shaped, 1)
            nc.gpsimd.affine_select(out=c["selT"][:, :, :], in_=c["selT"][:, :, :], compare_op=ALU.is_ge,
                                    fill=0.0, base=0, pattern=[[P, 8], [1, P]],
                                    channel_multiplier=-HD).then_inc(shaped, 1)
            pool.wait_ge(shaped, 2)
            nc.gpsimd.affine_select(out=c["selT"][:, :, :], in_=c["selT"][:, :, :], compare_op=ALU.is_ge,
                                    fill=0.0, base=HD - 1, pattern=[[-P, 8], [-1, P]], channel_multiplier=HD)


def passes(nc, out, w, u, kts, first, last):
    mm = None
    for n, (kw, ku) in enumerate(kts):
        for j, (wp, up) in enumerate(((0, 0), (0, 1), (1, 0))):
            mm = nc.tensor.matmul(out, w[wp](kw), u[up](ku), start=first and n == 0 and j == 0,
                                  stop=last and n == len(kts) - 1 and j == 2)
    return mm


class WeightRing:

    def __init__(self, nc, ctx, tag, kmax):
        self.nc = nc
        self.raw = ctx.enter_context(nc.sbuf_tensor(f"{tag}w_raw", [P, 2, kmax, P], F32))
        self.hi = ctx.enter_context(nc.sbuf_tensor(f"{tag}w_hi", [P, 2, kmax, P], F32R))
        self.lo = ctx.enter_context(nc.sbuf_tensor(f"{tag}w_lo", [P, 2, kmax, P], F32R))
        self.loaded = [ctx.enter_context(nc.semaphore(f"{tag}w_loaded{i}")) for i in range(2)]
        self.hi_done = ctx.enter_context(nc.semaphore(f"{tag}w_hi_done"))
        self.lo_done = ctx.enter_context(nc.semaphore(f"{tag}w_lo_done"))
        self.used = ctx.enter_context(nc.semaphore(f"{tag}w_used"))

    def load(self, sp, src, slot, kts):
        sp.dma_start(self.raw[:, slot, 0:kts, :].rearrange("p k c -> p (k c)"), src).then_inc(self.loaded[slot], 16)

    def high(self, act, v, pair, slot, kts):
        act.wait_ge(self.loaded[slot], pair * 16 + 16)
        act.wait_ge(self.used, v + 1)
        self.nc.scalar.activation(self.hi[:, slot, 0:kts, :], self.raw[:, slot, 0:kts, :],
                                  ACT.Copy).then_inc(self.hi_done, 1)

    def low(self, pool, v, slot, kts):
        pool.wait_ge(self.hi_done, v + 1)
        self.nc.gpsimd.tensor_tensor(self.lo[:, slot, 0:kts, :], self.raw[:, slot, 0:kts, :],
                                     self.hi[:, slot, 0:kts, :].bitcast(F32), ALU.subtract).then_inc(self.lo_done, 1)


def wrapped(b):
    return (b + 1) % NB


def project(nc, t, c, s):
    NU = 20
    QK, VU, GU = 8, 8, 12
    FIN = 10
    with ExitStack() as ctx:
        def sb(name, shape, dt=F32):
            return ctx.enter_context(nc.sbuf_tensor("a_" + name, shape, dt))

        def ps(name, shape):
            return ctx.enter_context(nc.psum_tensor("a_" + name, shape, F32))

        def sem(name):
            return ctx.enter_context(nc.semaphore("a_" + name))

        ring = WeightRing(nc, ctx, "a_", KD)
        x = sb("x", [P, KD, N])
        xsq = sb("xsq", [P, KD, N])
        ssum = sb("ssum", [P, N])
        sd, rstd = sb("sd", [P, N]), sb("rstd", [P, N])
        uh, ul = sb("uh", [P, KD, N], F32R), sb("ul", [P, KD, N], F32R)
        zqk = sb("zqk", [P, QK, N])
        zsq = sb("zsq", [P, 2, N])
        zsh, zsl = sb("zsh", [P, 2, N], F32R), sb("zsl", [P, 2, N], F32R)
        sd16, r16 = sb("sd16", [16, N]), sb("r16", [16, N])
        r16h, r16l = sb("r16h", [16, N], F32R), sb("r16l", [16, N], F32R)
        sel, selT = sb("sel", [P, 8, 16], F32R), sb("selT", [16, 8, P], F32R)
        zn = sb("zn", [P, 2, N])
        znh, znl = sb("znh", [P, 2, N], F32R), sb("znl", [P, 2, N], F32R)
        z = sb("z", [P, 2, N])
        vt = sb("vt", [TG, NG, AW])
        vh, vl = sb("vh", [TG, NG, AW], F32R), sb("vl", [TG, NG, AW], F32R)
        sig = sb("sig", [P, N])
        glu = sb("glu", [P, 2, N])
        CQ = CT * PAST // 2
        room = c["gw"][:, :, :, :].rearrange("p c a b -> p (c a b)")
        cr, crh, crl = room[:, 0:CQ], room[:, CQ:2 * CQ].bitcast(F32R), room[:, 2 * CQ:3 * CQ].bitcast(F32R)
        zero = sb("zero", [P, CT, HIST])

        acc = ps("acc", [P, 2, 512])
        ps_rs = ps("ps_rs", [P, 512])
        ps_ss = ps("ps_ss", [P, 512])
        ps_bc = ps("ps_bc", [P, 2, 512])
        ps_vt = ps("ps_vt", [P, 2, 512])

        u_read = sem("u_read")
        x_in, x_hi, x_lo, x_sq, x_sum = sem("x_in"), sem("x_hi"), sem("x_lo"), sem("x_sq"), sem("x_sum")
        rs_mm, rs_sd, rs = sem("rs_mm"), sem("rs_sd"), sem("rs")
        z_out, z_sq = sem("z_out"), sem("z_sq")
        ss_mm, ss_sd, ss_r = sem("ss_mm"), sem("ss_sd"), sem("ss_r")
        bc_mm, zn_out, znh_out, znl_out = sem("bc_mm"), sem("zn_out"), sem("znh_out"), sem("znl_out")
        v_tr, v_out, vh_out, vl_out = sem("v_tr"), sem("v_out"), sem("vh_out"), sem("vl_out")
        sig_out, glu_out = sem("sig_out"), sem("glu_out")
        st_qk = [sem("st_q"), sem("st_k")]
        st_v = sem("st_v")
        st_glu = [sem("st_g0"), sem("st_g1")]
        x_first = [sem(f"x_first{k}") for k in range(KD)]
        x_add = sem("x_add")
        sel_in, zs_hi, zs_lo, r_hi, r_lo = sem("sel_in"), sem("zs_hi"), sem("zs_lo"), sem("r_hi"), sem("r_lo")
        cr_in, cr_hi, cr_lo, st_cr = sem("cr_in"), sem("cr_hi"), sem("cr_lo"), sem("st_cr")
        zeroed, passed = sem("zeroed"), sem("passed")
        vec = c["vec"]

        def weights(sp, i):
            m = i % NU
            ring.load(sp, t["w_in"][m * P:(m + 1) * P, :], i % 2, KD)

        block = ctx.enter_context(nc.Block())

        @block.sync
        def _(sp):
            for k in range(KD):
                sp.dma_start(x[:, k, :], t["x"][0:P, k * N:(k + 1) * N]).then_inc(x_first[k], 16)
                if k == 0:
                    weights(sp, 0)
            weights(sp, 1)
            for i in range(2, 4):
                sp.wait_ge(ring.lo_done, i - 1)
                weights(sp, i)
            ext = t["ext"]
            sp.dma_start(c["bias"][:, :, :], bass.AP(ext.tensor, P - 1, [[EXT - 1, P], [P * EXT, HEADS], [1, BW]])).then_inc(c["bias_in"], 16)
            sp.dma_start(t["o_ck"], t["ck_rows"]).then_inc(passed, 16)
            sp.dma_start(t["o_cv"], t["cv_rows"]).then_inc(passed, 16)
            sp.dma_start(t["o_g"][:, HIST + SEQ:HIST + SEQ + HIST], t["state"]).then_inc(passed, 16)
            sp.wait_ge(zeroed, 1)
            sp.dma_start(t["o_g"].rearrange("(c p) n -> p c n", p=P)[:, :, 0:HIST], zero[:, :, :]).then_inc(passed, 16)
            sp.sem_inc(st_v, 48)
            sp.sem_inc(st_cr, 32)
            for q in range(2):
                sp.sem_inc(st_qk[q], (32, 48)[q])
                sp.sem_inc(st_glu[q], 32)
            with sp.Fori(0, NB) as b:
                for i in range(NU):
                    if i == 2:
                        sp.wait_ge(x_hi, b * KD + KD)
                        sp.wait_ge(x_lo, b * KD + KD)
                        sp.dma_start(x[:, :, :].rearrange("p k n -> p (k n)"),
                                     t["x"][bass.ds(wrapped(b) * P, P), :]).then_inc(x_in, 16)
                    sp.wait_ge(ring.lo_done, b * NU + (i + 3))
                    weights(sp, i + 4)
                    if i == 4:
                        sp.wait_ge(cr_lo, b + 1)
                        sp.dma_start(cr, t["cache"][:, bass.ds((b % 4) * CQ, CQ)]).then_inc(cr_in, 16)
                    if i == 9:
                        sp.wait_ge(cr_lo, b + 2)
                        for dst, src in ((s["ch"], crh), (s["cl"], crl)):
                            sp.dma_start(dst[:, bass.ds((b % 4) * CQ, CQ)], src.bitcast(F32)).then_inc(st_cr, 16)
                    if FIN <= i < FIN + QK:
                        j = i - FIN
                        m, q = j // 2, j % 2
                        rows = slice(m * P, (m + 1) * P)
                        sp.wait_ge(znl_out, b * QK + (j + 1))
                        sp.dma_start(s["qk"[q] + "h"][rows, bass.ds(b * N, N)], znh[:, q, :].bitcast(F32)).then_inc(st_qk[q], 16)
                        sp.dma_start(s["qk"[q] + "l"][rows, bass.ds(b * N, N)], znl[:, q, :].bitcast(F32)).then_inc(st_qk[q], 16)
                        if q:
                            sp.dma_start(t["o_k"][rows, bass.ds(b * N, N)], zn[:, q, :]).then_inc(st_qk[q], 16)
                    if i == VU + CT:
                        sp.wait_ge(vl_out, b * CT + CT)
                        for dst, src in ((t["o_v"], vt[:, :, :]), (s["vh"], vh[:, :, :].bitcast(F32)),
                                         (s["vl"], vl[:, :, :].bitcast(F32))):
                            sp.dma_start(dst[bass.ds(b * N, N), :].rearrange("(g p) d -> p g d", p=TG),
                                         src).then_inc(st_v, 16)
                    if i > GU and i % 2:
                        m = (i - GU) // 2
                        sp.wait_ge(glu_out, b * CT + (m + 2))
                        rows, cut = slice(m * P, (m + 1) * P), N - DEC
                        sp.dma_start(t["o_g"][rows, bass.ds(b * N + HIST, cut)],
                                     glu[:, m % 2, 0:cut]).then_inc(st_glu[m % 2], 16)
                        sp.dma_start(t["o_g"][rows, bass.ds(b * N + (b >> 2) * HIST + (HIST + cut), DEC)],
                                     glu[:, m % 2, cut:N]).then_inc(st_glu[m % 2], 16)
            for q in range(2):
                sp.wait_ge(ring.loaded[q], 16 * (NU * NB // 2 + 2))
                sp.wait_ge(st_qk[q], (32, 48)[q] * (1 + NB * CT))
                sp.wait_ge(st_glu[q], 32 * (1 + 2 * NB))
            sp.wait_ge(x_in, 16 * NB)
            sp.wait_ge(cr_in, 16 * NB)
            sp.wait_ge(st_cr, 32 * (NB + 1))
            sp.wait_ge(passed, 16 * 4)
            sp.wait_ge(st_v, 48 * (NB + 1))

        @block.scalar
        def _(act):
            def square_x(n_in):
                act.wait_ge(x_in, n_in)
                nc.scalar.activation(xsq[:, :, :], x[:, :, :], ACT.Square).then_inc(x_sq, 1)

            def split_x(k):
                nc.scalar.activation(uh[:, k, :], x[:, k, :], ACT.Identity,
                                     scale=vec[:, V_GMIX + k:V_GMIX + k + 1]).then_inc(x_hi, 1)

            def sqrt_rs(n):
                act.wait_ge(rs_mm, n)
                nc.scalar.activation(sd[:, :], ps_rs[:, 0:N], ACT.Sqrt, scale=1.0 / D,
                                     bias=c["eps"][:, :]).then_inc(rs_sd, 1)

            nc.scalar.activation(sel[:, :, :], c["sel"][:, :, :], ACT.Copy).then_inc(sel_in, 1)
            nc.scalar.activation(selT[:, :, :], c["selT"][:, :, :], ACT.Copy).then_inc(sel_in, 1)
            ring.high(act, 0, 0, 0, KD)
            for k in range(KD):
                act.wait_ge(x_first[k], 16)
                split_x(k)
                nc.scalar.activation(xsq[:, k, :], x[:, k, :], ACT.Square).then_inc(x_sq, 1)
            ring.high(act, 1, 0, 1, KD)
            sqrt_rs(1)
            with act.Fori(0, NB) as b:
                for i in range(NU):
                    if i == NU - 1:
                        act.wait_ge(x_in, b * 16 + 16)
                        for k in range(KD):
                            if k < KD - 1:
                                act.wait_ge(u_read, b * (KD - 1) + (k + 1))
                            else:
                                act.wait_ge(ring.used, b * NU + (i + 3))
                            split_x(k)
                    ring.high(act, b * NU + (i + 2), b * (NU // 2) + (i + 2) // 2, i % 2, KD)
                    if i == 6:
                        act.wait_ge(cr_in, b * 16 + 16)
                        act.wait_ge(st_cr, b * 32 + 32)
                        nc.scalar.activation(crh, cr, ACT.Copy).then_inc(cr_hi, 1)
                    if i == 4:
                        square_x(b * 16 + 16)
                    if i < QK:
                        act.wait_ge(z_out, b * NU + (i + 3))
                        if i >= 2:
                            act.wait_ge(ss_mm, b * QK + (i - 1))
                        nc.scalar.activation(zsq[:, i % 2, :], zqk[:, i, :], ACT.Square).then_inc(z_sq, 1)
                        act.wait_ge(z_sq, b * QK + (i + 1))
                        nc.scalar.activation(zsh[:, i % 2, :], zsq[:, i % 2, :], ACT.Copy).then_inc(zs_hi, 1)
                    if i == QK:
                        act.wait_ge(ss_mm, b * QK + QK)
                        nc.scalar.activation(sd16[:, :], ps_ss[0:16, 0:N], ACT.Sqrt, scale=1.0 / HD,
                                             bias=c["eps"][0:16, :]).then_inc(ss_sd, 1)
                        sqrt_rs(b + 2)
                    if i == QK + 1:
                        act.wait_ge(ss_r, b + 1)
                        nc.scalar.activation(r16h[:, :], r16[:, :], ACT.Copy).then_inc(r_hi, 1)
                    if VU < i <= VU + CT:
                        m = i - 1 - VU
                        act.wait_ge(v_tr, b * CT + (m + 1))
                        act.wait_ge(st_v, b * 48 + 48)
                        nc.scalar.activation(vh[:, :, m * P:(m + 1) * P],
                                             ps_vt[0:TG, m % 2, :].rearrange("p (g d) -> p g d", g=NG),
                                             ACT.Copy).then_inc(vh_out, 1)
                    if FIN <= i < FIN + QK:
                        j = i - FIN
                        q = j % 2
                        act.wait_ge(zn_out, b * QK + (j + 1))
                        nc.scalar.activation(znh[:, q, :], zn[:, q, :], ACT.Copy).then_inc(znh_out, 1)
                    if i > GU and i % 2:
                        m = (i - GU) // 2
                        act.wait_ge(z_out, b * NU + (i + 3))
                        nc.scalar.activation(sig[:, :], z[:, 1, :], ACT.Sigmoid).then_inc(sig_out, 1)

        @block.gpsimd
        def _(pool):
            nc.gpsimd.memset(zero[:, :, :], 0.0).then_inc(zeroed, 1)
            ring.low(pool, 0, 0, KD)
            ring.low(pool, 1, 1, KD)
            with pool.Fori(0, NB) as b:
                for i in range(NU):
                    ring.low(pool, b * NU + (i + 2), i % 2, KD)

        @block.vector
        def _(dve):
            def sum_x(n):
                dve.wait_ge(x_sq, n)
                nc.vector.tensor_reduce(out=ssum[:, :], in_=xsq[:, :, :].rearrange("p k n -> p n k"),
                                        axis=AX.X, op=ALU.add).then_inc(x_sum, 1)

            def split_x(n, k):
                dve.wait_ge(x_hi, n + (k + 1))
                nc.vector.scalar_tensor_tensor(ul[:, k, :], x[:, k, :], vec[:, V_GMIX + k:V_GMIX + k + 1],
                                               uh[:, k, :].bitcast(F32), ALU.mult, ALU.subtract).then_inc(x_lo, 1)

            for k in range(KD):
                split_x(0, k)
                dve.wait_ge(x_sq, k + 1)
                if k == 1:
                    nc.vector.tensor_tensor(ssum[:, :], xsq[:, 0, :], xsq[:, 1, :], ALU.add).then_inc(x_add, 1)
                if k > 1:
                    dve.wait_ge(x_add, k - 1)
                    nc.vector.tensor_tensor(ssum[:, :], ssum[:, :], xsq[:, k, :],
                                            ALU.add).then_inc(x_sum if k == KD - 1 else x_add, 1)
            dve.sem_inc(cr_lo, 1)
            dve.sem_inc(z_out, 2)
            dve.sem_inc(glu_out, 1)
            with dve.Fori(0, NB) as b:
                for i in range(NU):
                    if i == NU - 1:
                        for k in range(KD):
                            split_x(b * KD + KD, k)
                    if i == 0:
                        dve.wait_ge(rs_sd, b + 1)
                        dve.wait_ge(z_out, b * NU + 2)
                        nc.vector.reciprocal(rstd[:, :], sd[:, :]).then_inc(rs, 1)
                        dve.wait_ge(rs, b + 1)
                    if i == 5:
                        sum_x(b + (KD + 1))
                    dve.wait_ge(ring.used, b * NU + (i + 3))
                    if i == VU or (i >= GU and i % 2 == 0):
                        dve.wait_ge(glu_out, b * CT + (max(i - GU, 0) // 2 + 1))
                    dst = zqk[:, i, :] if i < QK else z[:, i % 2, :]
                    nc.vector.tensor_tensor(dst, acc[:, i % 2, 0:N], rstd[:, :], ALU.mult).then_inc(z_out, 1)
                    if i < QK:
                        dve.wait_ge(zs_hi, b * QK + (i + 1))
                        nc.vector.tensor_tensor(zsl[:, i % 2, :], zsq[:, i % 2, :], zsh[:, i % 2, :].bitcast(F32),
                                                ALU.subtract).then_inc(zs_lo, 1)
                    if i == QK + 1:
                        dve.wait_ge(r_hi, b + 1)
                        nc.vector.tensor_tensor(r16l[:, :], r16[:, :], r16h[:, :].bitcast(F32), ALU.subtract).then_inc(r_lo, 1)
                    if i == 7:
                        dve.wait_ge(cr_hi, b + 1)
                        nc.vector.tensor_tensor(crl, cr, crh.bitcast(F32), ALU.subtract).then_inc(cr_lo, 1)
                    if i == QK:
                        dve.wait_ge(ss_sd, b + 1)
                        nc.vector.reciprocal(r16[:, :], sd16[:, :]).then_inc(ss_r, 1)
                    if VU < i <= VU + CT:
                        m = i - 1 - VU
                        cols = slice(m * P, (m + 1) * P)
                        tr = ps_vt[0:TG, m % 2, :].rearrange("p (g d) -> p g d", g=NG)
                        dve.wait_ge(vh_out, b * CT + (m + 1))
                        nc.vector.tensor_copy(vt[:, :, cols], tr).then_inc(v_out, 1)
                        nc.vector.tensor_tensor(vl[:, :, cols], tr, vh[:, :, cols].bitcast(F32),
                                                ALU.subtract).then_inc(vl_out, 1)
                    if FIN <= i < FIN + QK:
                        j = i - FIN
                        q = j % 2
                        gain = vec[:, V_GK:V_GK + 1] if q else c["gq8"][:, :]
                        dve.wait_ge(bc_mm, b * QK + (j + 1))
                        dve.wait_ge(st_qk[q], (b * CT + (j // 2 + 1)) * (32, 48)[q])
                        nc.vector.scalar_tensor_tensor(zn[:, q, :], zqk[:, j, :], gain, ps_bc[:, q, 0:N],
                                                       ALU.mult, ALU.mult).then_inc(zn_out, 1)
                        dve.wait_ge(zn_out, b * QK + (j + 1))
                        dve.wait_ge(znh_out, b * QK + (j + 1))
                        nc.vector.tensor_tensor(znl[:, q, :], zn[:, q, :], znh[:, q, :].bitcast(F32),
                                                ALU.subtract).then_inc(znl_out, 1)
                    if i > GU and i % 2:
                        m = (i - GU) // 2
                        dve.wait_ge(sig_out, b * CT + (m + 1))
                        dve.wait_ge(z_out, b * NU + (i + 3))
                        dve.wait_ge(st_glu[m % 2], b * 64 + 32 * (m // 2 + 1))
                        nc.vector.tensor_tensor(glu[:, m % 2, :], z[:, 0, :], sig[:, :],
                                                ALU.mult).then_inc(glu_out, 1)

        @block.tensor
        def _(pe):
            pe.sem_inc(ring.used, 2)

            def sum_x(n):
                pe.wait_ge(x_sum, n)
                nc.tensor.matmul(ps_rs[:, 0:N], c["ones"][:, :], ssum[:, :], start=True, stop=True).then_inc(rs_mm, 1)

            sum_x(1)
            with pe.Fori(0, NB) as b:
                for i in range(NU):
                    pe.wait_ge(ring.lo_done, b * NU + (i + 1))
                    pe.wait_ge(z_out, b * NU + (i + 1))
                    w = [lambda k: ring.hi[:, i % 2, k, :], lambda k: ring.lo[:, i % 2, k, :]]
                    u = [lambda k: uh[:, k, :], lambda k: ul[:, k, :]]
                    if i == 0:
                        for k in range(KD):
                            pe.wait_ge(x_lo, b * KD + (k + 1))
                            mm = passes(nc, acc[:, 0, 0:N], w, u, [(k, k)], k == 0, k == KD - 1)
                    elif i == NU - 1:
                        for k in range(KD):
                            mm = passes(nc, acc[:, i % 2, 0:N], w, u, [(k, k)], k == 0, k == KD - 1)
                            if k < KD - 1:
                                mm.then_inc(u_read, 1)
                    else:
                        mm = passes(nc, acc[:, i % 2, 0:N], w, u, [(k, k) for k in range(KD)], True, True)
                    mm.then_inc(ring.used, 1)
                    if i == QK:
                        sum_x(b + 2)
                    if 1 <= i <= QK:
                        j = i - 1
                        pe.wait_ge(sel_in, 2)
                        pe.wait_ge(zs_lo, b * QK + (j + 1))
                        nc.tensor.matmul(ps_ss[0:16, 0:N], sel[:, j, :], zsh[:, j % 2, :], start=j == 0, stop=False)
                        nc.tensor.matmul(ps_ss[0:16, 0:N], sel[:, j, :], zsl[:, j % 2, :], start=False,
                                         stop=j == QK - 1).then_inc(ss_mm, 1)
                    if VU < i <= VU + CT:
                        m = i - 1 - VU
                        pe.wait_ge(z_out, b * NU + (i + 2))
                        if m >= 2:
                            pe.wait_ge(vl_out, b * CT + (m - 1))
                        for g in range(NG):
                            tr = nc.tensor.transpose(ps_vt[0:TG, m % 2, g * P:(g + 1) * P],
                                                     z[:, (i - 1) % 2, g * TG:(g + 1) * TG], c["ident"][:, :])
                        tr.then_inc(v_tr, 1)
                    if FIN <= i < FIN + QK:
                        j = i - FIN
                        pe.wait_ge(r_lo, b + 1)
                        if j >= 2:
                            pe.wait_ge(zn_out, b * QK + (j - 1))
                        nc.tensor.matmul(ps_bc[:, j % 2, 0:N], selT[:, j, :], r16h[:, :], start=True, stop=False)
                        nc.tensor.matmul(ps_bc[:, j % 2, 0:N], selT[:, j, :], r16l[:, :], start=False,
                                         stop=True).then_inc(bc_mm, 1)


def attend(nc, t, c, s):
    PQ, GT, WIN, PW = P, 6, 6 * P, BW
    UG = 2 * HEADS
    HP = HEADS // 2
    with ExitStack() as ctx:
        def sb(name, shape, dt=F32):
            return ctx.enter_context(nc.sbuf_tensor("b_" + name, shape, dt))

        def ps(name, shape):
            return ctx.enter_context(nc.psum_tensor("b_" + name, shape, F32))

        def sem(name):
            return ctx.enter_context(nc.semaphore("b_" + name))

        bias, bias_in = c["bias"], c["bias_in"]
        qh, ql = (sb(n, [P, HP, 2 * PQ], F32R) for n in ("qh", "ql"))
        kh, kl = (sb(n, [P, 2, HP, WIN], F32R) for n in ("kh", "kl"))
        vh, vl = (sb(n, [P, 2, GT, AW], F32R) for n in ("vh", "vl"))
        pr = sb("pr", [P, 3, PW])
        nmx, rsum, rinv = sb("nmx", [P, 3]), sb("rsum", [P, 3]), sb("rinv", [P, 3])
        pth, ptl = (sb(n, [P, 2, GT, 2, 2 * PQ], F32R) for n in ("pth", "ptl"))
        ath, atl = (sb(n, [P, 2, 2 * PQ], F32R) for n in ("ath", "atl"))
        tmp = sb("tmp", [P, N])

        ps_s = ps("ps_s", [P, 2, 2, 512])
        ps_t = ps("ps_t", [P, 2, 512])
        ps_o = ps("ps_o", [P, 2, 2, 2 * PQ])

        masked, gw_in = sem("masked"), sem("gw_in")
        win_in = [sem("win_in0"), sem("win_in1")]
        q_in = [sem(f"q_in{hp}") for hp in range(HP)]
        sc_turn, q_turn = sem("sc_turn"), sem("q_turn")
        qk_done, sc_done, ex_done, rinv_done, pn_done, tr_done = (sem(n) for n in (
            "qk_done", "sc_done", "ex_done", "rinv_done", "pn_done", "tr_done"))
        pth_done, ptl_done, pv_done, ath_done, atl_done = (sem(n) for n in (
            "pth_done", "ptl_done", "pv_done", "ath_done", "atl_done"))
        stored = [sem("stored0"), sem("stored1")]
        cv_step = sem("cv_step")

        def pair(j, first):
            return {"q0": j * PQ, "j": j, "mq": PQ, "tile0": first, "keys": [P] * (j + 5 - first),
                    "bias0": (first - j) * P}

        FIRST = [{"g": g, "slot": g % 2, "pairs": [pair(j, 4 - 2 * g) for j in range(2)]} for g in range(2)]
        SAMPLE = {"g": 8, "slot": 0,
                  "pairs": [{"q0": 0, "j": 0, "mq": DEC, "tile0": 0, "keys": [P] * 4 + [DEC], "bias0": 0}]}

        def inner(it):
            return [{"g": it * 2 + (2 + k), "slot": k, "pairs": [pair(j, j) for j in range(2)]} for k in range(2)]

        def sections(eng, run):
            run(FIRST, 0, 0, 0)
            with eng.Fori(0, 3) as it:
                run(inner(it), it * (2 * UG) + 2 * UG, it * (2 * HP) + 2 * HP, it * 2 + 2)
            run([SAMPLE], 8 * UG, 8 * HP, 8)

        def units(groups):
            return [{**p, "slot": g["slot"], "hp": hp, "hh": hh, "g": g["g"], "group": k, "w": sum(p["keys"]),
                     "quad": k * HP + hp}
                    for k, g in enumerate(groups) for hp in range(HP) for p in g["pairs"] for hh in range(2)]

        def out_at(us, i):
            per = 4 if us[0]["mq"] == P else 2
            return i // per - 1 + 1 if i % per == per - 1 and i // per >= 1 else 0

        def products(g):
            ps_ = g["pairs"]
            if len(ps_) == 1:
                return [(k, wd, 0, DEC) for k, wd in enumerate(ps_[0]["keys"])]
            lo, lo1 = ps_[0]["tile0"], ps_[1]["tile0"]
            whole = [(a, P, 0, 2 * PQ) for a in range(lo1, 5)]
            return whole + [(a, P, 0, PQ) for a in range(lo, lo1)] + [(5, P, PQ, PQ)]

        def parts(u):
            n = len(u["keys"])
            return [(0, range(min(n, 3)), 1 if n > 3 else 2)] + ([(1, range(3, n), 1)] if n > 3 else [])

        def pieces(u, part, tiles):
            mq, q0 = u["mq"], u["q0"]
            full, a = sum(u["keys"][k] == P for k in tiles), u["tile0"] + tiles[0]
            flat = ps_t[:, part, 0:full * P].rearrange("p (t q) -> p t q", q=P)[:, :, 0:mq]
            out = [(flat, lambda tl: tl[:, u["quad"] % 2, a:a + full, u["hh"], q0:q0 + mq])]
            if full < len(tiles):
                k = u["keys"][-1]
                out.append((ps_t[0:k, part, full * P:full * P + mq],
                            lambda tl: tl[0:k, u["quad"] % 2, a + full, u["hh"], q0:q0 + mq]))
            return out

        def rows(d):
            return d.rearrange("(c p) n -> p c n", p=P)

        block = ctx.enter_context(nc.Block())

        @block.sync
        def _(sp):
            def load_window(g):
                sl, at = g["slot"], g["g"]
                short = (2 - at) * 2 * PQ if isinstance(at, int) and at < 2 else 0
                k0 = at * (2 * PQ) - (PAST - short)
                for dst, src in ((kh, "kh"), (kl, "kl")):
                    sp.dma_start(dst[:, sl, :, short:WIN].bitcast(F32),
                                 rows(s[src])[:, :, bass.ds(k0, WIN - short)]).then_inc(win_in[sl], 16)
                for dst, src in ((vh, "vh"), (vl, "vl")):
                    sp.dma_start(dst[:, sl, short // P:GT, :].bitcast(F32),
                                 s[src][bass.ds(k0, WIN - short), :].rearrange("(t p) d -> p t d", p=P)).then_inc(win_in[sl], 16)

            def load_q(n, c0, width):
                for hp in range(HP):
                    if not (isinstance(n, int) and n == 0):
                        sp.wait_ge(qk_done, n * UG + 4 * (hp + 1) - UG)
                        sp.sem_inc(q_turn, 1)
                    for dst, src in ((qh, "qh"), (ql, "ql")):
                        sp.dma_start(dst[:, hp, 0:width].bitcast(F32),
                                     s[src][hp * P:(hp + 1) * P, bass.ds(c0, width)]).then_inc(q_in[hp], 16)

            def store_group(n, c0, width):
                for hp in range(HP):
                    sp.wait_ge(atl_done, n * HP + (hp + 1))
                    for dst, src in ((s["mh"], ath), (s["ml"], atl)):
                        sp.dma_start(dst[hp * P:(hp + 1) * P, c0], src[:, hp % 2, 0:width].bitcast(F32)).then_inc(stored[hp % 2], 16)

            G = 2 * PQ
            load_q(0, 0, G)
            load_window(FIRST[0])
            load_window(FIRST[1])
            for ch in range(NCH):
                gw_load(sp, t, c["gw"], 0, ch, gw_in)
            for q in range(2):
                sp.sem_inc(stored[q], 32)

            def group(n, last):
                load_q(n + 1, SEQ if last else (n + 1) * G, DEC if last else G)
                store_group(n, bass.ds(n * G, G), G)
                sp.wait_ge(pv_done, n * HP + HP)

            for k in range(2):
                group(k, False)
                load_window({"g": 2 + k, "slot": k})
            with sp.Fori(0, 2) as it:
                for k in range(2):
                    group(it * 2 + (2 + k), False)
                    load_window({"g": it * 2 + (4 + k), "slot": k})
            group(6, False)
            new = bass.ds(SEQ, DEC)
            for dst, name in ((kh, "kh"), (kl, "kl")):
                sp.dma_start(dst[:, 0, :, PAST:PAST + DEC].bitcast(F32), rows(s[name])[:, :, new]).then_inc(win_in[0], 16)
                sp.dma_start(dst[:, 0, :, 0:PAST].bitcast(F32),
                             s["c" + name[1]][:, 0:CT * PAST].rearrange("p (c n) -> p c n", c=HP)).then_inc(win_in[0], 16)
            for dst, name in ((vh, "vh"), (vl, "vl")):
                sp.dma_start(dst[0:DEC, 0, 4, :].bitcast(F32), s[name][new, :]).then_inc(win_in[0], 16)
                sp.dma_start(dst[:, 0, 0:4, :].bitcast(F32),
                             s["c" + name[1]][:, CT * PAST:].rearrange("p (c n) -> p c n", c=HP)).then_inc(win_in[0], 16)
            group(7, True)
            store_group(8, bass.ds(SEQ, DEC), DEC)
            for q in range(2):
                sp.wait_ge(stored[q], 32 * (1 + 9 * HP // 2))

        @block.gpsimd
        def _(pool):
            y, gw, vec = c["y"], c["gw"], c["vec"]
            pool.wait_ge(gw_in, 16 * NCH)
            n = 0
            for ct in range(CT):
                yc = y[:, ct, :].rearrange("p (a b) -> p a b", b=CW)
                w0 = V_CW + ct * TAPS
                nc.gpsimd.tensor_scalar(yc, gw[:, ct, :, 0:CW], vec[:, w0:w0 + 1],
                                        vec[:, V_CB + ct:V_CB + ct + 1], ALU.mult, ALU.add).then_inc(cv_step, 1)
            for k in range(1, TAPS):
                for ct in range(CT):
                    yc = y[:, ct, :].rearrange("p (a b) -> p a b", b=CW)
                    tc = tmp[:, :].rearrange("p (a b) -> p a b", b=CW)
                    wk = V_CW + ct * TAPS + k
                    pool.wait_ge(cv_step, CT + 2 * n)
                    nc.gpsimd.tensor_scalar(tc, gw[:, ct, :, k:k + CW], vec[:, wk:wk + 1], 0.0,
                                            ALU.mult, ALU.add).then_inc(cv_step, 1)
                    pool.wait_ge(cv_step, CT + 2 * n + 1)
                    nc.gpsimd.tensor_tensor(yc, yc, tc, ALU.add).then_inc(cv_step, 1)
                    n += 1

        @block.vector
        def _(dve):
            dve.wait_ge(bias_in, 16)
            nc.vector.memset(bias[0:CHUNK, :, PW - CHUNK:PW], NEG).then_inc(masked, 1)
            nc.vector.memset(bias[CHUNK:P, :, 0:CHUNK], NEG).then_inc(masked, 1)

            def run(groups, n0, k0, g0):
                us = units(groups)
                last_of = {u["quad"]: i for i, u in enumerate(us)}

                def scores(i):
                    u = us[i]
                    mq, h, half = u["mq"], 2 * u["hp"] + u["hh"], u["w"] // 2
                    dve.wait_ge(masked, 2)
                    dve.wait_ge(qk_done, n0 + (i + 1))
                    if i >= 3:
                        dve.wait_ge(tr_done, n0 * 2 + 2 * (i - 2))
                    dve.sem_inc(sc_turn, 1)
                    nc.vector.tensor_tensor_reduce(
                        out=pr[0:mq, i % 3, 0:2 * half].rearrange("p (a b) -> p a b", a=2),
                        in0=ps_s[0:mq, i % 2, :, 0:half],
                        in1=bias[0:mq, h, u["bias0"]:u["bias0"] + 2 * half].rearrange("p (a b) -> p a b", a=2),
                        scale=-1.0, scalar=3e38, op0=ALU.add, op1=ALU.min,
                        accum_out=nmx[0:mq, i % 3:i % 3 + 1]).then_inc(sc_done, 1)

                def normalise(i):
                    u = us[i]
                    mq, w, q = u["mq"], u["w"], i % 3
                    dve.wait_ge(ex_done, n0 + (i + 1))
                    if i >= 3:
                        dve.wait_ge(pn_done, n0 + (i - 2))
                    nc.vector.reciprocal(rinv[0:mq, q:q + 1], rsum[0:mq, q:q + 1]).then_inc(rinv_done, 1)
                    dve.wait_ge(rinv_done, n0 + (i + 1))
                    nc.vector.tensor_scalar(pr[0:mq, q, 0:w], pr[0:mq, q, 0:w], rinv[0:mq, q:q + 1], None,
                                            ALU.mult).then_inc(pn_done, 1)

                def low(i, which):
                    for part, tiles, steps in parts(us[i]):
                        if part == which:
                            dve.wait_ge(pth_done, n0 * 2 + (2 * i + part + 1))
                            for src, dst in pieces(us[i], part, tiles):
                                last = nc.vector.tensor_tensor(dst(ptl), src, dst(pth).bitcast(F32), ALU.subtract)
                            last.then_inc(ptl_done, steps)

                def out_low(k):
                    u = us[last_of[k]]
                    wd = 2 * PQ if u["mq"] == P else DEC
                    dve.wait_ge(ath_done, k0 + (k + 1))
                    for hh in range(2):
                        part = slice(HD * hh, HD * hh + HD)
                        last = nc.vector.tensor_tensor(atl[part, k % 2, 0:wd], ps_o[part, k % 2, hh, 0:wd],
                                                       ath[part, k % 2, 0:wd].bitcast(F32), ALU.subtract)
                    last.then_inc(atl_done, 1)

                for i in range(3):
                    scores(i)
                normalise(0)
                for i in range(len(us)):
                    low(i, 0)
                    if i + 1 < len(us):
                        normalise(i + 1)
                    low(i, 1)
                    if i + 3 < len(us):
                        scores(i + 3)
                    if out_at(us, i):
                        out_low(out_at(us, i) - 1)
                out_low(us[-1]["quad"])

            sections(dve, run)

        @block.scalar
        def _(act):
            def run(groups, n0, k0, g0):
                us = units(groups)
                last_of = {u["quad"]: i for i, u in enumerate(us)}

                def exp(i):
                    u = us[i]
                    mq, w, q = u["mq"], u["w"], i % 3
                    act.wait_ge(sc_done, n0 + (i + 1))
                    nc.scalar.activation(pr[0:mq, q, 0:w], pr[0:mq, q, 0:w], ACT.Exp, scale=-1.0,
                                         bias=nmx[0:mq, q:q + 1], accum_out=rsum[0:mq, q:q + 1]).then_inc(ex_done, 1)

                def high(i):
                    u = us[i]
                    if u["quad"] >= 2:
                        act.wait_ge(pv_done, k0 + (u["quad"] - 1))
                    for part, tiles, steps in parts(u):
                        act.wait_ge(tr_done, n0 * 2 + (2 * i + part + 1))
                        for src, dst in pieces(u, part, tiles):
                            last = nc.scalar.activation(dst(pth), src, ACT.Copy)
                        last.then_inc(pth_done, steps)

                def out_high(k):
                    u = us[last_of[k]]
                    wd = 2 * PQ if u["mq"] == P else DEC
                    act.wait_ge(pv_done, k0 + (k + 1))
                    act.wait_ge(stored[k % 2], g0 * 64 + 32 * (k // 2 + 1))
                    for hh in range(2):
                        part = slice(HD * hh, HD * hh + HD)
                        last = nc.scalar.activation(ath[part, k % 2, 0:wd], ps_o[part, k % 2, hh, 0:wd], ACT.Copy)
                    last.then_inc(ath_done, 1)

                for i in range(2):
                    exp(i)
                for i in range(len(us)):
                    high(i)
                    if i + 2 < len(us):
                        exp(i + 2)
                    if out_at(us, i):
                        out_high(out_at(us, i) - 1)
                out_high(us[-1]["quad"])

            sections(act, run)

        @block.tensor
        def _(pe):
            def run(groups, n0, k0, g0):
                us = units(groups)
                per = len(us) // (HP * len(groups))

                def scores(i):
                    u = us[i]
                    part, ct = slice(HD * u["hh"], HD * u["hh"] + HD), u["hp"]
                    mq, sl, q0, at = u["mq"], u["slot"], u["q0"], u["tile0"] * P
                    if i == 0 or us[i - 1]["group"] != u["group"]:
                        got = 64 * 4 + 16 * 8 if mq != P else u["g"] * 32 + (64 - 32 * sl)
                        pe.wait_ge(win_in[sl], got)
                    if u["hh"] == 0 and u["j"] == 0:
                        pe.wait_ge(q_in[ct], u["g"] * 32 + 32)
                    if i >= 2:
                        pe.wait_ge(sc_done, n0 + (i - 1))
                    half = u["w"] // 2
                    for a in range(2):
                        keys = slice(at + a * half, at + (a + 1) * half)
                        for j, (qt, kt) in enumerate(((qh, kh), (qh, kl), (ql, kh))):
                            mm = nc.tensor.matmul(ps_s[0:mq, i % 2, a, 0:half], qt[part, ct, q0:q0 + mq],
                                                  kt[part, sl, ct, keys], start=j == 0, stop=j == 2)
                    mm.then_inc(qk_done, 1)

                def transposes(i):
                    u = us[i]
                    mq = u["mq"]
                    pe.wait_ge(pn_done, n0 + (i + 1))
                    for part, tiles, steps in parts(u):
                        if i >= 1:
                            pe.wait_ge(ptl_done, n0 * 2 + (2 * i + part - 1))
                        for at, k in enumerate(tiles):
                            wd = u["keys"][k]
                            mm = nc.tensor.transpose(ps_t[0:wd, part, at * P:at * P + mq],
                                                     pr[0:mq, i % 3, k * P:k * P + wd], c["ident"][0:mq, 0:mq])
                        mm.then_inc(tr_done, steps)

                def values(k, part):
                    u = us[k * per]
                    todo = products(groups[u["group"]])
                    n = len(todo)
                    if part == 0:
                        pe.wait_ge(ptl_done, n0 * 2 + 2 * per * (k + 1))
                        if k >= 2:
                            pe.wait_ge(atl_done, k0 + (k - 1))
                    mm = None
                    for x in range(n * part // per, n * (part + 1) // per):
                        a, wd, q0, nq = todo[x]
                        for j, (pt, vt) in enumerate(((pth, vh), (ptl, vh), (pth, vl))):
                            mm = nc.tensor.matmul(ps_o[:, k % 2, :, q0:q0 + nq],
                                                  vt[0:wd, u["slot"], a, u["hp"] * P:(u["hp"] + 1) * P],
                                                  pt[0:wd, k % 2, a, :, q0:q0 + nq],
                                                  start=x == 0 and j == 0, stop=x == n - 1 and j == 2)
                    if part == per - 1:
                        mm.then_inc(pv_done, 1)

                for i in range(3):
                    scores(i)
                for i in range(len(us)):
                    transposes(i)
                    if i + 3 < len(us):
                        scores(i + 3)
                    if i >= per:
                        values(i // per - 1, i % per)
                for part in range(per):
                    values(us[-1]["quad"], part)

            sections(pe, run)


def finish(nc, t, c, s):
    OU, HF = 8, KF // 2
    HU = 2 * HF + KD
    GU = [OU, OU + HU]
    DU = [g + 2 * HF for g in GU]
    E0 = OU + 2 * HU
    NU = E0 + KD
    KE = KD + KP
    T0 = KF + KD
    NTAP = CT * TAPS
    with ExitStack() as ctx:
        def sb(name, shape, dt=F32):
            return ctx.enter_context(nc.sbuf_tensor("c_" + name, shape, dt))

        def ps(name, shape):
            return ctx.enter_context(nc.psum_tensor("c_" + name, shape, F32))

        def sem(name):
            return ctx.enter_context(nc.semaphore("c_" + name))

        ring = WeightRing(nc, ctx, "c_", HF)
        h = sb("h", [P, KD, N])
        mh, ml = (sb(n, [P, KD, N], F32R) for n in ("mh", "ml"))
        uh, ul = (sb(n, [P, KD, N], F32R) for n in ("uh", "ul"))
        hh, hl = (sb(n, [P, HF, N], F32R) for n in ("hh", "hl"))
        p = sb("p", [P, KP, N])
        ph, pl = (sb(n, [P, KP, N], F32R) for n in ("ph", "pl"))
        sq, ssum, sd, rstd = (sb(n, [P, N]) for n in ("sq", "ssum", "sd", "rstd"))
        g, sig, up = (sb(n, [P, N]) for n in ("g", "sig", "up"))
        hid = sb("hid", [P, N])
        yo = sb("yo", [P, 2, N])
        y, gw = c["y"], c["gw"]
        cx = sb("cx", [P, CT, N])
        csum, csd, crs = (sb(n, [P, N]) for n in ("csum", "csd", "crs"))
        acc, acc_p = ps("acc", [P, 2, 512]), ps("acc_p", [P, 2, 512])
        ps_n, ps_c = ps("ps_n", [P, 512]), ps("ps_c", [P, 512])

        x_in = [sem(f"x_in{m}") for m in range(KD)]
        mix_in, p_in, p_hi, p_lo, gw_in = (sem(n) for n in ("mix_in", "p_in", "p_hi", "p_lo", "gw_in"))
        left = sem("left")
        u_hi, u_lo, sq_out, sum_out = (sem(n) for n in ("u_hi", "u_lo", "sq_out", "sum_out"))
        n_mm, n_sd, n_r = sem("n_mm"), sem("n_sd"), sem("n_r")
        sig_out, gs_out, hid_out, hid_hi, hid_lo = (sem(n) for n in (
            "sig_out", "gs_out", "hid_out", "hid_hi", "hid_lo"))
        e_out, y_out = sem("e_out"), sem("y_out")
        stored = [sem("stored0"), sem("stored1")]
        tap = sem("tap")
        cv_sum, cv_mm, cv_xc, cv_sq, cv_sd, cv_r, cv_xn, cv_aff, cv_sig, cv_out, cv_hi, cv_lo = (sem("cv_" + n) for n in (
            "sum", "mm", "xc", "sq", "sd", "r", "xn", "aff", "sig", "out", "hi", "lo"))
        vec = c["vec"]

        def place(u):
            if u < OU:
                return "out", 0, u
            if u >= E0:
                return "ple", 0, u - E0
            half, r = divmod(u - OU, HU)
            return ("gu", half, r) if r < 2 * HF else ("down", half, r - 2 * HF)

        def ktiles(u):
            return {"out": KD, "gu": KD, "down": HF, "ple": KE}[place(u)[0]]

        def weights(sp, u):
            kind, half, m = place(u)
            if kind == "out":
                src = t["w_out"][m * P:(m + 1) * P, :]
            elif kind == "gu":
                r = half * 2 * HF + m
                src = t["w_gu"][r * P:(r + 1) * P, :]
            elif kind == "down":
                src = t["w_down"][m * P:(m + 1) * P, half * HF * P:(half + 1) * HF * P]
            else:
                src = t["w_ple"][m * P:(m + 1) * P, :]
            ring.load(sp, src, u % 2, ktiles(u))

        def phases(eng, b, step, fstep, cut=0, peel=0, first=0):
            for u in range(OU):
                step(b, u)
            for half in range(2):
                start = 0 if half else first
                for f in range(start):
                    fstep(b, half, f)
                with eng.Fori(start, HF - cut // 2 - peel) as f:
                    fstep(b, half, f)
                for f in range(HF - peel, HF):
                    fstep(b, half, f)
                for u in range(DU[half] - cut, DU[half] + KD):
                    step(b, u)
            for u in range(E0, NU):
                step(b, u)

        block = ctx.enter_context(nc.Block())

        def mix_load(sp, b):
            for dst, src in ((mh, "mh"), (ml, "ml")):
                sp.dma_start(dst[:, 0:CT, :].bitcast(F32),
                             s[src].rearrange("(k p) n -> p k n", p=P)[:, :, bass.ds(b * N, N)]).then_inc(mix_in, 16)

        def x_load(sp, b, m):
            sp.dma_start(h[:, m, :], t["x"][bass.ds(b * P, P), m * N:(m + 1) * N]).then_inc(x_in[m], 16)

        def p_load(sp, b):
            sp.dma_start(p[:, :, :].rearrange("p k n -> p (k n)"), t["p"][bass.ds(b * P, P), :]).then_inc(p_in, 16)

        @block.sync
        def _(sp):
            weights(sp, 0)
            mix_load(sp, 0)
            weights(sp, 1)
            for m in range(KD):
                x_load(sp, 0, m)
            p_load(sp, 0)
            for u in range(2, 4):
                sp.wait_ge(ring.lo_done, u - 1)
                weights(sp, u)
            for q in range(2):
                sp.sem_inc(stored[q], 16)

            def step(b, u):
                if u >= E0:
                    m = u - E0
                    sp.wait_ge(y_out, b * KD + (m + 1))
                    sp.dma_start(t["o_y"][bass.ds(b * P, P), m * N:(m + 1) * N], yo[:, m % 2, :]).then_inc(stored[m % 2], 16)
                    x_load(sp, wrapped(b), m)
                if 1 <= u <= 7:
                    for ch in range(2 * u - 2, min(2 * u, NCH)):
                        gw_load(sp, t, gw, wrapped(b), ch, gw_in)
                if u == DU[0] + 3:
                    sp.wait_ge(ring.used, b * NU + (OU + 2))
                    mix_load(sp, wrapped(b))
                    sp.wait_ge(p_lo, b + 1)
                    p_load(sp, wrapped(b))
                sp.wait_ge(ring.lo_done, b * NU + (u + 3))
                if u == 0:
                    sp.wait_ge(tap, b * NTAP + 1)
                weights(sp, (u + 4) % NU)

            def fstep(b, half, f):
                for j in range(2):
                    sp.wait_ge(ring.lo_done, b * NU + f * 2 + (GU[half] + j + 3))
                    ring.load(sp, t["w_gu"][bass.ds(f * (2 * P) + (half * 2 * HF + 4 + j) * P, P), :], j, KD)

            with sp.Fori(0, NB) as b:
                phases(sp, b, step, fstep, 4)
            for q in range(2):
                sp.wait_ge(ring.loaded[q], 16 * (NU * NB // 2 + 2))
                sp.wait_ge(stored[q], 16 * (1 + NB * KD // 2))
            for m in range(KD):
                sp.wait_ge(x_in[m], 16 * (NB + 1))
            sp.wait_ge(mix_in, 32 * (NB + 1))
            sp.wait_ge(p_in, 16 * (NB + 1))

        @block.scalar
        def _(act):

            def tail(n, stage):
                if stage == "square":
                    act.wait_ge(cv_xc, n * CT + CT)
                    nc.scalar.activation(cx[:, :, :], y[:, :, :], ACT.Square).then_inc(cv_sq, 1)
                elif stage == "sd":
                    act.wait_ge(cv_mm, n * 2 + 2)
                    nc.scalar.activation(csd[:, :], ps_c[:, 0:N], ACT.Sqrt, scale=1.0 / AW, bias=c["eps"][:, :]).then_inc(cv_sd, 1)
                elif stage == "high":
                    act.wait_ge(cv_out, n + 1)
                    nc.scalar.activation(mh[:, CT:KD, :], cx[:, :, :], ACT.Copy).then_inc(cv_hi, 1)
                else:
                    act.wait_ge(cv_aff, n * CT + (stage + 1))
                    gain, off = (vec[:, v + stage:v + stage + 1] for v in (V_LG, V_LB))
                    nc.scalar.activation(y[:, stage, :], y[:, stage, :], ACT.Sigmoid, scale=gain, bias=off).then_inc(cv_sig, 1)

            def tile_out(b, u, n, m, gain):
                act.wait_ge(left, b * NU + (u + 3))
                nc.scalar.activation(uh[:, m, :], h[:, m, :], ACT.Identity,
                                     scale=vec[:, gain + m:gain + m + 1]).then_inc(u_hi, 1)
                if m == 0:
                    if n:
                        act.wait_ge(n_mm, b * 2 + 1)
                    nc.scalar.activation(ssum[:, :], h[:, m, :], ACT.Square).then_inc(sq_out, 1)
                else:
                    if m >= 2:
                        act.wait_ge(sum_out, b * 14 + (n // KD * 7 + m - 1))
                    nc.scalar.activation(sq[:, :], h[:, m, :], ACT.Square).then_inc(sq_out, 1)

            def norm(b, i):
                act.wait_ge(n_mm, b * 2 + (i + 1))
                nc.scalar.activation(sd[:, :], ps_n[:, 0:N], ACT.Sqrt, scale=1.0 / D, bias=c["eps"][:, :]).then_inc(n_sd, 1)

            def step(b, u):
                v = u + 2
                kind, half, m = place(u)
                ring.high(act, b * NU + v, b * (NU // 2) + v // 2, v % 2, ktiles(v % NU))
                if kind == "out":
                    tile_out(b, u, 0, m, V_GFFN)
                elif kind == "down" and half:
                    tile_out(b, u, KD, m, V_GPLE)
                elif kind == "ple":
                    if m == 0:
                        norm(b, 1)
                    act.wait_ge(left, b * NU + (u + 3))
                    nc.scalar.activation(sig[:, :], g[:, :], ACT.Sigmoid).then_inc(sig_out, 1)
                if u == 3:
                    act.wait_ge(p_in, b * 16 + 16)
                    nc.scalar.activation(ph[:, :, :], p[:, :, :], ACT.Copy).then_inc(p_hi, 1)
                if u == OU - 1:
                    norm(b, 0)
                if u == DU[1] + 3:
                    tail(b + 1, "square")
                if u == DU[1] + 6:
                    tail(b + 1, "sd")
                if E0 < u <= E0 + CT:
                    tail(b + 1, u - E0 - 1)
                if u == E0 + 5:
                    tail(b + 1, "high")

            def fstep(b, half, f):
                n, kts = half * HF, ktiles(DU[half]) if isinstance(f, int) else KD
                ring.high(act, b * NU + f * 2 + (GU[half] + 2), b * (NU // 2) + f + (GU[half] // 2 + 1), 0, kts)
                act.wait_ge(left, b * NU + f * 2 + (GU[half] + 3))
                nc.scalar.activation(sig[:, :], g[:, :], ACT.Sigmoid).then_inc(sig_out, 1)
                ring.high(act, b * NU + f * 2 + (GU[half] + 3), b * (NU // 2) + f + (GU[half] // 2 + 1), 1, kts)
                act.wait_ge(hid_out, b * KF + f + (n + 1))
                nc.scalar.activation(hh[:, bass.ds(f, 1), :], hid[:, :].unsqueeze(1), ACT.Copy).then_inc(hid_hi, 1)

            tail(0, "square")
            ring.high(act, 0, 0, 0, KD)
            tail(0, "sd")
            ring.high(act, 1, 0, 1, KD)
            for stage in (0, 1, 2, 3, "high"):
                tail(0, stage)
            with act.Fori(0, NB) as b:
                phases(act, b, step, fstep, peel=1)

        @block.gpsimd
        def _(pool):
            ring.low(pool, 0, 0, KD)
            ring.low(pool, 1, 1, KD)

            def step(b, u):
                ring.low(pool, b * NU + (u + 2), u % 2, ktiles((u + 2) % NU))

            def fstep(b, half, f):
                for j in range(2):
                    ring.low(pool, b * NU + f * 2 + (GU[half] + j + 2), j, ktiles(DU[half]) if isinstance(f, int) else KD)

            with pool.Fori(0, NB) as b:
                phases(pool, b, step, fstep, peel=1)

        @block.vector
        def _(dve):
            dve.sem_inc(left, 2)
            dve.sem_inc(tap, 1)

            def tail(n, stage):
                if stage == "sum":
                    nc.vector.tensor_reduce(out=csum[:, :], in_=y[:, :, :].rearrange("p c n -> p n c"),
                                            axis=AX.X, op=ALU.add).then_inc(cv_sum, 1)
                elif stage == "center":
                    dve.wait_ge(cv_mm, n * 2 + 1)
                    for ct in range(CT):
                        nc.vector.scalar_tensor_tensor(y[:, ct, :], ps_c[:, 0:N], -1.0 / AW, y[:, ct, :],
                                                       ALU.mult, ALU.add).then_inc(cv_xc, 1)
                elif stage == "sum2":
                    dve.wait_ge(cv_sq, n + 1)
                    nc.vector.tensor_reduce(out=csum[:, :], in_=cx[:, :, :].rearrange("p c n -> p n c"),
                                            axis=AX.X, op=ALU.add).then_inc(cv_sum, 1)
                elif stage == "scale":
                    dve.wait_ge(cv_sd, n + 1)
                    nc.vector.reciprocal(crs[:, :], csd[:, :]).then_inc(cv_r, 1)
                    dve.wait_ge(cv_r, n + 1)
                    for ct in range(CT):
                        nc.vector.tensor_tensor(y[:, ct, :], y[:, ct, :], crs[:, :], ALU.mult).then_inc(cv_xn, 1)
                    for ct in range(CT):
                        dve.wait_ge(cv_xn, n * CT + (ct + 1))
                        nc.vector.tensor_scalar(cx[:, ct, :], y[:, ct, :], vec[:, V_LG + ct:V_LG + ct + 1],
                                                vec[:, V_LB + ct:V_LB + ct + 1], ALU.mult, ALU.add).then_inc(cv_aff, 1)
                elif stage == "swish":
                    dve.wait_ge(cv_sig, n * CT + CT)
                    nc.vector.tensor_tensor(cx[:, :, :], cx[:, :, :], y[:, :, :], ALU.mult).then_inc(cv_out, 1)
                else:
                    dve.wait_ge(cv_hi, n + 1)
                    nc.vector.tensor_tensor(ml[:, CT:KD, :], cx[:, :, :], mh[:, CT:KD, :].bitcast(F32),
                                            ALU.subtract).then_inc(cv_lo, 1)

            def taps(b, k, n):
                for ct in range(CT):
                    yc = y[:, ct, :].rearrange("p (a b) -> p a b", b=CW)
                    dve.wait_ge(tap, b * NTAP + (n * CT + ct - CT + 2))
                    nc.vector.scalar_tensor_tensor(
                        yc, gw[:, ct, :, bass.ds(k, CW)], vec[:, bass.ds(k + (V_CW + ct * TAPS), 1)], yc,
                        ALU.mult, ALU.add).then_inc(tap, 1)

            def first_tap(b):
                dve.wait_ge(gw_in, b * (16 * NCH) + 16 * NCH)
                for ct in range(CT):
                    wk = V_CW + ct * TAPS + HIST
                    nc.vector.tensor_scalar(y[:, ct, :].rearrange("p (a b) -> p a b", b=CW), gw[:, ct, :, HIST:HIST + CW],
                                            vec[:, wk:wk + 1], vec[:, V_CB + ct:V_CB + ct + 1], ALU.mult,
                                            ALU.add).then_inc(tap, 1)

            def tile_out(b, u, n, m, gain):
                dve.wait_ge(left, b * NU + (u + 3))
                dve.wait_ge(u_hi, b * (2 * KD) + (n + m + 1))
                nc.vector.scalar_tensor_tensor(ul[:, m, :], h[:, m, :], vec[:, gain + m:gain + m + 1],
                                               uh[:, m, :].bitcast(F32), ALU.mult, ALU.subtract).then_inc(u_lo, 1)
                if m:
                    dve.wait_ge(sq_out, b * (2 * KD) + (n + m + 1))
                    if m >= 2:
                        dve.wait_ge(sum_out, b * 14 + (n // KD * 7 + m - 1))
                    nc.vector.tensor_tensor(ssum[:, :], ssum[:, :], sq[:, :], ALU.add).then_inc(sum_out, 1)

            def norm(b, i):
                dve.wait_ge(n_sd, b * 2 + (i + 1))
                nc.vector.reciprocal(rstd[:, :], sd[:, :]).then_inc(n_r, 1)

            def step(b, u):
                kind, half, m = place(u)
                if kind == "ple":
                    if m == 0:
                        norm(b, 1)
                    dve.wait_ge(ring.used, b * NU + (u + 3))
                    dve.wait_ge(n_r, b * 2 + 2)
                    nc.vector.tensor_tensor(g[:, :], acc[:, m % 2, 0:N], rstd[:, :], ALU.mult).then_inc(left, 1)
                    dve.wait_ge(sig_out, b * T0 + (KF + m + 1))
                    nc.vector.tensor_tensor(up[:, :], acc_p[:, m % 2, 0:N], sig[:, :], ALU.mult).then_inc(e_out, 1)
                    dve.wait_ge(e_out, b * KD + (m + 1))
                    dve.wait_ge(stored[m % 2], b * (8 * KD) + 16 * (m // 2 + 1))
                    nc.vector.tensor_tensor(yo[:, m % 2, :], up[:, :], h[:, m, :], ALU.add).then_inc(y_out, 1)
                else:
                    dve.wait_ge(ring.used, b * NU + (u + 3))
                    if kind == "out":
                        dve.wait_ge(x_in[m], b * 16 + 16)
                    nc.vector.tensor_tensor(h[:, m, :], acc[:, u % 2, 0:N], h[:, m, :], ALU.add).then_inc(left, 1)
                    if kind == "out":
                        tile_out(b, u, 0, m, V_GFFN)
                    elif half:
                        tile_out(b, u, KD, m, V_GPLE)
                    else:
                        taps(b, 2 * HF + m, 1 + HF + m)
                if u == 4:
                    dve.wait_ge(p_hi, b + 1)
                    nc.vector.tensor_tensor(pl[:, :, :], p[:, :, :], ph[:, :, :].bitcast(F32), ALU.subtract).then_inc(p_lo, 1)
                if u == OU - 1:
                    norm(b, 0)
                    first_tap(b)
                if u == DU[1]:
                    dve.wait_ge(tap, b * NTAP + (NTAP + 1))
                    tail(b + 1, "sum")
                for at, stage in ((DU[1] + 2, "center"), (DU[1] + 4, "sum2"), (DU[1] + 6, "scale"),
                                  (E0 + 5, "swish"), (E0 + 6, "low")):
                    if u == at:
                        tail(b + 1, stage)

            def fstep(b, half, f):
                n, u = half * HF, GU[half]
                dve.wait_ge(n_r, b * 2 + 1)
                dve.wait_ge(ring.used, b * NU + f * 2 + (u + 3))
                nc.vector.tensor_tensor(g[:, :], acc[:, 0, 0:N], rstd[:, :], ALU.mult).then_inc(left, 1)
                dve.wait_ge(sig_out, b * T0 + f + (n + 1))
                dve.wait_ge(left, b * NU + f * 2 + (u + 3))
                nc.vector.tensor_tensor(g[:, :], g[:, :], sig[:, :], ALU.mult).then_inc(gs_out, 1)
                dve.wait_ge(ring.used, b * NU + f * 2 + (u + 4))
                nc.vector.tensor_tensor(up[:, :], acc[:, 1, 0:N], rstd[:, :], ALU.mult).then_inc(left, 1)
                dve.wait_ge(gs_out, b * KF + f + (n + 1))
                dve.wait_ge(left, b * NU + f * 2 + (u + 4))
                nc.vector.tensor_tensor(hid[:, :], g[:, :], up[:, :], ALU.mult).then_inc(hid_out, 1)
                dve.wait_ge(hid_out, b * KF + f + (n + 1))
                dve.wait_ge(hid_hi, b * KF + f + (n + 1))
                nc.vector.tensor_tensor(hl[:, bass.ds(f, 1), :], hid[:, :].unsqueeze(1),
                                        hh[:, bass.ds(f, 1), :].bitcast(F32), ALU.subtract).then_inc(hid_lo, 1)
                taps(b, f + n, f + (1, HF + KD + 1)[half])

            for stage in ("sum", "center", "sum2", "scale", "swish", "low"):
                tail(0, stage)
            with dve.Fori(0, NB) as b:
                phases(dve, b, step, fstep)

        @block.tensor
        def _(pe):
            pe.sem_inc(ring.used, 2)

            def w(q):
                return [lambda k: ring.hi[:, q, k, :], lambda k: ring.lo[:, q, k, :]]

            U = [lambda k: uh[:, k, :], lambda k: ul[:, k, :]]
            M = [lambda k: mh[:, k, :], lambda k: ml[:, k, :]]
            H = [lambda k: hh[:, k, :], lambda k: hl[:, k, :]]
            E = [lambda k: ph[:, k, :], lambda k: pl[:, k, :]]
            ALL = [(k, k) for k in range(KD)]

            def norm(b, i):
                pe.wait_ge(sum_out, b * 14 + 7 * (i + 1))
                nc.tensor.matmul(ps_n[:, 0:N], c["ones"][:, :], ssum[:, :], start=True, stop=True).then_inc(n_mm, 1)

            def first_use(b, i, out, wq):
                pe.wait_ge(u_lo, b * (2 * KD) + (KD * (i + 1) - 2))
                passes(nc, out, wq, U, ALL[:KD - 2], True, False)
                for k in range(KD - 2, KD):
                    pe.wait_ge(u_lo, b * (2 * KD) + (KD * i + k + 1))
                    mm = passes(nc, out, wq, U, [(k, k)], False, k == KD - 1)
                return mm

            def tail(n, i):
                pe.wait_ge(cv_sum, n * 2 + (i + 1))
                nc.tensor.matmul(ps_c[:, 0:N], c["ones"][:, :], csum[:, :], start=True, stop=True).then_inc(cv_mm, 1)

            def step(b, u):
                kind, half, m = place(u)
                q = u % 2
                out = acc[:, q, 0:N]
                if u == 0:
                    pe.wait_ge(mix_in, b * 32 + 32)
                pe.wait_ge(ring.lo_done, b * NU + (u + 1))
                pe.wait_ge(left, b * NU + (u + 1))
                if u == 0:
                    passes(nc, out, w(q), M, ALL[:CT], True, False)
                    pe.wait_ge(cv_lo, b + 1)
                    mm = passes(nc, out, w(q), M, ALL[CT:], False, True)
                elif kind == "out":
                    mm = passes(nc, out, w(q), M, ALL, True, True)
                elif kind == "down":
                    if m == 0:
                        pe.wait_ge(hid_lo, b * KF + (HF * (half + 1) - 1))
                        passes(nc, out, w(q), H, [(k, k) for k in range(HF - 1)], True, False)
                        pe.wait_ge(hid_lo, b * KF + HF * (half + 1))
                        mm = passes(nc, out, w(q), H, [(HF - 1, HF - 1)], False, True)
                    else:
                        mm = passes(nc, out, w(q), H, [(k, k) for k in range(HF)], True, True)
                else:
                    if m == 0:
                        pe.wait_ge(p_lo, b + 1)
                    if m >= 2:
                        pe.wait_ge(e_out, b * KD + (m - 1))
                    passes(nc, acc_p[:, q, 0:N], w(q), E, [(KD + k, k) for k in range(KP)], True, True)
                    mm = first_use(b, 1, out, w(q)) if m == 0 else passes(nc, out, w(q), U, ALL, True, True)
                mm.then_inc(ring.used, 1)
                if u == E0:
                    norm(b, 1)
                if u == DU[1] + 1:
                    tail(b + 1, 0)
                if u == DU[1] + 5:
                    tail(b + 1, 1)

            def fstep(b, half, f):
                for j in range(2):
                    pe.wait_ge(ring.lo_done, b * NU + f * 2 + (GU[half] + j + 1))
                    pe.wait_ge(left, b * NU + f * 2 + (GU[half] + j + 1))
                    if isinstance(f, int) and half == j == 0:
                        mm = first_use(b, 0, acc[:, j, 0:N], w(j))
                    else:
                        mm = passes(nc, acc[:, j, 0:N], w(j), U, ALL, True, True)
                    mm.then_inc(ring.used, 1)
                    if isinstance(f, int) and half == j == 0:
                        norm(b, 0)

            tail(0, 0)
            tail(0, 1)
            with pe.Fori(0, NB) as b:
                phases(pe, b, step, fstep, first=1)


def kernel(x_prompt, x_sample, p_prompt, p_sample, cache_k, cache_v, state_conv, g_mix, w_in, q_gain, k_gain,
           rel_bias, conv_w, conv_b, conv_ln_g, conv_ln_b, w_out, g_ffn, w_gate_up, w_down, g_ple, w_ple_gate,
           w_ple_proj):
    import numpy as np
    import concourse.bacc as bacc
    from concourse.bass_utils import run_bass_kernel_spmd

    a = np.asarray

    def tiles(w):
        k, m = w.shape
        return a(w).reshape(k // P, P, m // P, P).transpose(2, 1, 0, 3).reshape(m, k)

    def blocks(v):
        f = v.shape[1]
        return v.reshape(NB, N, f // P, P).transpose(0, 3, 2, 1).reshape(NB * P, f // P * N)

    def paired(first, second):
        return np.stack([first.reshape(-1, P, first.shape[1]), second.reshape(-1, P, second.shape[1])],
                        1).reshape(-1, first.shape[1])

    def columns(v):
        return a(v).reshape(-1, P).T

    wi = tiles(w_in[0])
    part = [wi[AW * i:AW * (i + 1)] for i in range(5)]
    gu = tiles(w_gate_up[0])
    ins = {
        "x": blocks(np.concatenate([a(x_prompt)[0], a(x_sample)[0]])),
        "p": blocks(np.concatenate([a(p_prompt)[0, 0], a(p_sample)[0, 0]])),
        "w_in": np.concatenate([paired(part[0], part[1]), part[2], paired(part[3], part[4])]),
        "w_out": tiles(w_out[0]),
        "w_gu": paired(gu[:FF], gu[FF:]),
        "w_down": tiles(w_down[0]),
        "w_ple": np.concatenate([tiles(w_ple_gate[0]), tiles(w_ple_proj[0])], 1),
        "ck_rows": a(cache_k)[0, 0, DEC:].reshape(PAST - DEC, AW),
        "cv_rows": a(cache_v)[0, 0, DEC:].reshape(PAST - DEC, AW),
        "cache": np.concatenate([
            a(cache_k)[0, 0].reshape(PAST, CT, P).transpose(2, 1, 0).reshape(P, CT * PAST),
            a(cache_v)[0, 0].reshape(PAST // P, P, AW).transpose(1, 0, 2).reshape(P, PAST // P * AW)], 1),
        "state": a(state_conv)[0, 0].T,
        "vec": np.concatenate([
            columns(g_mix), columns(g_ffn), columns(g_ple),
            np.tile(a(q_gain)[0], 2)[:, None], np.tile(a(k_gain)[0], 2)[:, None],
            columns(conv_b), columns(conv_ln_g), columns(conv_ln_b),
            a(conv_w)[0].reshape(TAPS, CT, P).transpose(2, 1, 0).reshape(P, CT * TAPS)], 1),
        "ext": np.tile(np.concatenate([np.repeat(a(rel_bias)[0, :, 256:257], PAST, 1),
                                       a(rel_bias)[0, :, 255:0:-1]], 1), (1, P)),
    }
    outs = {"o_y": (NB * P, KD * N), "o_k": (AW, NT), "o_v": (NT, AW), "o_g": (AW, GPAD),
            "o_ck": (PAST - DEC, AW), "o_cv": (PAST - DEC, AW)}
    nc = bacc.Bacc("TRN2", target_bir_lowering=False, num_devices=1)
    t, arrays = {}, {}
    for name, v in ins.items():
        arrays["in_" + name] = np.ascontiguousarray(v)
        t[name] = nc.dram_tensor("in_" + name, v.shape, F32, kind="ExternalInput").ap()
    for name, shape in outs.items():
        t[name] = nc.dram_tensor(name, shape, F32, kind="ExternalOutput").ap()
    build(nc, t)
    r = run_bass_kernel_spmd(nc, [arrays], core_ids=[0]).results[0]
    y = r["o_y"].reshape(NB, P, KD, N).transpose(0, 3, 2, 1).reshape(NT, D)
    k, v, g = r["o_k"].T, r["o_v"], r["o_g"].T
    heads = (1, 1, PAST, HEADS, HD)
    return (y[None, :SEQ], y[None, SEQ:],
            k[SEQ - PAST:SEQ].reshape(heads), v[SEQ - PAST:SEQ].reshape(heads), g[None, None, SEQ:SEQ + HIST],
            np.concatenate([r["o_ck"], k[SEQ:]]).reshape(heads), np.concatenate([r["o_cv"], v[SEQ:]]).reshape(heads),
            g[None, None, GPAD - HIST:])
```
